# Optimizing a Trainium2 kernel written in Bass

```python
import math
import jax, jax.numpy as jnp
from jax import lax
import numpy as np

D_MODEL = 1024
BATCH = 1
SEQ = 512
DEPTH = 1

MEM_LEN = 256
RET_HEADS = 4
RET_HEAD_DIM = 128
RET_WIDTH = RET_HEADS * RET_HEAD_DIM
DIFF_HEADS = 4
DIFF_HALF_DIM = 64
DIFF_V_DIM = 2 * DIFF_HALF_DIM
DIFF_WIDTH = DIFF_HEADS * DIFF_V_DIM
MIX_WIDTH = RET_WIDTH + DIFF_WIDTH
IN_COLS = 4 * RET_WIDTH + 3 * DIFF_WIDTH
MEM_HEADS = 4
MEM_HEAD_DIM = D_MODEL // MEM_HEADS
D_FF = 2816
CHUNK = 128
Q_BLOCK = 128
EPS = 1e-6
NEG_BIG = -1e30


def rms_norm(x, g):
    xf = x.astype(jnp.float32)
    y = xf * lax.rsqrt(jnp.mean(xf * xf, axis=-1, keepdims=True) + EPS)
    return (y * g.astype(jnp.float32)).astype(x.dtype)

def group_norm(x, g):
    xf = x.astype(jnp.float32)
    mu = jnp.mean(xf, axis=-1, keepdims=True)
    xc = xf - mu
    y = xc * lax.rsqrt(jnp.mean(xc * xc, axis=-1, keepdims=True) + EPS)
    return (y * g.astype(jnp.float32)).astype(x.dtype)

def swiglu(h, w1, w3, w2):
    return (jax.nn.silu(h @ w1) * (h @ w3)) @ w2

def retention(q, k, v):
    b, s, h, d = q.shape
    nc = s // CHUNK
    log_gamma = jnp.log1p(-jnp.exp2(-5.0 - jnp.arange(h, dtype=jnp.float32)))
    idx = jnp.arange(CHUNK, dtype=jnp.float32)
    rel = idx[:, None] - idx[None, :]
    intra_decay = jnp.where(rel[None] >= 0,
                            jnp.exp(log_gamma[:, None, None] * jnp.maximum(rel, 0.0)[None]), 0.0)
    q = q.astype(jnp.float32).reshape(b, nc, CHUNK, h, d)
    k = k.astype(jnp.float32).reshape(b, nc, CHUNK, h, d) * (d ** -0.5)
    v = v.astype(jnp.float32).reshape(b, nc, CHUNK, h, d)
    scores = jnp.einsum('bnihd,bnjhd->bnhij', q, k) * intra_decay
    o_intra = jnp.einsum('bnhij,bnjhe->bnihe', scores, v)
    k_decay = jnp.exp(log_gamma[None, :] * (CHUNK - 1.0 - idx)[:, None])
    kv = jnp.einsum('bnjhd,jh,bnjhe->bnhde', k, k_decay, v)
    chunk_decay = jnp.exp(log_gamma * CHUNK)[None, :, None, None]

    def step(state, kv_c):
        return chunk_decay * state + kv_c, state

    init = jnp.zeros((b, h, d, d), jnp.float32)
    _, states = lax.scan(step, init, jnp.moveaxis(kv, 1, 0))
    states = jnp.moveaxis(states, 0, 1)
    q_decay = jnp.exp(log_gamma[None, :] * (idx + 1.0)[:, None])
    o_cross = jnp.einsum('bnihd,ih,bnhde->bnihe', q, q_decay, states)
    return (o_intra + o_cross).reshape(b, s, h, d)

def diff_attention(q, k, v, lam):
    b, s, h, _, dh = q.shape
    dv = v.shape[-1]
    nb = s // Q_BLOCK
    slopes = jnp.exp2(-8.0 * jnp.arange(1, h + 1, dtype=jnp.float32) / h)
    scale = dh ** -0.5
    kpos = jnp.arange(s)
    qb = jnp.moveaxis(q.reshape(b, nb, Q_BLOCK, h, 2, dh), 1, 0)

    def block(args):
        q_blk, blk = args
        qpos = blk * Q_BLOCK + jnp.arange(Q_BLOCK)
        dist = (qpos[:, None] - kpos[None, :]).astype(jnp.float32)
        sc = jnp.einsum('bqhmd,bkhmd->bhmqk', q_blk, k).astype(jnp.float32) * scale
        sc = sc - slopes[None, :, None, None, None] * dist
        sc = jnp.where(dist >= 0, sc, NEG_BIG)
        p = jax.nn.softmax(sc, axis=-1)
        a = p[:, :, 0] - lam * p[:, :, 1]
        return jnp.einsum('bhqk,bkhe->bqhe', a.astype(v.dtype), v)

    out = lax.map(block, (qb, jnp.arange(nb)))
    return jnp.moveaxis(out, 0, 1).reshape(b, s, h, dv)

def hybrid_mixer(h, w_in, ret_norm, diff_q_norm, diff_k_norm,
                 lambda_q1, lambda_k1, lambda_q2, lambda_k2, diff_norm, w_out, lam_init):
    b, s, _ = h.shape
    proj = h @ w_in
    cuts = [RET_WIDTH, 2 * RET_WIDTH, 3 * RET_WIDTH, 4 * RET_WIDTH,
            4 * RET_WIDTH + DIFF_WIDTH, 4 * RET_WIDTH + 2 * DIFF_WIDTH]
    rq, rk, rv, rg, dq, dk, dvv = jnp.split(proj, cuts, axis=-1)
    shp_r = (b, s, RET_HEADS, RET_HEAD_DIM)
    ro = retention(rq.reshape(shp_r), rk.reshape(shp_r), rv.reshape(shp_r))
    ro = group_norm(ro, ret_norm).reshape(b, s, RET_WIDTH).astype(h.dtype)
    ro = jax.nn.silu(rg) * ro
    shp_d = (b, s, DIFF_HEADS, 2, DIFF_HALF_DIM)
    dq = rms_norm(dq.reshape(shp_d), diff_q_norm)
    dk = rms_norm(dk.reshape(shp_d), diff_k_norm)
    dvv = dvv.reshape(b, s, DIFF_HEADS, DIFF_V_DIM)
    lam = (jnp.exp(jnp.sum(lambda_q1.astype(jnp.float32) * lambda_k1.astype(jnp.float32)))
           - jnp.exp(jnp.sum(lambda_q2.astype(jnp.float32) * lambda_k2.astype(jnp.float32)))
           + lam_init)
    do = diff_attention(dq, dk, dvv, lam)
    do = (rms_norm(do, diff_norm) * (1.0 - lam_init)).reshape(b, s, DIFF_WIDTH).astype(h.dtype)
    return jnp.concatenate([ro, do], axis=-1) @ w_out

def memory_attention(h, mem_n, w_q, w_kv, w_o, q_norm, k_norm):
    b, s, _ = h.shape
    m = mem_n.shape[1]
    q = rms_norm((h @ w_q).reshape(b, s, MEM_HEADS, MEM_HEAD_DIM), q_norm)
    kv = (mem_n @ w_kv).reshape(b, m, 2, MEM_HEADS, MEM_HEAD_DIM)
    k = rms_norm(kv[:, :, 0], k_norm)
    v = kv[:, :, 1]
    sc = jnp.einsum('bqhd,bkhd->bhqk', q, k).astype(jnp.float32) * (MEM_HEAD_DIM ** -0.5)
    p = jax.nn.softmax(sc, axis=-1).astype(v.dtype)
    o = jnp.einsum('bhqk,bkhd->bqhd', p, v).reshape(b, s, D_MODEL)
    return o @ w_o

def first_inputs(seed: int = 0) -> dict:
    key = jax.random.key(seed)
    ks = iter(jax.random.split(key, 40))

    def dense(fan_in, fan_out):
        return jax.random.normal(next(ks), (DEPTH, fan_in, fan_out), jnp.float32) * fan_in ** -0.5

    def gain(n):
        return 1.0 + 0.02 * jax.random.normal(next(ks), (DEPTH, n), jnp.float32)

    def small(n):
        return 0.1 * jax.random.normal(next(ks), (DEPTH, n), jnp.float32)

    return {
        "x": jax.random.normal(next(ks), (BATCH, SEQ, D_MODEL), jnp.float32),
        "mem": jax.random.normal(next(ks), (BATCH, MEM_LEN, D_MODEL), jnp.float32),
        "norm_ffn1": gain(D_MODEL),
        "ffn1_w1": dense(D_MODEL, D_FF),
        "ffn1_w3": dense(D_MODEL, D_FF),
        "ffn1_w2": dense(D_FF, D_MODEL),
        "norm_mix": gain(D_MODEL),
        "w_in": dense(D_MODEL, IN_COLS),
        "ret_norm": gain(RET_HEAD_DIM),
        "diff_q_norm": gain(DIFF_HALF_DIM),
        "diff_k_norm": gain(DIFF_HALF_DIM),
        "lambda_q1": small(DIFF_HALF_DIM),
        "lambda_k1": small(DIFF_HALF_DIM),
        "lambda_q2": small(DIFF_HALF_DIM),
        "lambda_k2": small(DIFF_HALF_DIM),
        "diff_norm": gain(DIFF_V_DIM),
        "w_out": dense(MIX_WIDTH, D_MODEL),
        "norm_mem_q": gain(D_MODEL),
        "norm_mem_kv": gain(D_MODEL),
        "mem_w_q": dense(D_MODEL, D_MODEL),
        "mem_w_kv": dense(D_MODEL, 2 * D_MODEL),
        "mem_q_norm": gain(MEM_HEAD_DIM),
        "mem_k_norm": gain(MEM_HEAD_DIM),
        "mem_w_o": dense(D_MODEL, D_MODEL),
        "norm_ffn2": gain(D_MODEL),
        "ffn2_w1": dense(D_MODEL, D_FF),
        "ffn2_w3": dense(D_MODEL, D_FF),
        "ffn2_w2": dense(D_FF, D_MODEL),
        "norm_out": gain(D_MODEL),
    }

def first_block(x, mem, norm_ffn1, ffn1_w1, ffn1_w3, ffn1_w2, norm_mix, w_in, ret_norm,
              diff_q_norm, diff_k_norm, lambda_q1, lambda_k1, lambda_q2, lambda_k2, diff_norm,
              w_out, norm_mem_q, norm_mem_kv, mem_w_q, mem_w_kv, mem_q_norm, mem_k_norm, mem_w_o,
              norm_ffn2, ffn2_w1, ffn2_w3, ffn2_w2, norm_out):
    for l in range(DEPTH):
        lam_init = 0.8 - 0.6 * math.exp(-0.3 * l)
        x = x + 0.5 * swiglu(rms_norm(x, norm_ffn1[l]), ffn1_w1[l], ffn1_w3[l], ffn1_w2[l])
        x = x + hybrid_mixer(rms_norm(x, norm_mix[l]), w_in[l], ret_norm[l], diff_q_norm[l],
                             diff_k_norm[l], lambda_q1[l], lambda_k1[l], lambda_q2[l],
                             lambda_k2[l], diff_norm[l], w_out[l], lam_init)
        x = x + memory_attention(rms_norm(x, norm_mem_q[l]), rms_norm(mem, norm_mem_kv[l]),
                                 mem_w_q[l], mem_w_kv[l], mem_w_o[l], mem_q_norm[l], mem_k_norm[l])
        x = x + 0.5 * swiglu(rms_norm(x, norm_ffn2[l]), ffn2_w1[l], ffn2_w3[l], ffn2_w2[l])
        x = rms_norm(x, norm_out[l])
    return x


NEG_INF = -1e30
BIG = 1e30

NSA_HEADS = 16
NSA_GROUPS = 4
NSA_HPG = NSA_HEADS // NSA_GROUPS
NSA_DH = 64
NSA_SCALE = NSA_DH ** -0.5
CMP_BLOCK = 32
CMP_STRIDE = 16
CMP_HIDDEN = 128
SEL_BLOCK = 64
SEL_TOPK = 16
N_LOCAL_FORCED = 2
WINDOW = 512
SEL_QBLOCK = 32
WIN_QBLOCK = 128

ML_HEADS = 4
ML_DH = 128
ML_CHUNK = 64
CONV_WIDTH = 4

MEM_DH = 128
MEM_SCALE = MEM_DH ** -0.5

D_FF_2 = -(-8 * D_MODEL // (3 * 256)) * 256

N_BRANCH = 3
NSA_Q = NSA_HEADS * NSA_DH
NSA_KV = NSA_GROUPS * NSA_DH
ML_W = ML_HEADS * ML_DH
MEM_W = MEM_HEADS * MEM_DH
IN_SPLITS = (NSA_Q, 6 * NSA_KV, 3 * NSA_HEADS, 3 * ML_W, 2 * ML_HEADS, ML_W, MEM_W, N_BRANCH * D_MODEL)
IN_WIDTH = NSA_Q + 6 * NSA_KV + 3 * NSA_HEADS + 3 * ML_W + 2 * ML_HEADS + ML_W + MEM_W + N_BRANCH * D_MODEL


def rmsnorm(x, g):
    xf = x.astype(jnp.float32)
    y = xf * lax.rsqrt(jnp.mean(xf * xf, axis=-1, keepdims=True) + EPS)
    return (y * g.astype(jnp.float32)).astype(x.dtype)

def masked_softmax(s, mask):
    s = jnp.where(mask, s.astype(jnp.float32), NEG_INF)
    return jax.nn.softmax(s, axis=-1) * mask

def compress_blocks(kv, pe, w1, w2):
    S = kv.shape[1]
    n_cmp = (S - CMP_BLOCK) // CMP_STRIDE + 1
    idx = jnp.arange(n_cmp)[:, None] * CMP_STRIDE + jnp.arange(CMP_BLOCK)[None, :]
    blocks = kv[:, idx] + pe[None, None, :, None, :]
    hid = jax.nn.silu(jnp.einsum('bnlgd,ldh->bngh', blocks, w1))
    return jnp.einsum('bngh,hd->bngd', hid, w2)

def nsa_compressed(q, k, v, pe_k, w1_k, w2_k, pe_v, w1_v, w2_v):
    S = q.shape[1]
    kc = compress_blocks(k, pe_k, w1_k, w2_k)
    vc = compress_blocks(v, pe_v, w1_v, w2_v)
    n_cmp = kc.shape[1]
    s = jnp.einsum('bsghd,bngd->bghsn', q, kc) * NSA_SCALE
    t = jnp.arange(S)
    end = jnp.arange(n_cmp) * CMP_STRIDE + CMP_BLOCK - 1
    p = masked_softmax(s, end[None, :] <= t[:, None])
    o = jnp.einsum('bghsn,bngd->bsghd', p.astype(vc.dtype), vc)
    return o, p

def cmp_to_sel_map(n_cmp, n_sel):
    c0 = jnp.arange(n_cmp) * CMP_STRIDE
    s0 = jnp.arange(n_sel) * SEL_BLOCK
    ov = jnp.minimum(c0[:, None] + CMP_BLOCK, s0[None, :] + SEL_BLOCK) - jnp.maximum(c0[:, None], s0[None, :])
    return jnp.clip(ov, 0, None).astype(jnp.float32) / CMP_BLOCK

def nsa_select(p_cmp, S):
    n_cmp = p_cmp.shape[-1]
    n_sel = S // SEL_BLOCK
    imp = jnp.einsum('bghsn,nj->bgsj', p_cmp, cmp_to_sel_map(n_cmp, n_sel))
    qblk = jnp.arange(S) // SEL_BLOCK
    j = jnp.arange(n_sel)
    rel = qblk[:, None] - j[None, :]
    causal = rel >= 0
    forced = causal & ((j[None, :] == 0) | (rel < N_LOCAL_FORCED))
    score = jnp.where(forced, BIG, jnp.where(causal, imp, NEG_INF))
    top_s, top_i = lax.top_k(score, min(SEL_TOPK, n_sel))
    return top_i, top_s > 0.5 * NEG_INF

def nsa_selected(q, k, v, top_i, top_ok):
    B, S, G, HPG, dh = q.shape
    n_sel = S // SEL_BLOCK
    nk = top_i.shape[-1]
    nq = S // SEL_QBLOCK
    kb = k.reshape(B, n_sel, SEL_BLOCK, G, dh).transpose(0, 3, 1, 2, 4)
    vb = v.reshape(B, n_sel, SEL_BLOCK, G, dh).transpose(0, 3, 1, 2, 4)
    qb = jnp.moveaxis(q.reshape(B, nq, SEL_QBLOCK, G, HPG, dh), 1, 0)
    ib = jnp.moveaxis(top_i.reshape(B, G, nq, SEL_QBLOCK, nk), 2, 0)
    mb = jnp.moveaxis(top_ok.reshape(B, G, nq, SEL_QBLOCK, nk), 2, 0)
    bi = jnp.arange(B)[:, None, None, None]
    gi = jnp.arange(G)[None, :, None, None]

    def body(args):
        qi, ii, mi, blk = args
        kg = kb[bi, gi, ii]
        vg = vb[bi, gi, ii]
        tpos = blk * SEL_QBLOCK + jnp.arange(SEL_QBLOCK)
        kpos = ii[..., None] * SEL_BLOCK + jnp.arange(SEL_BLOCK)
        mask = mi[..., None] & (kpos <= tpos[None, None, :, None, None])
        s = jnp.einsum('bqghd,bgqnld->bghqnl', qi, kg) * NSA_SCALE
        p = masked_softmax(s.reshape(B, G, HPG, SEL_QBLOCK, nk * SEL_BLOCK),
                           mask.reshape(B, G, 1, SEL_QBLOCK, nk * SEL_BLOCK))
        p = p.reshape(B, G, HPG, SEL_QBLOCK, nk, SEL_BLOCK).astype(vg.dtype)
        return jnp.einsum('bghqnl,bgqnld->bqghd', p, vg)

    out = lax.map(body, (qb, ib, mb, jnp.arange(nq)))
    return jnp.moveaxis(out, 0, 1).reshape(B, S, G, HPG, dh)

def nsa_window(q, k, v):
    B, S, G, HPG, dh = q.shape
    nq = S // WIN_QBLOCK
    span = WIN_QBLOCK + WINDOW
    kp = jnp.pad(k, ((0, 0), (WINDOW, 0), (0, 0), (0, 0)))
    vp = jnp.pad(v, ((0, 0), (WINDOW, 0), (0, 0), (0, 0)))
    qb = jnp.moveaxis(q.reshape(B, nq, WIN_QBLOCK, G, HPG, dh), 1, 0)

    def body(args):
        qi, blk = args
        start = blk * WIN_QBLOCK
        ks = lax.dynamic_slice_in_dim(kp, start, span, axis=1)
        vs = lax.dynamic_slice_in_dim(vp, start, span, axis=1)
        tpos = start + jnp.arange(WIN_QBLOCK)
        kpos = start - WINDOW + jnp.arange(span)
        d = tpos[:, None] - kpos[None, :]
        mask = (d >= 0) & (d < WINDOW) & (kpos[None, :] >= 0)
        s = jnp.einsum('bqghd,bkgd->bghqk', qi, ks) * NSA_SCALE
        p = masked_softmax(s, mask).astype(vs.dtype)
        return jnp.einsum('bghqk,bkgd->bqghd', p, vs)

    out = lax.map(body, (qb, jnp.arange(nq)))
    return jnp.moveaxis(out, 0, 1).reshape(B, S, G, HPG, dh)

def causal_conv(x, w, b):
    C = x.shape[-1]
    y = lax.conv_general_dilated(x, w[:, None, :], window_strides=(1,), padding=[(CONV_WIDTH - 1, 0)],
                                 dimension_numbers=('NWC', 'WIO', 'NWC'), feature_group_count=C)
    return y + b

def mlstm_chunkwise(q, k, v, i_pre, logf):
    B, S, H, dh = q.shape
    L = ML_CHUNK
    nc = S // L
    q = q.astype(jnp.float32)
    k = k.astype(jnp.float32) * (dh ** -0.5)
    v = v.astype(jnp.float32)

    def chunks(a):
        return jnp.moveaxis(a.reshape(B, nc, L, *a.shape[2:]), 1, 0)

    tril = jnp.tril(jnp.ones((L, L), dtype=bool))

    def step(carry, xs):
        C, n, m = carry
        qj, kj, vj, ij, fj = xs
        qh = qj.transpose(0, 2, 1, 3)
        kh = kj.transpose(0, 2, 1, 3)
        vh = vj.transpose(0, 2, 1, 3)
        b = jnp.cumsum(fj, axis=1).transpose(0, 2, 1)
        ih = ij.transpose(0, 2, 1)
        dlog = jnp.where(tril, b[..., :, None] - b[..., None, :] + ih[..., None, :], -jnp.inf)
        inter = b + m[..., None]
        m_t = jnp.maximum(inter, jnp.max(dlog, axis=-1))
        dw = jnp.exp(dlog - m_t[..., None])
        iw = jnp.exp(inter - m_t)
        sqk = jnp.einsum('bhld,bhsd->bhls', qh, kh) * dw
        num = jnp.einsum('bhls,bhsd->bhld', sqk, vh) + iw[..., None] * jnp.einsum('bhed,bhld->bhle', C, qh)
        den = jnp.sum(sqk, axis=-1) + iw * jnp.einsum('bhd,bhld->bhl', n, qh)
        h = num / jnp.maximum(jnp.abs(den), jnp.exp(-m_t))[..., None]
        b_end = b[..., -1]
        wlog = b_end[..., None] - b + ih
        m_new = jnp.maximum(b_end + m, jnp.max(wlog, axis=-1))
        ws = jnp.exp(wlog - m_new[..., None])
        decay = jnp.exp(b_end + m - m_new)
        C_new = decay[..., None, None] * C + jnp.einsum('bhs,bhse,bhsd->bhed', ws, vh, kh)
        n_new = decay[..., None] * n + jnp.einsum('bhs,bhsd->bhd', ws, kh)
        return (C_new, n_new, m_new), h

    init = (jnp.zeros((B, H, dh, dh), jnp.float32), jnp.zeros((B, H, dh), jnp.float32), jnp.zeros((B, H), jnp.float32))
    _, hs = lax.scan(step, init, (chunks(q), chunks(k), chunks(v), chunks(i_pre), chunks(logf)))
    return hs.transpose(1, 0, 3, 2, 4).reshape(B, S, H, dh)

def memory_xattn(q, mem, g, w_kv):
    B, S, _ = q.shape
    M = mem.shape[1]
    kv = rmsnorm(mem, g) @ w_kv
    k = kv[..., :MEM_W].reshape(B, M, MEM_HEADS, MEM_DH)
    v = kv[..., MEM_W:].reshape(B, M, MEM_HEADS, MEM_DH)
    qh = q.reshape(B, S, MEM_HEADS, MEM_DH)
    s = jnp.einsum('bshd,bmhd->bhsm', qh, k).astype(jnp.float32) * MEM_SCALE
    p = jax.nn.softmax(s, axis=-1).astype(v.dtype)
    return jnp.einsum('bhsm,bmhd->bshd', p, v).reshape(B, S, MEM_W)

def second_inputs(seed: int = 0) -> dict:
    key = jax.random.key(seed)
    ks = jax.random.split(key, 32)
    L = DEPTH

    def nrm(k, shape, scale):
        return jax.random.normal(k, shape, jnp.float32) * scale

    def gain(k, shape):
        return 1.0 + 0.05 * jax.random.normal(k, shape, jnp.float32)

    gate_b = jnp.concatenate([
        0.1 * jax.random.normal(ks[10], (L, ML_HEADS), jnp.float32),
        jnp.linspace(3.0, 6.0, ML_HEADS, dtype=jnp.float32)[None, :] + 0.1 * jax.random.normal(ks[11], (L, ML_HEADS), jnp.float32),
    ], axis=-1)
    return {
        "x": nrm(ks[0], (BATCH, SEQ, D_MODEL), 1.0),
        "mem": nrm(ks[1], (BATCH, MEM_LEN, D_MODEL), 1.0),
        "g_pre_mix": gain(ks[2], (L, D_MODEL)),
        "w_in": nrm(ks[3], (L, D_MODEL, IN_WIDTH), D_MODEL ** -0.5),
        "cmp_pe_k": nrm(ks[4], (L, CMP_BLOCK, NSA_DH), 0.1),
        "cmp_w1_k": nrm(ks[5], (L, CMP_BLOCK, NSA_DH, CMP_HIDDEN), (CMP_BLOCK * NSA_DH) ** -0.5),
        "cmp_w2_k": nrm(ks[6], (L, CMP_HIDDEN, NSA_DH), CMP_HIDDEN ** -0.5),
        "cmp_pe_v": nrm(ks[7], (L, CMP_BLOCK, NSA_DH), 0.1),
        "cmp_w1_v": nrm(ks[8], (L, CMP_BLOCK, NSA_DH, CMP_HIDDEN), (CMP_BLOCK * NSA_DH) ** -0.5),
        "cmp_w2_v": nrm(ks[9], (L, CMP_HIDDEN, NSA_DH), CMP_HIDDEN ** -0.5),
        "ml_conv_w": nrm(ks[12], (L, CONV_WIDTH, 2 * ML_W), CONV_WIDTH ** -0.5),
        "ml_conv_b": nrm(ks[13], (L, 2 * ML_W), 0.02),
        "ml_gate_b": gate_b,
        "ml_head_g": gain(ks[14], (L, ML_W)),
        "g_mem": gain(ks[15], (L, D_MODEL)),
        "w_mem_kv": nrm(ks[16], (L, D_MODEL, 2 * MEM_W), D_MODEL ** -0.5),
        "w_proj_nsa": nrm(ks[17], (L, NSA_Q, D_MODEL), NSA_Q ** -0.5),
        "w_proj_ml": nrm(ks[18], (L, ML_W, D_MODEL), ML_W ** -0.5),
        "w_proj_mem": nrm(ks[19], (L, MEM_W, D_MODEL), MEM_W ** -0.5),
        "w_out": nrm(ks[20], (L, D_MODEL, D_MODEL), D_MODEL ** -0.5),
        "g_post_mix": gain(ks[21], (L, D_MODEL)),
        "g_pre_ffn": gain(ks[22], (L, D_MODEL)),
        "w_ffn_in": nrm(ks[23], (L, D_MODEL, 2 * D_FF_2), D_MODEL ** -0.5),
        "w_ffn_down": nrm(ks[24], (L, D_FF_2, D_MODEL), D_FF_2 ** -0.5),
        "g_post_ffn": gain(ks[25], (L, D_MODEL)),
    }

def second_block(x, mem, g_pre_mix, w_in, cmp_pe_k, cmp_w1_k, cmp_w2_k, cmp_pe_v, cmp_w1_v, cmp_w2_v,
              ml_conv_w, ml_conv_b, ml_gate_b, ml_head_g, g_mem, w_mem_kv, w_proj_nsa, w_proj_ml,
              w_proj_mem, w_out, g_post_mix, g_pre_ffn, w_ffn_in, w_ffn_down, g_post_ffn):
    B, S, _ = x.shape
    offsets = np.cumsum(IN_SPLITS)[:-1].tolist()
    for l in range(DEPTH):
        h = rmsnorm(x, g_pre_mix[l])
        z = h @ w_in[l]
        q_nsa, kv_nsa, g_nsa, qkv_ml, if_ml, o_ml, q_mem, g_merge = jnp.split(z, offsets, axis=-1)

        q = q_nsa.reshape(B, S, NSA_GROUPS, NSA_HPG, NSA_DH)
        kv = kv_nsa.reshape(B, S, 6, NSA_GROUPS, NSA_DH)
        o_cmp, p_cmp = nsa_compressed(q, kv[:, :, 0], kv[:, :, 1], cmp_pe_k[l], cmp_w1_k[l], cmp_w2_k[l],
                                      cmp_pe_v[l], cmp_w1_v[l], cmp_w2_v[l])
        top_i, top_ok = nsa_select(p_cmp, S)
        o_slc = nsa_selected(q, kv[:, :, 2], kv[:, :, 3], top_i, top_ok)
        o_win = nsa_window(q, kv[:, :, 4], kv[:, :, 5])
        gb = jax.nn.sigmoid(g_nsa.reshape(B, S, NSA_GROUPS, NSA_HPG, 3))
        y_nsa = (gb[..., 0:1] * o_cmp + gb[..., 1:2] * o_slc + gb[..., 2:3] * o_win).reshape(B, S, NSA_Q)

        qk = jax.nn.silu(causal_conv(qkv_ml[..., :2 * ML_W], ml_conv_w[l], ml_conv_b[l]))
        q_m = qk[..., :ML_W].reshape(B, S, ML_HEADS, ML_DH)
        k_m = qk[..., ML_W:].reshape(B, S, ML_HEADS, ML_DH)
        v_m = qkv_ml[..., 2 * ML_W:].reshape(B, S, ML_HEADS, ML_DH)
        gates = if_ml.astype(jnp.float32) + ml_gate_b[l].astype(jnp.float32)
        i_pre = gates[..., :ML_HEADS]
        logf = jax.nn.log_sigmoid(gates[..., ML_HEADS:])
        h_ml = mlstm_chunkwise(q_m, k_m, v_m, i_pre, logf)
        h_ml = h_ml * lax.rsqrt(jnp.mean(h_ml * h_ml, axis=-1, keepdims=True) + EPS)
        h_ml = h_ml.reshape(B, S, ML_W) * ml_head_g[l].astype(jnp.float32)
        y_ml = (jax.nn.sigmoid(o_ml.astype(jnp.float32)) * h_ml).astype(x.dtype)

        y_mem = memory_xattn(q_mem, mem, g_mem[l], w_mem_kv[l])

        gm = jax.nn.sigmoid(g_merge.reshape(B, S, N_BRANCH, D_MODEL))
        y = (gm[:, :, 0] * (y_nsa @ w_proj_nsa[l]) + gm[:, :, 1] * (y_ml @ w_proj_ml[l])
             + gm[:, :, 2] * (y_mem @ w_proj_mem[l]))
        x = x + rmsnorm(y @ w_out[l], g_post_mix[l])

        h = rmsnorm(x, g_pre_ffn[l])
        gu = h @ w_ffn_in[l]
        gate, up = gu[..., :D_FF_2], gu[..., D_FF_2:]
        x = x + rmsnorm((jax.nn.silu(gate) * up) @ w_ffn_down[l], g_post_ffn[l])
    return x


def setup_inputs(seed=0):
    out = dict(first_inputs(seed))
    for name, value in second_inputs(seed + 1).items():
        if name != "x":
            out[name + "_2"] = value
    return out


def reference(
    x, mem, norm_ffn1, ffn1_w1, ffn1_w3, ffn1_w2, norm_mix, w_in, ret_norm, diff_q_norm,
    diff_k_norm, lambda_q1, lambda_k1, lambda_q2, lambda_k2, diff_norm, w_out, norm_mem_q,
    norm_mem_kv, mem_w_q, mem_w_kv, mem_q_norm, mem_k_norm, mem_w_o, norm_ffn2, ffn2_w1,
    ffn2_w3, ffn2_w2, norm_out, mem_2, g_pre_mix_2, w_in_2, cmp_pe_k_2, cmp_w1_k_2, cmp_w2_k_2,
    cmp_pe_v_2, cmp_w1_v_2, cmp_w2_v_2, ml_conv_w_2, ml_conv_b_2, ml_gate_b_2, ml_head_g_2,
    g_mem_2, w_mem_kv_2, w_proj_nsa_2, w_proj_ml_2, w_proj_mem_2, w_out_2, g_post_mix_2,
    g_pre_ffn_2, w_ffn_in_2, w_ffn_down_2, g_post_ffn_2,
):
    x = first_block(
        x, mem, norm_ffn1, ffn1_w1, ffn1_w3, ffn1_w2, norm_mix, w_in, ret_norm, diff_q_norm,
        diff_k_norm, lambda_q1, lambda_k1, lambda_q2, lambda_k2, diff_norm, w_out, norm_mem_q,
        norm_mem_kv, mem_w_q, mem_w_kv, mem_q_norm, mem_k_norm, mem_w_o, norm_ffn2, ffn2_w1,
        ffn2_w3, ffn2_w2, norm_out,
    )
    return second_block(
        x, mem_2, g_pre_mix_2, w_in_2, cmp_pe_k_2, cmp_w1_k_2, cmp_w2_k_2, cmp_pe_v_2,
        cmp_w1_v_2, cmp_w2_v_2, ml_conv_w_2, ml_conv_b_2, ml_gate_b_2, ml_head_g_2, g_mem_2,
        w_mem_kv_2, w_proj_nsa_2, w_proj_ml_2, w_proj_mem_2, w_out_2, g_post_mix_2, g_pre_ffn_2,
        w_ffn_in_2, w_ffn_down_2, g_post_ffn_2,
    )


_drawn_inputs = setup_inputs


def setup_inputs(seed=0):
    import zlib

    import numpy as np

    out = dict(_drawn_inputs(seed))
    spreads = {}
    factors = {'norm_ffn1': 3.304,
     'ret_norm': 5.545,
     'diff_q_norm': 4.184,
     'diff_k_norm': 4.155,
     'diff_norm': 3.497,
     'norm_mem_q': 8.0,
     'norm_mem_kv': 8.0,
     'mem_q_norm': 8.0,
     'mem_k_norm': 8.0,
     'norm_ffn2': 6.054,
     'cmp_pe_k_2': 64.0,
     'ml_conv_b_2': 28.545,
     'g_mem_2': 5.377,
     'cmp_w1_k_2': 5.018,
     'cmp_w2_k_2': 5.064,
     'cmp_pe_v_2': 8.0,
     'ml_head_g_2': 8.0}
    for name, (base, spread) in spreads.items():
        noise = np.random.default_rng([zlib.crc32(name.encode()), seed]).standard_normal(out[name].shape)
        drawn = base * np.exp(spread * noise) if base else spread * noise
        out[name] = __import__('jax').numpy.asarray(drawn.astype(out[name].dtype))
    for name, factor in factors.items():
        out[name] = (out[name] * factor).astype(out[name].dtype)
    return out
```

```python
from contextlib import ExitStack, contextmanager

import numpy as np

import concourse.bass as bass
from concourse import mybir

F32 = mybir.dt.float32
ACT = mybir.ActivationFunctionType
ALU = mybir.AluOpType
AX = mybir.AxisListType

P = 128
D = 1024
T = 512
M = 256
KD = D // P
TT = T // P
MT = M // P
FF = 2816
KF = FF // P
KH = KF // 2
EPS = 1e-6
NEG = -1e30
HEADS = 4
CMP_L, CMP_S, CMP_N = 32, 16, 31
GROUPS = 4
LAM_INIT = 0.2
SLOTS = 6

G_FFN1, G_MIX, G_MEMQ, G_MEMKV, G_FFN2, G_OUT, G_PRE2, G_MEM2, G_POST2, G_PREF2, G_POSTF2 = range(0, 88, 8)
C_RET, C_DQ, C_DK, C_DN = 88, 89, 90, 91
C_MQ, C_MK = 92, 94
C_LAM = 96
C_HEAD = 100
C_HEADN = 11
C_GATEB = C_HEAD + HEADS * C_HEADN
C_PE = C_GATEB + 8
NPAR = C_PE + CMP_L

K_ID, K_ONE, K_BLK = 0, 128, 256
K_BASE = 384
K_CAUS = 0
K_CAUST = 512
K_CUM = 1024
K_CADD = 1536
K_CMUL = K_CADD + TT * CMP_N
K_SEL = K_CMUL + TT * CMP_N
NTAB = K_SEL + HEADS * P

NORM = dict(stats=1, free3=1, rcp=1, rinv=1, hs=KD)
SQUARES = dict(squares=KD, sums=KD, cleared=1)
CLEAR = dict(cleared=1)
RESCALE = dict(stats=1, free3=1, rcp=1, rinv=1, xs=KD, squares=KD, sums=KD, cleared=1)
FFN_UP = dict(products=4, free0=2, free1=2)
FFN_DOWN = dict(products=4, xs=2, squares=2, sums=2)
FFN_DOWN_Z = dict(products=4, free0=1, free1=1, squares=2, sums=2)
OUT_X = dict(products=4, xs=4, squares=4, sums=4)
OUT_Z = dict(products=4, free0=2, free1=2, squares=4, sums=4)
ADD_Z = dict(stats=1, free3=1, rcp=1, rinv=1, dve=KD, xs=KD, squares=KD, sums=KD, cleared=1)
ADD_Z_LAST = dict(stats=1, free3=1, rcp=1, rinv=1, dve=KD, xs=KD)
MEM_NORM = dict(stats=1, free3=1, rcp=1, rinv=1, mems=1)
RET = dict(products=4, free0=2, free1=1, free2=1, strips=1, scores=4, free4=2, free5=2, outs=1, free7=1,
           stats=2, free3=2, sqs=1, rcp=1, rinv=1, dve=1, cats=1)
LAM = dict(stats=1, free3=1, dve=3)
DIFF = dict(products=3, free0=1, free1=1, free2=1, strips=1, stats=3, free3=3, sqs=3, rcp=3, rinv=3,
            scores=8, free4=4, free5=4, negmax=8, exps=8, dve=16, probs=4, turned=4, free6=4,
            outs=1, free7=1, cats=1)
MEM1 = dict(products=6, free0=2, free1=2, free2=1, stats=2, free3=2, sqs=2, rcp=2, rinv=2, qks=4,
            scores=4, free4=2, free5=2, negmax=4, exps=4, dve=4, probs=4, turned=4, free6=4,
            outs=2, free7=2)
NJ = 32
NSA_PRE = dict(stats=1, free3=1, turned=1, free6=1)
NSA = dict(products=5, free0=2, free1=2, free2=1, heads=1, twins=1, stats=2, free3=2,
           scores=8 + NJ, free4=4 + NJ // 2, free5=4 + NJ // 2, cmps=4, negmax=NJ, exps=4 + NJ,
           dve=20 + NJ, probs=4 + NJ, turned=2 + 4 + NJ, free6=2 + 4 + NJ, outs=2, free7=2)
GATES = dict(gates=1, acts=5, free2=1, dve=4, stats=2, free3=2, turned=1, free6=1)
SPREAD = dict(scores=8, free4=4, free5=4)
ML = dict(products=4, free0=2, free1=1, free2=1, heads=1, dve=15, convs=2, exps=4, scores=4, free4=2,
          free5=2, outs=1, turned=1, free6=1, free7=1, sqs=1, stats=1, free3=1, rcp=1, rinv=1, cats=1)
MEM2 = dict(products=3, free0=1, free1=1, free2=1, scores=4, free4=2, free5=2, negmax=4, exps=4,
            dve=4, probs=4, turned=4, free6=4, outs=1, free7=1)
MERGE = dict(products=6, free0=3, free1=3, dve=2)

STREAM = [
    (KF // 2, FFN_UP, [8] * 4), (4, FFN_DOWN, [KH] * 4),
    (HEADS, RET, [8] * 4), (HEADS, DIFF, [8] * 3), (2, OUT_X, [8] * 4),
    (HEADS, MEM1, [8] * 6), (2, OUT_X, [8] * 4),
    (KF // 2, FFN_UP, [8] * 4), (4, FFN_DOWN, [KH] * 4),
    (GROUPS, NSA, [8] * 5), (HEADS, ML, [8] * 4), (HEADS, MEM2, [8] * 3),
    (KD, MERGE, [8, 8, 8, 4, 8, 4]), (2, OUT_Z, [8] * 4),
    (KF // 2, FFN_UP, [8] * 4), (4, FFN_DOWN_Z, [KH] * 4),
]


class Counts:

    def __init__(self):
        self.base = {**{f"free{b}": 1 for b in range(8)}, "cats": 1, "xs": 1}
        self.turn, self.events = None, {}

    def at(self, name, more=0):
        value = self.base.get(name, 0) + more
        if self.turn is not None and self.events.get(name, 0):
            value = self.turn * self.events[name] + value
        return value

    def past(self, events, turns=1):
        for name, k in events.items():
            self.base[name] = self.base.get(name, 0) + k * turns
        for slot in range(SLOTS):
            if slot in range(events.get("products", 0)):
                self.base[f"loads{slot}"] = self.base.get(f"loads{slot}", 0) + turns

    @contextmanager
    def turns(self, engine, turns, events):
        with engine.Fori(0, turns) as i:
            self.turn = i
            self.events = {**events, **{f"loads{s}": 1 for s in range(events["products"])}}
            yield i
        self.turn, self.events = None, {}
        self.past(events, turns)


def build(nc, xT, memT, mem2T, par, con, tab, headtab, w8, w11, w4, gatew, cmpw1, cmpw2, outT):
    with ExitStack() as ctx:
        def sb(name, *shape):
            return ctx.enter_context(nc.sbuf_tensor(name, [P, *shape], F32))

        def sem(name):
            return ctx.enter_context(nc.semaphore(name))

        bank = [ctx.enter_context(nc.psum_tensor(f"bank{b}", [P, 512], F32)) for b in range(8)]

        x = sb("x", KD, T)
        h = sb("h", KD, T)
        hid = sb("hid", KF, T)
        big = sb("big", KD * T)
        memh = sb("memh", KD, M)
        slot = [sb(f"slot{s}", KH if s < 4 else KD, P) for s in range(SLOTS)]
        params = sb("params", NPAR)
        consts = sb("consts", K_BASE)
        tables = sb("tables", NTAB)
        gate_w = sb("gate_w", KD, 56)
        w2 = sb("w2", P + 64)
        ssum = sb("ssum", T)
        sq = sb("sq", 2, T)
        sqh = sb("sqh", 2, T)
        var = sb("var", T)
        rc = sb("rc", T)
        rinv = sb("rinv", T)
        silu = sb("silu", 3, T)
        qs = sb("qs", 2, T)
        ks = sb("ks", 2, T)
        vs = sb("vs", T)
        PT = sb("PT", TT, T)
        sc = sb("sc", 2, T)
        ex = sb("ex", 3, T)
        strip = sb("strip", T)
        lanes = sb("lanes", 64)
        hp = sb("hp", 16)
        gates = sb("gates", TT, 48)
        ggate = sb("ggate", TT, 12)
        ifp = sb("ifp", TT, 8)
        lf = sb("lf", 4, TT, 4)
        acol = sb("acol", HEADS, TT)
        hidk = sb("hidk", CMP_N)
        hidv = sb("hidv", 4, 32)
        kc2 = sb("kc2", CMP_N)
        vb = sb("vb", 2, P)
        pc = sb("pc", 4, 32)
        small = sb("small", 16)
        o_sb = sb("o_sb", 2, T)
        xp = sb("xp", 2, T + 3)

        big8 = big[:, :].rearrange("p (k t) -> p k t", k=KD)
        w1c = big[:, :].rearrange("p (l h) -> p l h", l=CMP_L)
        kvc, PTc = o_sb[:, 0, :], o_sb[:, 1, :]
        rows = hid[:, 18:22, :]
        negM, emb = big8[:, 0:HEADS, :], big8[:, HEADS:2 * HEADS, :]
        ident, ones, blocks64 = consts[:, K_ID:K_ID + P], consts[:, K_ONE:K_ONE + P], consts[:, K_BLK:K_BLK + P]
        negmax, esum = lanes[:, 0:2], lanes[:, 4:7]
        nlam, dn_gain, rsm = lanes[:, 8:9], lanes[:, 9:10], lanes[:, 10:13]
        pebias = lanes[:, 14:16]
        le = lanes[:, 16:18]
        lprod = lanes[:, 18:20]
        maxs = lanes[:, 20:22]
        cmx, csum, cgate = lanes[:, 24:28], lanes[:, 28:32], lanes[:, 32:36]

        x_loaded = sem("x_loaded")
        params_loaded = sem("params_loaded")
        consts_loaded = sem("consts_loaded")
        tables_loaded = sem("tables_loaded")
        mem_loaded = sem("mem_loaded")
        cmp_loaded = sem("cmp_loaded")
        loaded = [sem(f"slot{s}_loaded") for s in range(SLOTS)]
        strips = sem("head_strip_loaded")
        twins = sem("key_twins_copied")
        stored = sem("stored")
        free = [sem(f"bank{b}_free") for b in range(8)]
        products = sem("panel_products")
        stats = sem("sums_over_partitions")
        scores = sem("scores_made")
        turned = sem("probs_turned")
        outs = sem("attention_out")
        gates_made = sem("gates_made")
        rcp = sem("reciprocal_mean_square")
        hs = sem("h_tiles")
        xs = sem("x_tiles")
        negmaxs = sem("negated_maxima")
        probs = sem("probabilities")
        cmps = sem("shifted_compressed_scores")
        cats = sem("head_outputs")
        mems = sem("memory_normed")
        qks = sem("queries_keys_normed")
        dves = sem("vector_steps")
        rinvs = sem("inverse_rms")
        squares = sem("squares")
        sqs = sem("head_squares")
        exps = sem("exponentials")
        convs = sem("conv_silus")
        acts = sem("scalar_steps")
        sums = sem("square_sums")
        cleared = sem("sum_cleared")
        heads = sem("head_tables")
        zeros_set = sem("zeros_set")

        block = ctx.enter_context(nc.Block())

        @block.sync
        def _(sp):
            n = Counts()
            panel = {8: 0, KH: 0, 4: 0}
            source = {8: w8, KH: w11, 4: w4}
            before = 4
            for phase, (turns, events, ktiles) in enumerate(STREAM):
                c = len(ktiles)
                per = {k: ktiles.count(k) for k in set(ktiles)}
                first = 0
                if phase == 0:
                    for j in range(c):
                        sp.dma_start(slot[j][:, 0:8, :], w8[j]).then_inc(loaded[j], 16)
                    n.past(events)
                    panel[8] += c
                    first = 1
                with n.turns(sp, turns - first, events) as i:
                    for j, k in enumerate(ktiles):
                        sp.wait_ge(products, n.at("products", j + 1 - min(c, before)))
                        at = panel[k] + ktiles[:j].count(k) + i * per[k]
                        src = source[k][bass.ds(at, 1)].rearrange("a p k c -> p (a k) c")
                        sp.dma_start(slot[j][:, 0:k, :], src).then_inc(loaded[j], 16)
                for k in per:
                    panel[k] += per[k] * (turns - first)
                before = c
            n.past(ADD_Z_LAST)
            done = TOTAL["xs"] - KD
            for k in range(KD):
                sp.wait_ge(xs, done + k + 1)
                sp.dma_start(outT[k], x[:, k, :]).then_inc(stored, 16)
            sp.wait_ge(stored, 16 * KD)

        @block.gpsimd
        def _(pool):
            n = Counts()
            for z in (pc[:, :, :], hidv[:, :, :], vb[:, :, :], xp[:, :, 0:3]):
                last = pool.memset(z, 0.0)
            last.then_inc(zeros_set, 1)

            def clear_sum(stat):
                pool.wait_ge(stats, n.at("stats", stat))
                pool.memset(ssum[:, :], 0.0).then_inc(cleared, 1)

            def add_square(k, parity, width=T):
                pool.wait_ge(squares, n.at("squares", k + 1))
                pool.wait_ge(sums, n.at("sums", k))
                pool.tensor_tensor(ssum[:, 0:width], ssum[:, 0:width], sq[:, parity, 0:width],
                                   ALU.add).then_inc(sums, 1)

            def sum_tiles(stat, width=T):
                clear_sum(stat)
                pool.wait_ge(cleared, n.at("cleared", 1))
                for k in range(KD):
                    add_square(k, k % 2, width)

            def sum_in_turns(turns, events, per):
                with n.turns(pool, turns, events):
                    for k in range(per):
                        add_square(k, k % 2)

            def cleared_before_turns():
                clear_sum(0)
                n.past(CLEAR)
                pool.wait_ge(cleared, n.at("cleared"))

            def ffn(down, per):
                n.past(FFN_UP, KF // 2)
                cleared_before_turns()
                sum_in_turns(4, down, per)

            sum_tiles(0)
            n.past(SQUARES)
            n.past(NORM)
            ffn(FFN_DOWN, 2)
            n.past(NORM)
            sum_tiles(0, M)
            n.past(SQUARES)
            n.past(RET, HEADS)
            n.past(LAM)
            n.past(MEM_NORM)
            n.past(DIFF, HEADS)
            cleared_before_turns()
            sum_in_turns(2, OUT_X, 4)
            n.past(NORM)
            n.past(MEM1, HEADS)
            cleared_before_turns()
            sum_in_turns(2, OUT_X, 4)
            n.past(NORM)
            ffn(FFN_DOWN, 2)
            sum_tiles(1)
            n.past(RESCALE)
            n.past(NORM)
            sum_tiles(0, M)
            n.past(SQUARES)
            n.past(GATES)
            n.past(NSA_PRE)
            with n.turns(pool, GROUPS, NSA) as i:
                pool.wait_ge(probs, n.at("probs"))
                pool.wait_ge(acts, n.at("acts"))
                pool.tensor_copy(ggate[:, :, :], gates[:, :, bass.ds(i * 12, 12)]).then_inc(heads, 1)
            n.past(MEM_NORM)
            n.past(SPREAD)
            with n.turns(pool, HEADS, ML) as i:
                pool.wait_ge(cats, n.at("cats"))
                pool.tensor_copy(hp[:, 12:16], acol[:, bass.ds(i, 1), :].rearrange("p a t -> p (a t)"))
                pool.tensor_copy(hp[:, 0:C_HEADN],
                                 params[:, bass.ds(C_HEAD + i * C_HEADN, C_HEADN)]).then_inc(heads, 1)
            n.past(MEM2, HEADS)
            n.past(MERGE, KD)
            cleared_before_turns()
            sum_in_turns(2, OUT_Z, 4)
            sum_tiles(1)
            n.past(ADD_Z)
            n.past(NORM)
            ffn(FFN_DOWN_Z, 2)

        @block.tensor
        def _(pe):
            n = Counts()

            def panel(j, out, moving, stationary_tokens=False, k0=0, ks_=KD, start=True, stop=True, ready=None):
                pe.wait_ge(loaded[j], 16 * n.at(f"loads{j}", 1))
                if stationary_tokens:
                    for t in range(moving.shape[2] // P):
                        for k in range(ks_):
                            mm = pe.matmul(out(t), moving[:, k, t * P:(t + 1) * P], slot[j][:, k, :],
                                           start=(k == 0), stop=(k == ks_ - 1))
                else:
                    for k in range(ks_):
                        if ready is not None:
                            pe.wait_ge(hs, ready - KD + k + 1)
                        mm = pe.matmul(out, slot[j][:, k, :], moving[:, k0 + k, :],
                                       start=(start and k == 0), stop=(stop and k == ks_ - 1))
                mm.then_inc(products, 1)

            def emptied(b, more=0):
                pe.wait_ge(free[b], n.at(f"free{b}", more))

            def stat(k, matrix, *sources):
                emptied(3, k)
                width = sources[0].shape[1]
                for a, s in enumerate(sources):
                    mm = pe.matmul(bank[3][:, 0:width], matrix, s, start=(a == 0),
                                   stop=(a == len(sources) - 1))
                mm.then_inc(stats, 1)

            def norm(width=T):
                pe.wait_ge(sums, n.at("sums"))
                stat(0, ones, ssum[:, 0:width])

            def ffn(down, resting):
                h_done = n.at("hs")
                with n.turns(pe, KF // 2, FFN_UP):
                    for u in range(2):
                        emptied(0, u)
                        panel(2 * u, bank[0][:, :], h, ready=h_done if u == 0 else None)
                        emptied(1, u)
                        panel(2 * u + 1, bank[1][:, :], h)
                hidden_done = n.at("free1")
                with n.turns(pe, 4, down):
                    for u in range(2):
                        emptied(u)
                        if "xs" in down:
                            pe.wait_ge(xs, n.at("xs"))
                        pe.wait_ge(free[1], hidden_done)
                        panel(2 * u, bank[u][:, :], hid, ks_=KH, stop=False)
                        panel(2 * u + 1, bank[u][:, :], hid, k0=KH, ks_=KH, start=False)

            def out_product(events, moving, ready_sem, ready):
                with n.turns(pe, 2, events):
                    for j in range(4):
                        if "xs" in events:
                            pe.wait_ge(xs, n.at("xs", j - 1))
                        else:
                            emptied(j % 2, j // 2)
                        pe.wait_ge(ready_sem, ready)
                        panel(j, bank[j % 2][:, :], moving)

            def scores_of(k, lhs, rhs, width):
                b = 4 + k % 2
                emptied(b, k // 2)
                for a in range(len(lhs)):
                    mm = pe.matmul(bank[b][:, 0:width], lhs[a], rhs[a], start=(a == 0), stop=(a == len(lhs) - 1))
                mm.then_inc(scores, 1)

            def turn_probs(k, tile, source, p):
                pe.wait_ge(probs, n.at("probs", p))
                emptied(6, k)
                for b in range(tile):
                    mm = pe.transpose(bank[6][:, b * P:(b + 1) * P], source[:, b * P:(b + 1) * P], ident)
                mm.then_inc(turned, 1)

            def causal_out(out, values, start=True):
                for j in range(TT):
                    mm = pe.matmul(out[:, j * P:T], values(j), PT[:, j, j * P:T], start=(start and j == 0),
                                   stop=(start and j == TT - 1), skip_group_check=not start)
                return mm

            pe.wait_ge(consts_loaded, 16)
            n.past(SQUARES)
            norm()
            n.past(NORM)
            ffn(FFN_DOWN, None)
            norm()
            n.past(NORM)
            n.past(SQUARES)

            h_done = n.at("hs")
            with n.turns(pe, HEADS, RET):
                emptied(0)
                panel(0, bank[0][:, :], h, ready=h_done)
                emptied(1)
                panel(1, bank[1][:, :], h)
                emptied(2)
                panel(2, lambda t: bank[2][:, t * P:(t + 1) * P], h, True)
                emptied(0, 1)
                panel(3, bank[0][:, :], h)
                emptied(1, 1)
                emptied(2, 1)
                emptied(7)
                for j in range(TT + 1):
                    if j < TT:
                        scores_of(j, [ks[:, 0, j * P:(j + 1) * P]], [qs[:, 0, j * P:T]], T - j * P)
                    if j >= 1:
                        emptied(4 + (j - 1) % 2, (j - 1) // 2 + 1)
                        mm = pe.matmul(bank[7][:, (j - 1) * P:T], vs[:, (j - 1) * P:j * P],
                                       PT[:, j - 1, (j - 1) * P:T], start=(j == 1), stop=(j == TT))
                mm.then_inc(outs, 1)
                emptied(7, 1)
                stat(0, ones, o_sb[:, 0, :])
                pe.wait_ge(sqs, n.at("sqs", 1))
                stat(1, ones, sqh[:, 0, :])

            pe.wait_ge(dves, n.at("dve", 1))
            emptied(3)
            pe.matmul(bank[3][:, 0:2], ones[0:64, :], lprod[0:64, :], start=True, stop=True).then_inc(stats, 1)
            n.past(LAM)
            norm(M)
            n.past(MEM_NORM)

            with n.turns(pe, HEADS, DIFF):
                emptied(0)
                panel(0, bank[0][:, :], h)
                emptied(1)
                panel(1, bank[1][:, :], h)
                pe.wait_ge(sqs, n.at("sqs", 1))
                stat(0, blocks64, sqh[:, 0, :])
                emptied(2)
                panel(2, lambda t: bank[2][:, t * P:(t + 1) * P], h, True)
                pe.wait_ge(sqs, n.at("sqs", 2))
                stat(1, blocks64, sqh[:, 1, :])
                emptied(0, 1)
                emptied(1, 1)
                emptied(2, 1)
                for s in range(8 + 2):
                    if s < 8:
                        i, m = s // 2, s % 2
                        half = slice(64 * m, 64 * m + 64)
                        scores_of(s, [qs[half, 0, i * P:(i + 1) * P]], [ks[half, 0, 0:(i + 1) * P]], (i + 1) * P)
                    if s >= 2 and s % 2 == 1:
                        i = (s - 2) // 2
                        turn_probs(i, i + 1, o_sb[:, i % 2, :], i + 1)
                emptied(6, 4)
                emptied(7)
                causal_out(bank[7], lambda j: vs[:, j * P:(j + 1) * P]).then_inc(outs, 1)
                pe.wait_ge(sqs, n.at("sqs", 3))
                stat(2, ones, sqh[:, 0, :])
            out_product(OUT_X, hid, cats, n.at("cats"))
            norm()
            n.past(NORM)

            h_done = n.at("hs")
            with n.turns(pe, HEADS, MEM1):
                for c in range(2):
                    emptied(c)
                    panel(c, bank[c][:, :], h, ready=h_done)
                pe.wait_ge(sqs, n.at("sqs", 1))
                stat(0, ones, sqh[:, 0, :], sqh[:, 1, :])
                pe.wait_ge(mems, n.at("mems"))
                for c in range(2):
                    emptied(c, 1)
                    panel(2 + c, bank[c][:, 0:M], memh)
                pe.wait_ge(sqs, n.at("sqs", 2))
                stat(1, ones, sqh[:, 0, 0:M], sqh[:, 1, 0:M])
                emptied(2)
                for c in range(2):
                    panel(4 + c, lambda t: bank[2][:, t * M + c * P:t * M + (c + 1) * P], memh, True)
                pe.wait_ge(qks, n.at("qks", 4))
                emptied(2, 1)
                for s in range(TT + 2):
                    if s < TT:
                        scores_of(s, [qs[:, c, s * P:(s + 1) * P] for c in range(2)],
                                  [ks[:, c, 0:M] for c in range(2)], M)
                    if s >= 2:
                        turn_probs(s - 2, MT, ex[:, (s - 2) % 3, :], s - 1)
                emptied(6, 4)
                for c in range(2):
                    emptied(7, c)
                    for j in range(MT):
                        mm = pe.matmul(bank[7][:, :], vs[:, j * M + c * P:j * M + (c + 1) * P], PT[:, j, :],
                                       start=(j == 0), stop=(j == MT - 1))
                    mm.then_inc(outs, 1)
            out_product(OUT_X, hid, free[7], n.at("free7"))
            norm()
            n.past(NORM)
            ffn(FFN_DOWN, None)
            norm()
            n.past(RESCALE)
            norm()
            n.past(NORM)
            n.past(SQUARES)

            pe.wait_ge(tables_loaded, 16)
            pe.wait_ge(params_loaded, 16)
            pe.wait_ge(cmp_loaded, 48)
            pe.wait_ge(hs, n.at("hs"))
            emptied(2)
            for t in range(TT):
                for k in range(KD):
                    mm = pe.matmul(bank[2][:, t * 56:(t + 1) * 56], h[:, k, t * P:(t + 1) * P], gate_w[:, k, :],
                                   start=(k == 0), stop=(k == KD - 1))
            mm.then_inc(gates_made, 1)
            pe.wait_ge(dves, n.at("dve", 3))
            emptied(3)
            for t in range(TT):
                mm = pe.matmul(bank[3][0:4, t * P:T], lf[:, 1, t, :], tables[:, K_CUM:K_CUM + T - t * P],
                               start=(t == 0), stop=(t == TT - 1))
            mm.then_inc(stats, 1)
            emptied(6)
            for t in range(TT):
                pe.matmul(bank[6][0:4, t * P:T], lf[:, 2, t, :], tables[:, K_CUM:K_CUM + T - t * P],
                          start=(t == 0), stop=False)
            for t in range(TT):
                mm = pe.matmul(bank[6][0:4, t * P:(t + 1) * P], ifp[:, t, 0:4], ident, start=False,
                               stop=(t == TT - 1))
            mm.then_inc(turned, 1)
            emptied(6, 1)
            emptied(3, 1)
            for t in range(TT):
                mm = pe.matmul(bank[3][:, 4 * t:4 * t + 4], rows[0:4, 0, t * P:(t + 1) * P], ident[0:4, 0:4],
                               start=True, stop=True)
            mm.then_inc(stats, 1)
            n.past(GATES)

            for row, b, done in ((slice(0, 64), 3, stats), (slice(64, P), 6, turned)):
                emptied(b)
                for l in range(CMP_L):
                    mm = pe.matmul(bank[b][:, 0:1], w1c[row, l, :], params[row, C_PE + l:C_PE + l + 1],
                                   start=(l == 0), stop=(l == CMP_L - 1))
                mm.then_inc(done, 1)
            n.past(NSA_PRE)

            with n.turns(pe, GROUPS, NSA):
                emptied(0)
                panel(0, bank[0][:, :], h)
                emptied(1)
                panel(1, bank[1][:, :], h)
                emptied(0, 1)
                panel(2, bank[0][:, :], h)
                emptied(1, 1)
                panel(3, bank[1][:, :], h)
                emptied(2)
                panel(4, lambda t: bank[2][:, t * P:(t + 1) * P], h, True)
                emptied(0, 2)
                for row, b, done in ((slice(0, 64), 3, stats), (slice(64, P), 6, turned)):
                    emptied(b)
                    for l in range(CMP_L):
                        mm = pe.matmul(bank[b][:, 0:CMP_N], w1c[row, l, :],
                                       kvc[row, l:l + CMP_S * (CMP_N - 1) + 1:CMP_S],
                                       start=(l == 0), stop=(l == CMP_L - 1))
                    mm.then_inc(done, 1)
                emptied(3, 1)
                pe.matmul(bank[3][:, 0:CMP_N], w2[:, 0:P], hidk[:, :], start=True, stop=True).then_inc(stats, 1)
                emptied(6, 1)
                pe.matmul(bank[6][:, 0:64], hidv[:, :, :].rearrange("p a b -> p (a b)"), w2[:, P:P + 64],
                          start=True, stop=True).then_inc(turned, 1)
                emptied(3, 2)
                emptied(6, 2)
                for i in range(TT + 1):
                    if i < TT:
                        for odd in range(2):
                            half = slice(64 * odd, 64 * odd + 64)
                            emptied(4 + odd, i)
                            for pair in range(2):
                                mm = pe.matmul(bank[4 + odd][:, pair * 32:pair * 32 + CMP_N],
                                               qs[half, pair, i * P:(i + 1) * P], kc2[half, :],
                                               start=True, stop=True)
                            mm.then_inc(scores, 1)
                    if i >= 1:
                        pe.wait_ge(probs, n.at("probs", i))
                        emptied(6, 1 + i)
                        pe.transpose(bank[6][:, 0:P], pc[:, :, :].rearrange("p a b -> p (a b)"), ident).then_inc(turned, 1)
                pe.wait_ge(twins, 32 * n.at("twins", 1))
                emptied(2, 1)
                for s in range(NJ + 3):
                    if s < NJ:
                        head, br, i = s // 8, s // 4 % 2, s % 4
                        half = slice(64 * (head % 2), 64 * (head % 2) + 64)
                        b = 4 + s % 2
                        emptied(b, 4 + s // 2)
                        pe.matmul(bank[b][:, 0:(i + 1) * P], qs[half, head // 2, i * P:(i + 1) * P],
                                  ks[half, br, 0:(i + 1) * P], start=True, stop=True).then_inc(scores, 1)
                    if s >= 3 and (s - 3) % 4 == 3:
                        head, br = (s - 3) // 8, (s - 3) // 4 % 2
                        emptied(6, 6 + s - 2)
                        if head % 2 == 0 and br == 0:
                            emptied(7, head // 2)
                            pe.matmul(bank[7][:, :], vb[:, head // 2, :], PTc, start=True, stop=True)
                        half = slice(64 * (head % 2), 64 * (head % 2) + 64)
                        mm = causal_out(bank[7][half, :], lambda j: vs[:, j * P + 64 * br:j * P + 64 * br + 64],
                                        start=False)
                        if head % 2 == 1 and br == 1:
                            mm.then_inc(outs, 1)
                    if 2 <= s < NJ + 2:
                        turn_probs(6 + s - 2, (s - 2) % 4 + 1, ex[:, (s - 2) % 3, :], 4 + s - 1)
            norm(M)
            n.past(MEM_NORM)

            pe.wait_ge(dves, n.at("dve"))
            pe.wait_ge(acts, n.at("acts"))
            for s in range(8):
                scores_of(s, [tables[0:4, K_SEL + (s % 4) * P:K_SEL + (s % 4 + 1) * P]],
                          [rows[0:4, 1 if s < 4 else 3, :]], T)
            n.past(SPREAD)
            with n.turns(pe, HEADS, ML):
                emptied(0)
                panel(0, bank[0][:, :], h)
                emptied(1)
                panel(1, bank[1][:, :], h)
                emptied(0, 1)
                panel(2, bank[0][:, :], h)
                emptied(2)
                panel(3, lambda t: bank[2][:, t * P:(t + 1) * P], h, True)
                pe.wait_ge(convs, n.at("convs", 2))
                emptied(2, 1)
                emptied(7)
                emptied(6)
                for j in range(TT + 1):
                    if j < TT:
                        scores_of(j, [ks[:, 0, j * P:(j + 1) * P]], [qs[:, 0, j * P:T]], T - j * P)
                    if j >= 1:
                        a = j - 1
                        emptied(4 + a % 2, a // 2 + 1)
                        mm = pe.matmul(bank[7][:, a * P:T], vs[:, a * P:j * P], PT[:, a, a * P:T],
                                       start=(a == 0), stop=(j == TT))
                        if j == TT:
                            mm.then_inc(outs, 1)
                        mm = pe.matmul(bank[6][:, a * P:T], ones, PT[:, a, a * P:T],
                                       start=(a == 0), stop=(j == TT))
                mm.then_inc(turned, 1)
                pe.wait_ge(sqs, n.at("sqs", 1))
                stat(0, ones, sqh[:, 0, :])

            pe.wait_ge(mems, n.at("mems"))
            with n.turns(pe, HEADS, MEM2):
                emptied(0)
                panel(0, bank[0][:, :], h)
                emptied(1)
                panel(1, bank[1][:, 0:M], memh)
                emptied(2)
                panel(2, lambda t: bank[2][:, t * P:(t + 1) * P], memh, True)
                emptied(0, 1)
                emptied(1, 1)
                emptied(2, 1)
                for s in range(TT + 2):
                    if s < TT:
                        scores_of(s, [qs[:, 0, s * P:(s + 1) * P]], [ks[:, 0, 0:M]], M)
                    if s >= 2:
                        turn_probs(s - 2, MT, ex[:, (s - 2) % 3, :], s - 1)
                emptied(6, 4)
                emptied(7)
                for j in range(MT):
                    mm = pe.matmul(bank[7][:, :], vs[:, j * P:(j + 1) * P], PT[:, j, :],
                                   start=(j == 0), stop=(j == MT - 1))
                mm.then_inc(outs, 1)

            branches_done = (n.at("cats"), n.at("free7"))
            with n.turns(pe, KD, MERGE):
                for j, (k0, kt) in enumerate(((0, 8), (8, 4), (12, 4))):
                    emptied(0, j)
                    panel(2 * j, bank[0][:, :], h)
                    emptied(1, j)
                    pe.wait_ge(cats, branches_done[0])
                    pe.wait_ge(free[7], branches_done[1])
                    panel(2 * j + 1, bank[1][:, :], hid, k0=k0, ks_=kt)
            out_product(OUT_Z, big8, dves, n.at("dve"))
            norm()
            n.past(ADD_Z)
            norm()
            n.past(NORM)
            ffn(FFN_DOWN_Z, None)
            norm()
            n.past(ADD_Z_LAST)

        @block.scalar
        def _(act):
            n = Counts()
            act.dma_start(params[:, :], par).then_inc(params_loaded, 16)
            act.dma_start(x[:, :, :], xT).then_inc(x_loaded, 16)
            act.dma_start(consts[:, :], con).then_inc(consts_loaded, 16)
            act.dma_start(memh[:, :, :], memT).then_inc(mem_loaded, 16)
            act.dma_start(tables[:, :], tab).then_inc(tables_loaded, 16)
            act.dma_start(gate_w[:, :, :], gatew).then_inc(cmp_loaded, 16)
            act.dma_start(w1c[:, :, :], cmpw1).then_inc(cmp_loaded, 16)
            act.dma_start(w2[:, :], cmpw2).then_inc(cmp_loaded, 16)

            def square(k, parity, source, first=False):
                if not (first and k < 2):
                    act.wait_ge(sums, n.at("sums", k - 1))
                act.activation(sq[:, parity, 0:source.shape[1]], source, ACT.Square).then_inc(squares, 1)

            def root(k):
                act.wait_ge(rcp, n.at("rcp", k + 1))
                act.activation(rinv[:, :], rc[:, :], ACT.Sqrt).then_inc(rinvs, 1)

            def head_square(k, half, source, read):
                act.wait_ge(stats, n.at("stats", read))
                act.activation(sqh[:, half, 0:source.shape[1]], source, ACT.Square).then_inc(sqs, 1)

            def copy(out, source, b, scale=1.0):
                act.activation(out, source, ACT.Copy, scale=scale).then_inc(free[b], 1)

            def x_squares(turns, events, per):
                with n.turns(act, turns, events) as i:
                    for k in range(per):
                        act.wait_ge(xs, n.at("xs", k + 1))
                        square(k, k % 2, x[:, bass.ds(i * per + k, 1), :].rearrange("p a t -> p (a t)"))

            def z_squares(turns, events, per, z, panels_each):
                with n.turns(act, turns, events) as i:
                    for k in range(per):
                        b = k % 2
                        act.wait_ge(products, n.at("products", panels_each * (k + 1)))
                        square(k, k % 2, bank[b][:, :])
                        copy(z[:, bass.ds(i * per + k, 1), :].rearrange("p a t -> p (a t)"), bank[b][:, :], b)

            def norm():
                root(0)
                n.past(NORM)

            def ffn_up():
                with n.turns(act, KF // 2, FFN_UP):
                    for u in range(2):
                        act.wait_ge(products, n.at("products", 2 * u + 1))
                        act.wait_ge(free[1], n.at("free1", u - 1) if u else n.at("free1"))
                        act.activation(silu[:, u, :], bank[0][:, :], ACT.Silu).then_inc(free[0], 1)

            def ffn():
                ffn_up()
                n.past(CLEAR)
                x_squares(4, FFN_DOWN, 2)
                norm()

            def exponential(k, width):
                act.wait_ge(negmaxs, n.at("negmax", k + 1))
                act.activation(ex[:, k % 3, 0:width], sc[:, k % 2, 0:width], ACT.Exp, bias=negmax[:, k % 2:k % 2 + 1],
                               accum_out=esum[:, k % 3:k % 3 + 1]).then_inc(exps, 1)

            def place_turned(k, i, blocks):
                act.wait_ge(turned, n.at("turned", k + 1))
                copy(PT[:, 0:blocks, i * P:(i + 1) * P],
                     bank[6][:, 0:blocks * P].rearrange("p (a b) -> p a b", a=blocks), 6)

            act.wait_ge(x_loaded, 16)
            for k in range(KD):
                square(k, k % 2, x[:, k, :], first=True)
            n.past(SQUARES)
            norm()
            ffn()
            act.wait_ge(mem_loaded, 16)
            for k in range(KD):
                square(k, k % 2, memh[:, k, :])
            n.past(SQUARES)

            def load_strip(i):
                act.wait_ge(cats, n.at("cats"))
                act.dma_start(strip[:, :], headtab[bass.ds(i, 1)].rearrange("a p t -> p (a t)")).then_inc(strips, 16)

            with n.turns(act, HEADS, RET) as i:
                load_strip(i)
                act.wait_ge(products, n.at("products", 1))
                copy(qs[:, 0, :], bank[0][:, :], 0)
                act.wait_ge(products, n.at("products", 3))
                copy(vs[:, :], bank[2][:, :], 2)
                act.wait_ge(products, n.at("products", 4))
                act.wait_ge(cats, n.at("cats"))
                act.activation(silu[:, 0, :], bank[0][:, :], ACT.Silu).then_inc(free[0], 1)
                act.wait_ge(outs, n.at("outs", 1))
                copy(o_sb[:, 0, :], bank[7][:, :], 7)
                act.wait_ge(free[3], n.at("free3", 1))
                head_square(0, 0, o_sb[:, 1, :], 1)
                root(0)

            act.wait_ge(stats, n.at("stats", 1))
            act.activation(le, bank[3][:, 0:2], ACT.Exp).then_inc(free[3], 1)
            n.past(LAM)
            root(0)
            n.past(MEM_NORM)

            with n.turns(act, HEADS, DIFF) as i:
                load_strip(i + HEADS)
                for c in range(2):
                    act.wait_ge(products, n.at("products", c + 1))
                    head_square(c, c, bank[c][:, :], 0)
                root(0)
                root(1)
                act.wait_ge(products, n.at("products", 3))
                copy(vs[:, :], bank[2][:, :], 2)
                for s in range(8 + 4):
                    if s < 8:
                        exponential(s, (s // 2 + 1) * P)
                    if s >= 4 and s % 2 == 1:
                        i = (s - 4) // 2
                        place_turned(i, i, i + 1)
                act.wait_ge(outs, n.at("outs", 1))
                head_square(2, 0, bank[7][:, :], 2)
                root(2)
            n.past(CLEAR)
            x_squares(2, OUT_X, 4)
            norm()

            with n.turns(act, HEADS, MEM1) as i:
                for c in range(2):
                    act.wait_ge(products, n.at("products", c + 1))
                    act.wait_ge(stats, n.at("stats"))
                    mm = act.activation(sqh[:, c, :], bank[c][:, :], ACT.Square)
                mm.then_inc(sqs, 1)
                root(0)
                for c in range(2):
                    act.wait_ge(products, n.at("products", c + 3))
                    act.wait_ge(stats, n.at("stats", 1))
                    mm = act.activation(sqh[:, c, 0:M], bank[c][:, 0:M], ACT.Square)
                mm.then_inc(sqs, 1)
                root(1)
                act.wait_ge(products, n.at("products", 6))
                copy(vs[:, :], bank[2][:, :], 2)
                for s in range(TT + 2):
                    if s < TT:
                        exponential(s, M)
                    if s >= 2:
                        place_turned(s - 2, s - 2, MT)
                for c in range(2):
                    act.wait_ge(outs, n.at("outs", c + 1))
                    copy(hid[:, bass.ds(i * 2 + c, 1), :].rearrange("p a t -> p (a t)"), bank[7][:, :], 7)
            act.dma_start(memh[:, :, :], mem2T).then_inc(mem_loaded, 16)
            n.past(CLEAR)
            x_squares(2, OUT_X, 4)
            norm()
            ffn_up()
            n.past(CLEAR)
            x_squares(4, FFN_DOWN, 2)
            root(0)
            for k in range(KD):
                act.wait_ge(xs, n.at("xs", k + 1))
                square(k, k % 2, x[:, k, :])
            n.past(RESCALE)
            norm()
            act.wait_ge(mem_loaded, 32)
            for k in range(KD):
                square(k, k % 2, memh[:, k, :])
            n.past(SQUARES)

            act.wait_ge(gates_made, 1)
            g4 = bank[2][:, 0:TT * 56].rearrange("p (t c) -> p t c", t=TT)
            act.activation(gates[:, :, :], g4[:, :, 0:48], ACT.Sigmoid).then_inc(acts, 1)
            act.wait_ge(free[2], n.at("free2", 1))
            act.activation(lf[:, 3, :, :], ifp[:, :, 4:8], ACT.Abs).then_inc(acts, 1)
            act.wait_ge(acts, 2)
            act.activation(lf[:, 3, :, :], lf[:, 3, :, :], ACT.Exp, scale=-1.0).then_inc(acts, 1)
            act.wait_ge(acts, 3)
            act.activation(lf[:, 3, :, :], lf[:, 3, :, :], ACT.Ln, bias=1.0).then_inc(acts, 1)
            act.wait_ge(free[3], n.at("free3", 1))
            act.activation(rows[0:4, 3, :], rows[0:4, 2, :], ACT.Exp, scale=-1.0).then_inc(acts, 1)
            n.past(GATES)
            act.wait_ge(stats, n.at("stats", 1))
            copy(pebias[:, 0:1], bank[3][:, 0:1], 3)
            act.wait_ge(turned, n.at("turned", 1))
            copy(pebias[:, 1:2], bank[6][:, 0:1], 6)
            n.past(NSA_PRE)

            act.wait_ge(free[6], n.at("free6"))
            act.wait_ge(zeros_set, 1)
            with n.turns(act, GROUPS, NSA) as i:
                act.wait_ge(products, n.at("products", 1))
                copy(qs[:, 0, :], bank[0][:, :], 0, 64 ** -0.5)
                act.wait_ge(products, n.at("products", 2))
                copy(qs[:, 1, :], bank[1][:, :], 1, 64 ** -0.5)
                act.wait_ge(products, n.at("products", 3))
                copy(kvc, bank[0][:, :], 0)
                act.wait_ge(products, n.at("products", 4))
                act.activation(ks[0:64, 0, :], bank[1][0:64, :], ACT.Copy)
                copy(ks[64:P, 1, :], bank[1][64:P, :], 1)
                act.wait_ge(free[1], n.at("free1", 2))
                act.dma_start(ks[64:P, 0, :], ks[0:64, 0, :]).then_inc(twins, 16)
                act.dma_start(ks[0:64, 1, :], ks[64:P, 1, :]).then_inc(twins, 16)
                act.wait_ge(products, n.at("products", 5))
                copy(vs[:, :], bank[2][:, :], 2)
                act.wait_ge(stats, n.at("stats", 1))
                act.activation(hidk[:, :], bank[3][:, 0:CMP_N], ACT.Silu, bias=pebias[:, 0:1]).then_inc(free[3], 1)
                act.wait_ge(turned, n.at("turned", 1))
                act.activation(hidv[:, :, 0:CMP_N], bank[6][:, 0:CMP_N].unsqueeze(1).to_broadcast([P, 4, CMP_N]),
                               ACT.Silu, bias=pebias[:, 1:2]).then_inc(free[6], 1)
                act.wait_ge(stats, n.at("stats", 2))
                copy(kc2[:, :], bank[3][:, 0:CMP_N], 3)
                for s in range(TT + 1):
                    if s < TT:
                        act.wait_ge(cmps, n.at("cmps", s + 1))
                        c4 = sc[:, s % 2, 0:P].rearrange("p (a b) -> p a b", a=4)[:, :, 0:CMP_N]
                        e4 = ex[:, s % 2, 0:P].rearrange("p (a b) -> p a b", a=4)[:, :, 0:CMP_N]
                        act.activation(e4, c4, ACT.Exp).then_inc(exps, 1)
                    if s >= 1:
                        act.wait_ge(turned, n.at("turned", 2 + s))
                        copy(PTc[:, (s - 1) * P:s * P], bank[6][:, 0:P], 6)
                for s in range(NJ + 2):
                    if s < NJ:
                        act.wait_ge(negmaxs, n.at("negmax", s + 1))
                        width = (s % 4 + 1) * P
                        act.activation(ex[:, s % 3, 0:width], sc[:, s % 2, 0:width], ACT.Exp,
                                       bias=negmax[:, s % 2:s % 2 + 1],
                                       accum_out=esum[:, s % 3:s % 3 + 1]).then_inc(exps, 1)
                    if s >= 2:
                        place_turned(6 + s - 2, (s - 2) % 4, (s - 2) % 4 + 1)
                    if s >= 3 and (s - 3) % 16 == 15:
                        pair = (s - 3) // 16
                        act.wait_ge(outs, n.at("outs", pair + 1))
                        copy(hid[:, bass.ds(i * 2 + pair, 1), :].rearrange("p a t -> p (a t)"), bank[7][:, :], 7)
                act.wait_ge(outs, n.at("outs", 2))
                copy(hid[:, bass.ds(i * 2 + 1, 1), :].rearrange("p a t -> p (a t)"), bank[7][:, :], 7)
            root(0)
            n.past(MEM_NORM)

            for s in range(8):
                act.wait_ge(scores, n.at("scores", s + 1))
                copy((negM if s < 4 else emb)[:, s % 4, :], bank[4 + s % 2][:, :], 4 + s % 2,
                     -1.0 if s < 4 else 1.0)
            n.past(SPREAD)
            with n.turns(act, HEADS, ML):
                act.wait_ge(heads, n.at("heads", 1))
                for c in range(2):
                    act.wait_ge(products, n.at("products", c + 1))
                    copy(xp[:, c, 3:T + 3], bank[c][:, :], c)
                for c, dst in ((0, qs), (1, ks)):
                    act.wait_ge(dves, n.at("dve", 4 * c + 4))
                    act.activation(dst[:, 0, :], o_sb[:, c, :], ACT.Silu, bias=hp[:, 8 + c:9 + c]).then_inc(convs, 1)
                act.wait_ge(products, n.at("products", 3))
                act.wait_ge(cats, n.at("cats"))
                act.activation(silu[:, 0, :], bank[0][:, :], ACT.Sigmoid).then_inc(free[0], 1)
                act.wait_ge(products, n.at("products", 4))
                copy(vs[:, :], bank[2][:, :], 2)
                for j in range(TT):
                    act.wait_ge(dves, n.at("dve", 9 + j))
                    act.activation(hid[:, 18 + j, 0:T - j * P], hid[:, 18 + j, 0:T - j * P], ACT.Exp).then_inc(exps, 1)
                act.wait_ge(turned, n.at("turned", 1))
                act.activation(var[:, :], bank[6][:, :], ACT.Abs).then_inc(free[6], 1)
                act.wait_ge(free[7], n.at("free7", 1))
                head_square(0, 0, o_sb[:, 0, :], 0)
                root(0)

            with n.turns(act, HEADS, MEM2) as i:
                act.wait_ge(products, n.at("products", 1))
                copy(qs[:, 0, :], bank[0][:, :], 0, P ** -0.5)
                act.wait_ge(products, n.at("products", 2))
                copy(ks[:, 0, 0:M], bank[1][:, 0:M], 1)
                act.wait_ge(products, n.at("products", 3))
                copy(vs[:, 0:MT * P], bank[2][:, 0:MT * P], 2)
                for s in range(TT + 2):
                    if s < TT:
                        exponential(s, M)
                    if s >= 2:
                        place_turned(s - 2, s - 2, MT)
                act.wait_ge(outs, n.at("outs", 1))
                copy(hid[:, bass.ds(i + 12, 1), :].rearrange("p a t -> p (a t)"), bank[7][:, :], 7)

            with n.turns(act, KD, MERGE):
                for j in range(3):
                    act.wait_ge(products, n.at("products", 2 * j + 1))
                    act.wait_ge(free[1], n.at("free1", j) if j < 1 else n.at("free1", j - 1))
                    act.activation(silu[:, j, :], bank[0][:, :], ACT.Sigmoid).then_inc(free[0], 1)
            n.past(CLEAR)
            z_squares(2, OUT_Z, 4, hid, 1)
            root(0)
            for k in range(KD):
                act.wait_ge(xs, n.at("xs", k + 1))
                square(k, k % 2, x[:, k, :])
            n.past(ADD_Z)
            norm()
            ffn_up()
            n.past(CLEAR)
            z_squares(4, FFN_DOWN_Z, 2, big8, 2)
            root(0)
            n.past(ADD_Z_LAST)

        @block.vector
        def _(dve):
            n = Counts()

            def reciprocal_mean(k, r, scale, eps, width=T):
                dve.wait_ge(stats, n.at("stats", k + 1))
                dve.tensor_scalar(var[:, 0:width], bank[3][:, 0:width], scale, eps, ALU.mult, ALU.add).then_inc(free[3], 1)
                dve.wait_ge(free[3], n.at("free3", k + 1))
                dve.reciprocal(rc[:, 0:width], var[:, 0:width]).then_inc(rcp, 1)
                dve.wait_ge(rinvs, n.at("rinv", r + 1))

            def scaled(out, source, gain, width=T):
                return dve.scalar_tensor_tensor(out, source, gain, rinv[:, 0:width], ALU.mult, ALU.mult)

            def apply_norm(g):
                for k in range(KD):
                    scaled(h[:, k, :], x[:, k, :], params[:, g + k:g + k + 1]).then_inc(hs, 1)

            def norm(g):
                reciprocal_mean(0, 0, 1.0 / D, EPS)
                apply_norm(g)
                n.past(NORM)

            def tile(a, k):
                return a[:, bass.ds(k, 1), :].rearrange("p a t -> p (a t)")

            def ffn_up():
                with n.turns(dve, KF // 2, FFN_UP) as i:
                    for u in range(2):
                        dve.wait_ge(free[0], n.at("free0", u + 1))
                        dve.wait_ge(products, n.at("products", 2 * u + 2))
                        dve.tensor_tensor(tile(hid, i * 2 + u), silu[:, u, :], bank[1][:, :],
                                          ALU.mult).then_inc(free[1], 1)

            def ffn_down():
                n.past(CLEAR)
                with n.turns(dve, 4, FFN_DOWN) as i:
                    for u in range(2):
                        dve.wait_ge(products, n.at("products", 2 * u + 2))
                        dve.scalar_tensor_tensor(tile(x, i * 2 + u), bank[u][:, :], 0.5, tile(x, i * 2 + u),
                                                 ALU.mult, ALU.add).then_inc(xs, 1)

            def out_x():
                n.past(CLEAR)
                with n.turns(dve, 2, OUT_X) as i:
                    for k in range(4):
                        dve.wait_ge(products, n.at("products", k + 1))
                        dve.tensor_tensor(tile(x, i * 4 + k), bank[k % 2][:, :], tile(x, i * 4 + k),
                                          ALU.add).then_inc(xs, 1)

            def masked_scores(k, width, mask, b_more=0, s_more=0):
                b = 4 + k % 2
                dve.wait_ge(scores, n.at("scores", s_more + k + 1))
                dve.memset(lanes[:, 42:43], 0.0)
                dve.tensor_tensor_reduce(sc[:, k % 2, 0:width], bank[b][:, 0:width], mask, 1.0, -3e38,
                                         ALU.add, ALU.max, maxs[:, k % 2:k % 2 + 1]).then_inc(free[b], 1)
                dve.wait_ge(free[b], n.at(f"free{b}", b_more + k // 2 + 1))
                dve.tensor_scalar(negmax[:, k % 2:k % 2 + 1], maxs[:, k % 2:k % 2 + 1], -1.0, None,
                                  ALU.mult).then_inc(negmaxs, 1)

            def normalise(k, width, gate=None, d_more=0, e_more=0):
                dve.wait_ge(exps, n.at("exps", e_more + k + 1))
                dve.reciprocal(rsm[:, k % 3:k % 3 + 1], esum[:, k % 3:k % 3 + 1]).then_inc(dves, 1)
                dve.wait_ge(dves, n.at("dve", d_more + k + 1))
                e = ex[:, k % 3, 0:width]
                if gate is None:
                    dve.tensor_scalar(e, e, rsm[:, k % 3:k % 3 + 1], None, ALU.mult).then_inc(probs, 1)
                else:
                    dve.tensor_scalar(e, e, rsm[:, k % 3:k % 3 + 1], gate, ALU.mult, ALU.mult).then_inc(probs, 1)

            no_mask = tables[:, K_CAUS:K_CAUS + M]

            for s in (*free, cats, xs):
                dve.sem_inc(s, 1)
            dve.wait_ge(params_loaded, 16)
            dve.wait_ge(tables_loaded, 16)
            n.past(SQUARES)
            norm(G_FFN1)
            ffn_up()
            ffn_down()
            norm(G_MIX)
            n.past(SQUARES)

            with n.turns(dve, HEADS, RET) as i:
                dve.wait_ge(products, n.at("products", 2))
                dve.tensor_copy(ks[:, 0, :], bank[1][:, :]).then_inc(free[1], 1)
                dve.wait_ge(strips, 16 * n.at("strips", 1))
                for j in range(TT):
                    b = 4 + j % 2
                    dve.wait_ge(scores, n.at("scores", j + 1))
                    dve.tensor_tensor(PT[:, j, j * P:T], bank[b][:, 0:T - j * P], strip[:, 0:T - j * P],
                                      ALU.mult).then_inc(free[b], 1)
                dve.wait_ge(stats, n.at("stats", 1))
                dve.wait_ge(free[7], n.at("free7", 1))
                dve.scalar_tensor_tensor(o_sb[:, 1, :], bank[3][:, :], -1.0 / P, o_sb[:, 0, :],
                                         ALU.mult, ALU.add).then_inc(free[3], 1)
                reciprocal_mean(1, 0, 1.0 / P, EPS)
                scaled(o_sb[:, 1, :], o_sb[:, 1, :], params[:, C_RET:C_RET + 1]).then_inc(dves, 1)
                dve.wait_ge(dves, n.at("dve", 1))
                dve.wait_ge(free[0], n.at("free0", 2))
                dve.tensor_tensor(tile(hid, i), o_sb[:, 1, :], silu[:, 0, :], ALU.mult).then_inc(cats, 1)

            dve.tensor_tensor(lprod[0:64, :], params[0:64, C_LAM:C_LAM + 2], params[0:64, C_LAM + 2:C_LAM + 4],
                              ALU.mult).then_inc(dves, 1)
            dve.tensor_scalar(dn_gain, params[:, C_DN:C_DN + 1], 1.0 - LAM_INIT, None, ALU.mult).then_inc(dves, 1)
            dve.wait_ge(free[3], n.at("free3", 1))
            dve.tensor_scalar(nlam, le[:, 1:2], le[:, 0:1], -LAM_INIT, ALU.subtract, ALU.add).then_inc(dves, 1)
            n.past(LAM)
            dve.wait_ge(dves, n.at("dve"))

            def norm_memory(g):
                reciprocal_mean(0, 0, 1.0 / D, EPS, M)
                for k in range(KD):
                    last = scaled(memh[:, k, :], memh[:, k, :], params[:, g + k:g + k + 1], M)
                last.then_inc(mems, 1)
                n.past(MEM_NORM)

            norm_memory(G_MEMKV)

            with n.turns(dve, HEADS, DIFF) as i:
                reciprocal_mean(0, 0, 1.0, 64 * EPS)
                scaled(qs[:, 0, :], bank[0][:, :], params[:, C_DQ:C_DQ + 1]).then_inc(free[0], 1)
                reciprocal_mean(1, 1, 1.0 / 64, EPS)
                scaled(ks[:, 0, :], bank[1][:, :], params[:, C_DK:C_DK + 1]).then_inc(free[1], 1)
                dve.wait_ge(strips, 16 * n.at("strips", 1))
                for s in range(8 + 1):
                    if s < 8:
                        width = (s // 2 + 1) * P
                        masked_scores(s, width, strip[:, T - width:T])
                    if s >= 1:
                        a, row, m = s - 1, (s - 1) // 2, (s - 1) % 2
                        width = (row + 1) * P
                        r, e = rsm[:, a % 3:a % 3 + 1], ex[:, a % 3, 0:width]
                        dve.wait_ge(exps, n.at("exps", a + 1))
                        dve.reciprocal(r, esum[:, a % 3:a % 3 + 1]).then_inc(dves, 1)
                        dve.wait_ge(dves, n.at("dve", 2 * a + 1))
                        if m == 0:
                            dve.tensor_scalar(e, e, r, None, ALU.mult).then_inc(dves, 1)
                        else:
                            dve.tensor_scalar(r, r, nlam, None, ALU.mult).then_inc(dves, 1)
                            dve.wait_ge(dves, n.at("dve", 2 * a + 2))
                            dve.scalar_tensor_tensor(o_sb[:, row % 2, 0:width], e, r, ex[:, (a - 1) % 3, 0:width],
                                                     ALU.mult, ALU.add).then_inc(probs, 1)
                reciprocal_mean(2, 2, 1.0 / P, EPS)
                scaled(tile(hid, i + HEADS), bank[7][:, :], dn_gain).then_inc(free[7], 1)
                dve.wait_ge(free[7], n.at("free7", 1))
                dve.tensor_copy(lanes[:, 40:41], lanes[:, 8:9]).then_inc(cats, 1)
            out_x()
            norm(G_MEMQ)

            with n.turns(dve, HEADS, MEM1):
                reciprocal_mean(0, 0, 1.0, M * EPS)
                for c in range(2):
                    dve.wait_ge(sqs, n.at("sqs", 1))
                    scaled(qs[:, c, :], bank[c][:, :], params[:, C_MQ + c:C_MQ + c + 1]).then_inc(free[c], 1)
                dve.tensor_copy(lanes[:, 41:42], lanes[:, 8:9]).then_inc(qks, 2)
                reciprocal_mean(1, 1, 1.0 / M, EPS, M)
                for c in range(2):
                    scaled(ks[:, c, 0:M], bank[c][:, 0:M], params[:, C_MK + c:C_MK + c + 1], M).then_inc(free[c], 1)
                dve.tensor_copy(lanes[:, 41:42], lanes[:, 8:9]).then_inc(qks, 2)
                for s in range(TT + 1):
                    if s < TT:
                        masked_scores(s, M, no_mask)
                    if s >= 1:
                        normalise(s - 1, M)
            out_x()
            norm(G_FFN2)
            ffn_up()
            ffn_down()
            reciprocal_mean(0, 0, 1.0 / D, EPS)
            for k in range(KD):
                scaled(x[:, k, :], x[:, k, :], params[:, G_OUT + k:G_OUT + k + 1]).then_inc(xs, 1)
            n.past(RESCALE)
            norm(G_PRE2)
            n.past(SQUARES)

            dve.wait_ge(acts, 1)
            g4 = bank[2][:, 0:TT * 56].rearrange("p (t c) -> p t c", t=TT)
            dve.tensor_tensor(ifp[:, :, :], g4[:, :, 48:56],
                              params[:, C_GATEB:C_GATEB + 8].unsqueeze(1).to_broadcast([P, TT, 8]),
                              ALU.add).then_inc(free[2], 1)
            dve.wait_ge(free[2], n.at("free2", 1))
            dve.tensor_scalar(lf[:, 0, :, :], ifp[:, :, 4:8], 0.0, None, ALU.min).then_inc(dves, 1)
            dve.wait_ge(dves, n.at("dve", 1))
            dve.wait_ge(acts, 4)
            dve.tensor_tensor(lf[:, 1, :, :], lf[:, 0, :, :], lf[:, 3, :, :], ALU.subtract).then_inc(dves, 1)
            dve.tensor_tensor(lf[:, 2, :, :], lf[:, 3, :, :], lf[:, 0, :, :], ALU.subtract).then_inc(dves, 1)
            dve.wait_ge(turned, n.at("turned", 1))
            dve.tensor_copy(rows[0:4, 0, :], bank[6][0:4, :]).then_inc(free[6], 1)
            dve.wait_ge(free[6], n.at("free6", 1))
            dve.tensor_tensor_scan(rows[0:4, 1, :], rows[0:4, 0, :], rows[0:4, 0, :], 0.0, ALU.max,
                                   ALU.max).then_inc(dves, 1)
            dve.wait_ge(dves, n.at("dve", 4))
            dve.wait_ge(stats, n.at("stats", 1))
            dve.tensor_tensor(rows[0:4, 2, :], bank[3][0:4, :], rows[0:4, 1, :], ALU.add).then_inc(free[3], 1)
            dve.wait_ge(stats, n.at("stats", 2))
            dve.tensor_copy(acol[:, :, :], bank[3][:, 0:16].rearrange("p (t h) -> p h t", t=TT)).then_inc(free[3], 1)
            n.past(GATES)
            n.past(NSA_PRE)

            dve.wait_ge(zeros_set, 1)
            with n.turns(dve, GROUPS, NSA):
                dve.wait_ge(turned, n.at("turned", 2))
                for a in range(4):
                    rows_a = slice(32 * a, 32 * a + 32)
                    last = dve.tensor_copy(vb[rows_a, a // 2, 64 * (a % 2):64 * (a % 2) + 64], bank[6][rows_a, 0:64])
                last.then_inc(free[6], 1)
                dve.wait_ge(heads, n.at("heads", 1))
                for s in range(TT + 1):
                    if s < TT:
                        c4 = sc[:, s % 2, 0:P].rearrange("p (a b) -> p a b", a=4)[:, :, 0:CMP_N]
                        add = tables[:, K_CADD + s * CMP_N:K_CADD + (s + 1) * CMP_N]
                        for odd in range(2):
                            dve.wait_ge(scores, n.at("scores", 2 * s + odd + 1))
                            dve.tensor_tensor(c4[:, odd::2, :],
                                              bank[4 + odd][:, 0:64].rearrange("p (a b) -> p a b", a=2)[:, :, 0:CMP_N],
                                              add.unsqueeze(1).to_broadcast([P, 2, CMP_N]),
                                              ALU.add).then_inc(free[4 + odd], 1)
                        dve.wait_ge(free[5], n.at("free5", s + 1))
                        dve.tensor_reduce(cmx, c4, AX.X, ALU.max).then_inc(dves, 1)
                        dve.wait_ge(dves, n.at("dve", 5 * s + 1))
                        dve.tensor_tensor(c4, c4, cmx.unsqueeze(2).to_broadcast([P, 4, CMP_N]),
                                          ALU.subtract).then_inc(cmps, 1)
                        e4 = ex[:, s % 2, 0:P].rearrange("p (a b) -> p a b", a=4)[:, :, 0:CMP_N]
                        mul = tables[:, K_CMUL + s * CMP_N:K_CMUL + (s + 1) * CMP_N]
                        dve.wait_ge(exps, n.at("exps", s + 1))
                        dve.tensor_reduce(csum, e4, AX.X, ALU.add).then_inc(dves, 1)
                        dve.wait_ge(dves, n.at("dve", 5 * s + 2))
                        dve.reciprocal(cgate, csum).then_inc(dves, 1)
                        dve.wait_ge(dves, n.at("dve", 5 * s + 3))
                        dve.tensor_tensor(cgate, cgate, ggate[:, s, 0::3], ALU.mult).then_inc(dves, 1)
                        dve.tensor_tensor(e4, e4, mul.unsqueeze(1).to_broadcast([P, 4, CMP_N]),
                                          ALU.mult).then_inc(dves, 1)
                        dve.wait_ge(dves, n.at("dve", 5 * s + 5))
                        if s >= 1:
                            dve.wait_ge(turned, n.at("turned", 2 + s))
                        dve.tensor_tensor(pc[:, :, 0:CMP_N], e4, cgate.unsqueeze(2).to_broadcast([P, 4, CMP_N]),
                                          ALU.mult).then_inc(probs, 1)
                for s in range(NJ + 1):
                    if s < NJ:
                        width = (s % 4 + 1) * P
                        masked_scores(s, width, tables[:, K_CAUS + T - width:K_CAUS + T], 4, 8)
                    if s >= 1:
                        a = s - 1
                        head, br, row = a // 8, a // 4 % 2, a % 4
                        normalise(a, (row + 1) * P, ggate[:, row, head * 3 + 1 + br:head * 3 + 2 + br], 20, 4)
            norm_memory(G_MEM2)
            n.past(SPREAD)

            with n.turns(dve, HEADS, ML) as i:
                dve.wait_ge(heads, n.at("heads", 1))
                for c in range(2):
                    dve.wait_ge(free[c], n.at(f"free{c}", 1))
                    y = o_sb[:, c, :]
                    for tap in range(4):
                        w = hp[:, 4 * c + tap:4 * c + tap + 1]
                        if tap == 0:
                            dve.tensor_scalar(y, xp[:, c, 0:T], w, None, ALU.mult).then_inc(dves, 1)
                        else:
                            dve.wait_ge(dves, n.at("dve", 4 * c + tap))
                            dve.scalar_tensor_tensor(y, xp[:, c, tap:tap + T], w, y, ALU.mult, ALU.add).then_inc(dves, 1)
                for j in range(TT):
                    w = T - j * P
                    dve.scalar_tensor_tensor(hid[:, 18 + j, 0:w], negM[:, bass.ds(i, 1), j * P:T].rearrange("p a t -> p (a t)"),
                                             hp[:, 12 + j:13 + j], tables[:, K_CAUST:K_CAUST + w],
                                             ALU.add, ALU.add).then_inc(dves, 1)
                for j in range(TT):
                    b, w = 4 + j % 2, T - j * P
                    dve.wait_ge(exps, n.at("exps", j + 1))
                    dve.wait_ge(scores, n.at("scores", j + 1))
                    dve.scalar_tensor_tensor(PT[:, j, j * P:T], bank[b][:, 0:w], P ** -0.5, hid[:, 18 + j, 0:w],
                                             ALU.mult, ALU.mult).then_inc(free[b], 1)
                dve.wait_ge(free[6], n.at("free6", 1))
                dve.tensor_tensor(var[:, :], var[:, :], tile(emb, i), ALU.max).then_inc(dves, 1)
                dve.wait_ge(dves, n.at("dve", 13))
                dve.reciprocal(rc[:, :], var[:, :]).then_inc(dves, 1)
                dve.wait_ge(dves, n.at("dve", 14))
                dve.wait_ge(outs, n.at("outs", 1))
                dve.tensor_tensor(o_sb[:, 0, :], bank[7][:, :], rc[:, :], ALU.mult).then_inc(free[7], 1)
                reciprocal_mean(0, 0, 1.0 / P, EPS)
                scaled(o_sb[:, 1, :], o_sb[:, 0, :], hp[:, 10:11]).then_inc(dves, 1)
                dve.wait_ge(dves, n.at("dve", 15))
                dve.wait_ge(free[0], n.at("free0", 2))
                dve.tensor_tensor(tile(hid, i + 8), o_sb[:, 1, :], silu[:, 0, :], ALU.mult).then_inc(cats, 1)

            with n.turns(dve, HEADS, MEM2):
                for s in range(TT + 1):
                    if s < TT:
                        masked_scores(s, M, no_mask)
                    if s >= 1:
                        normalise(s - 1, M)

            with n.turns(dve, KD, MERGE) as i:
                for j in range(3):
                    dve.wait_ge(free[0], n.at("free0", j + 1))
                    dve.wait_ge(products, n.at("products", 2 * j + 2))
                    dve.tensor_tensor(ex[:, j, :], silu[:, j, :], bank[1][:, :], ALU.mult).then_inc(free[1], 1)
                    if j == 1:
                        dve.wait_ge(free[1], n.at("free1", 2))
                        dve.tensor_tensor(sc[:, 0, :], ex[:, 0, :], ex[:, 1, :], ALU.add).then_inc(dves, 1)
                dve.wait_ge(free[1], n.at("free1", 3))
                dve.wait_ge(dves, n.at("dve", 1))
                dve.tensor_tensor(tile(big8, i), sc[:, 0, :], ex[:, 2, :], ALU.add).then_inc(dves, 1)

            def add_z(z, g, events):
                reciprocal_mean(0, 0, 1.0 / D, EPS)
                for k in range(KD + 1):
                    if k < KD:
                        scaled(z[:, k, :], z[:, k, :], params[:, g + k:g + k + 1]).then_inc(dves, 1)
                    if k >= 1:
                        dve.wait_ge(dves, n.at("dve", k))
                        dve.tensor_tensor(x[:, k - 1, :], x[:, k - 1, :], z[:, k - 1, :], ALU.add).then_inc(xs, 1)
                n.past(events)

            n.past(CLEAR)
            n.past(OUT_Z, 2)
            add_z(hid, G_POST2, ADD_Z)
            norm(G_PREF2)
            ffn_up()
            n.past(CLEAR)
            n.past(FFN_DOWN_Z, 4)
            add_z(big8, G_POSTF2, ADD_Z_LAST)


TOTAL = {"xs": 1 + 2 * 8 + 2 * 8 + 8 + 8 + 8}


def _panels(np_, w, cols, k0=0, k1=None):
    w = w[k0:k1]
    a = w.reshape(w.shape[0] // P, P, w.shape[1])
    return [np_.ascontiguousarray(a[:, :, c].transpose(1, 0, 2)) for c in cols]


def _tables():
    r = np.arange(P)
    con = np.zeros((P, K_BASE), np.float32)
    con[:, K_ID:K_ID + P] = np.eye(P)
    con[:, K_ONE:K_ONE + P] = 1
    con[:, K_BLK:K_BLK + P] = (r[:, None] // 64 == r[None, :] // 64)
    tab = np.zeros((P, NTAB), np.float32)
    tab[:, K_CAUS + T - P:K_CAUS + T] = np.where(r[None, :] <= r[:, None], 0, NEG)
    tab[:, K_CAUST:K_CAUST + P] = np.where(r[None, :] >= r[:, None], 0, NEG)
    c = np.arange(T)
    tab[:, K_CUM:K_CUM + T] = c[None, :] >= r[:, None]
    for t in range(TT):
        ok = (np.arange(CMP_N)[None, :] * CMP_S + CMP_L - 1) <= (t * P + r)[:, None]
        tab[:, K_CADD + t * CMP_N:K_CADD + (t + 1) * CMP_N] = np.where(ok, 0, NEG)
        tab[:, K_CMUL + t * CMP_N:K_CMUL + (t + 1) * CMP_N] = ok
    headtab = np.zeros((2 * HEADS, P, T), np.float32)
    for hd in range(HEADS):
        tab[hd, K_SEL + hd * P:K_SEL + (hd + 1) * P] = 1
        gamma = np.log1p(-2.0 ** (-5.0 - hd))
        rel = c[None, :] - r[:, None]
        headtab[hd] = np.where(rel >= 0, np.exp(gamma * np.maximum(rel, 0)), 0) * P ** -0.5
        slope = 2.0 ** (-8.0 * (hd + 1) / HEADS)
        dist = r[:, None] - (c[None, :] - (T - P))
        headtab[HEADS + hd] = np.where(dist >= 0, -slope * dist, NEG)
    return con, tab, headtab


def kernel(**inputs):
    import numpy as _np
    import concourse.bacc as _bacc
    from concourse import mybir as _mybir
    from concourse.bass_utils import run_bass_kernel_spmd as _run

    I = {k: _np.asarray(v) for k, v in inputs.items()}

    def W(name):
        return I[name][0]

    def cols(start, width=P):
        return slice(start, start + width)

    def two(a, b, width=64):
        return _np.r_[a:a + width, b:b + width]

    w8, w11, w4 = [], [], []

    def ffn(w1, w3, w2, off3=0):
        for f in range(KF):
            w8.extend(_panels(_np, w1, [cols(f * P)]))
            w8.extend(_panels(_np, w3, [cols(off3 + f * P)]))
        for m in range(KD):
            for half in range(2):
                w11.extend(_panels(_np, w2, [cols(m * P)], half * KH * P, (half + 1) * KH * P))

    ffn(W("ffn1_w1"), W("ffn1_w3"), W("ffn1_w2"))
    win = W("w_in")
    for hd in range(HEADS):
        w8.extend(_panels(_np, win, [cols(b * 512 + hd * P) for b in range(4)]))
    for hd in range(HEADS):
        w8.extend(_panels(_np, win, [cols(2048 + b * 512 + hd * P) for b in range(3)]))
    w8.extend(_panels(_np, W("w_out"), [cols(m * P) for m in range(KD)]))
    for hd in range(HEADS):
        w8.extend(_panels(_np, W("mem_w_q"), [cols(hd * M + c * P) for c in range(2)]))
        w8.extend(_panels(_np, W("mem_w_kv"), [cols(b * D + hd * M + c * P) for b in range(2) for c in range(2)]))
    w8.extend(_panels(_np, W("mem_w_o"), [cols(m * P) for m in range(KD)]))
    ffn(W("ffn2_w1"), W("ffn2_w3"), W("ffn2_w2"))
    win = W("w_in_2")
    kv0 = 1024
    for g in range(GROUPS):
        def kv(b):
            return kv0 + b * 256 + g * 64
        w8.extend(_panels(_np, win, [cols(g * 256), cols(g * 256 + P), two(kv(0), kv(1)), two(kv(2), kv(4)),
                                     two(kv(3), kv(5))]))
    ml0 = 1024 + 1536 + 48
    if0 = ml0 + 1536
    o0 = if0 + 8
    mq0 = o0 + 512
    gm0 = mq0 + 512
    for hd in range(HEADS):
        w8.extend(_panels(_np, win, [cols(ml0 + hd * P), cols(ml0 + 512 + hd * P), cols(o0 + hd * P),
                                     cols(ml0 + 1024 + hd * P)]))
    mkv = W("w_mem_kv_2")
    for hd in range(HEADS):
        w8.extend(_panels(_np, win, [cols(mq0 + hd * P)]))
        w8.extend(_panels(_np, mkv, [cols(hd * P), cols(512 + hd * P)]))
    for m in range(KD):
        w8.extend(_panels(_np, win, [cols(gm0 + m * P)]))
        w8.extend(_panels(_np, W("w_proj_nsa_2"), [cols(m * P)]))
        w8.extend(_panels(_np, win, [cols(gm0 + D + m * P)]))
        w4.extend(_panels(_np, W("w_proj_ml_2"), [cols(m * P)]))
        w8.extend(_panels(_np, win, [cols(gm0 + 2 * D + m * P)]))
        w4.extend(_panels(_np, W("w_proj_mem_2"), [cols(m * P)]))
    w8.extend(_panels(_np, W("w_out_2"), [cols(m * P) for m in range(KD)]))
    ffn(W("w_ffn_in_2"), W("w_ffn_in_2"), W("w_ffn_down_2"), FF)

    gatew = _np.concatenate([win[:, 2560:2608], win[:, if0:if0 + 8]], 1).reshape(KD, P, 56).transpose(1, 0, 2)
    cw1 = _np.concatenate([W("cmp_w1_k_2").transpose(1, 0, 2), W("cmp_w1_v_2").transpose(1, 0, 2)], 0)
    cw2 = _np.concatenate([W("cmp_w2_k_2"), W("cmp_w2_k_2"), W("cmp_w2_v_2")], 1)

    par = [W(k).reshape(KD, P).T for k in ("norm_ffn1", "norm_mix", "norm_mem_q", "norm_mem_kv", "norm_ffn2",
                                           "norm_out", "g_pre_mix_2", "g_mem_2", "g_post_mix_2", "g_pre_ffn_2",
                                           "g_post_ffn_2")]
    twice = lambda v: _np.concatenate([v, v])[:, None]
    par += [W("ret_norm")[:, None], twice(W("diff_q_norm")), twice(W("diff_k_norm")), W("diff_norm")[:, None],
            W("mem_q_norm").reshape(2, P).T, W("mem_k_norm").reshape(2, P).T,
            twice(W("lambda_q1")), twice(W("lambda_q2")), twice(W("lambda_k1")), twice(W("lambda_k2"))]
    cw, cb, hg = W("ml_conv_w_2"), W("ml_conv_b_2"), W("ml_head_g_2")
    for hd in range(HEADS):
        a, b = hd * P, 512 + hd * P
        par += [cw[:, a:a + P].T, cw[:, b:b + P].T, cb[a:a + P, None], cb[b:b + P, None], hg[a:a + P, None]]
    par += [_np.repeat(W("ml_gate_b_2")[None, :], P, 0),
            _np.concatenate([W("cmp_pe_k_2").T, W("cmp_pe_v_2").T], 0)]
    con, tab, headtab = _tables()

    arrays = {
        "xT": I["x"][0].T.reshape(KD, P, T).transpose(1, 0, 2),
        "memT": I["mem"][0].T.reshape(KD, P, M).transpose(1, 0, 2),
        "mem2T": I["mem_2"][0].T.reshape(KD, P, M).transpose(1, 0, 2),
        "par": _np.concatenate(par, 1), "con": con, "tab": tab, "headtab": headtab,
        "w8": _np.stack(w8), "w11": _np.stack(w11), "w4": _np.stack(w4),
        "gatew": gatew, "cmpw1": cw1, "cmpw2": cw2,
    }
    arrays = {k: _np.ascontiguousarray(v) for k, v in arrays.items()}
    nc = _bacc.Bacc("TRN2", target_bir_lowering=False, num_devices=1)
    args = [nc.dram_tensor(k, a.shape, _mybir.dt.from_np(a.dtype), kind="ExternalInput").ap() for k, a in arrays.items()]
    args.append(nc.dram_tensor("outT", (KD, P, T), _mybir.dt.float32, kind="ExternalOutput").ap())
    build(nc, *args)
    r = _run(nc, [arrays], core_ids=[0])
    return _np.ascontiguousarray(r.results[0]["outT"].reshape(D, T).T)[None]
```

```python
from contextlib import ExitStack, contextmanager

import numpy as np

import concourse.bass as bass
from concourse import mybir

F32 = mybir.dt.float32
F32R = mybir.dt.float32r
ACT = mybir.ActivationFunctionType
ALU = mybir.AluOpType
AX = mybir.AxisListType

P = 128
D = 1024
T = 512
M = 256
KD = D // P
TT = T // P
MT = M // P
FF = 2816
KF = FF // P
EPS = 1e-6
NEG = -1e30
HEADS = 4
CMP_L, CMP_S, CMP_N = 32, 16, 31
GROUPS = 4
LAM_INIT = 0.2
SLOTS = 6
RING = 4
DOWN = (8, 8, 6)

G_FFN1, G_MIX, G_MEMQ, G_MEMKV, G_FFN2, G_OUT, G_PRE2, G_MEM2, G_POST2, G_PREF2, G_POSTF2 = range(0, 88, 8)
C_RET, C_DQ, C_DK, C_DN = 88, 89, 90, 91
C_MQ, C_MK = 92, 94
C_LAM = 96
C_HEAD = 100
C_HEADN = 11
C_GATEB = C_HEAD + HEADS * C_HEADN
C_PE = C_GATEB + 8
NPAR = C_PE + CMP_L

K_ID, K_ONE, K_BLK = 0, 128, 256
K_BASE = 384
K_CAUS = 0
K_CAUST = 512
K_CUM = 1024
K_CADD = 1536
K_CMUL = K_CADD + TT * CMP_N
NTAB = K_CMUL + TT * CMP_N

NORM = dict(stats=1, free3=1, rcp=1, rinv=1, h32s=KD, hhis=KD, hlos=KD)
SQUARES = dict(squares=KD, sums=KD, cleared=1)
CLEAR = dict(cleared=1)
RESCALE = dict(stats=1, free3=1, rcp=1, rinv=1, xs=KD, squares=KD, sums=KD, cleared=1)
FFN_UP = dict(products=4, splits=4, highs=4, free0=2, free1=2)
FFN_DOWN = dict(products=12, xs=4, squares=4, sums=4)
FFN_DOWN_Z = dict(products=12, free0=2, free1=2, squares=4, sums=4)
OUT_X = dict(products=4, xs=4, squares=4, sums=4)
OUT_Z = dict(products=4, free0=2, free1=2, squares=4, sums=4)
ADD_Z = dict(stats=1, free3=1, rcp=1, rinv=1, dve=KD, xs=KD, squares=KD, sums=KD, cleared=1)
ADD_Z_LAST = dict(stats=1, free3=1, rcp=1, rinv=1, dve=KD, xs=KD)
MEM_NORM = dict(stats=1, free3=1, rcp=1, rinv=1, mems=1)
RET = dict(products=4, splits=4, highs=4, free0=2, free1=1, free2=1, strips=1, scores=4, free4=2, free5=2, outs=1, free7=1,
           stats=2, free3=2, sqs=1, rcp=1, rinv=1, dve=1, cats=1)
LAM = dict(stats=1, free3=1, dve=3)
DIFF = dict(products=3, splits=3, highs=3, free0=1, free1=1, free2=1, strips=1, stats=3, free3=3, sqs=3, rcp=3, rinv=3,
            scores=8, free4=4, free5=4, negmax=8, exps=8, dve=16, probs=4, turned=4, free6=4,
            outs=1, free7=1, cats=1)
MEM1 = dict(products=6, splits=2, highs=2, free0=2, free1=2, free2=1, stats=2, free3=2, sqs=2, rcp=2, rinv=2,
            scores=4, free4=2, free5=2, negmax=4, exps=4, dve=4, probs=4, turned=4, free6=4,
            outs=2, free7=2)
NJ = 32
CMP = dict(products=4, splits=4, highs=4, free0=2, free1=2, dve=2, acts=2, stats=2, free3=2, turned=2, free6=2)
NSA = dict(products=4, splits=4, highs=4, free0=1, free1=1, free2=1, free3=1, heads=1, twins=1,
           scores=8 + NJ, free4=4 + NJ // 2, free5=4 + NJ // 2, cmps=4, negmax=NJ, exps=4 + NJ,
           dve=20 + NJ, probs=4 + NJ, turned=4 + NJ, free6=4 + NJ, outs=2, free7=2)
GATES = dict(gates=1, acts=5, free2=1, dve=4, stats=2, free3=2, turned=1, free6=1)
SPREAD = dict(scores=8, free4=4, free5=4)
ML = dict(products=4, splits=4, highs=4, free0=2, free1=1, free2=1, heads=1, dve=15, convs=2, exps=4, scores=4, free4=2,
          free5=2, outs=1, turned=1, free6=1, free7=1, sqs=1, stats=1, free3=1, rcp=1, rinv=1, cats=1)
MEM2 = dict(products=3, splits=1, highs=1, free0=1, free1=1, free2=1, scores=4, free4=2, free5=2, negmax=4, exps=4,
            dve=4, probs=4, turned=4, free6=4, outs=1, free7=1)
MERGE = dict(products=6, splits=3, highs=3, free0=3, free1=3, dve=2)

STREAM = [
    (KF // 2, FFN_UP, [8] * 4), (2, FFN_DOWN, [*DOWN] * 4),
    (HEADS, RET, [8] * 4), (HEADS, DIFF, [8] * 3), (2, OUT_X, [8] * 4),
    (HEADS, MEM1, [8] * 6), (2, OUT_X, [8] * 4),
    (KF // 2, FFN_UP, [8] * 4), (2, FFN_DOWN, [*DOWN] * 4),
    (1, CMP, [8] * 4), (GROUPS, NSA, [8] * 4), (HEADS, ML, [8] * 4), (HEADS, MEM2, [8] * 3),
    (KD, MERGE, [8, 8, 8, 4, 8, 4]), (2, OUT_Z, [8] * 4),
    (KF // 2, FFN_UP, [8] * 4), (2, FFN_DOWN_Z, [*DOWN] * 4),
]


def slots_used(panels):
    return panels if panels <= SLOTS else RING


def slot_loads(events):
    panels = events.get("products", 0)
    return [(s, panels // slots_used(panels)) for s in range(slots_used(panels))] if panels else []


class Counts:

    def __init__(self):
        self.base = {**{f"free{b}": 1 for b in range(8)}, "cats": 1, "xs": 1}
        self.turn, self.events = None, {}

    def at(self, name, more=0):
        value = self.base.get(name, 0) + more
        if self.turn is not None and self.events.get(name, 0):
            value = self.turn * self.events[name] + value
        return value

    def past(self, events, turns=1):
        for name, k in events.items():
            self.base[name] = self.base.get(name, 0) + k * turns
        for slot, k in slot_loads(events):
            self.base[f"loads{slot}"] = self.base.get(f"loads{slot}", 0) + k * turns

    @contextmanager
    def turns(self, engine, turns, events):
        with engine.Fori(0, turns) as i:
            self.turn = i
            self.events = {**events, **{f"loads{s}": k for s, k in slot_loads(events)}}
            yield i
        self.turn, self.events = None, {}
        self.past(events, turns)


def build(nc, xT, memT, mem2T, par, con, tab, headtab, w8, w6, w4, gatew, cmpw1, cmpw2, outT):
    with ExitStack() as ctx:
        def sb(name, *shape):
            return ctx.enter_context(nc.sbuf_tensor(name, [P, *shape], F32))

        def sbr(name, *shape):
            return ctx.enter_context(nc.sbuf_tensor(name, [P, *shape], F32R))

        def sem(name):
            return ctx.enter_context(nc.semaphore(name))

        bank = [ctx.enter_context(nc.psum_tensor(f"bank{b}", [P, 512], F32)) for b in range(8)]

        x = sb("x", KD, T)
        hhi, hlo = sbr("hhi", KD, T), sbr("hlo", KD, T)
        hid = sb("hid", KF, T)
        big = sb("big", KD * T)
        memh = sb("memh", KD, M)
        slot = [sb(f"slot{s}", KD, P) for s in range(RING)]
        slot += [hid[:, t:t + 2, :].rearrange("p a (b c) -> p (a b) c", c=P) for t in (16, 20)]
        parts = [sbr(f"parts{s}", 2, KD, P) for s in range(2)]
        params = sb("params", NPAR)
        consts = sb("consts", K_BASE)
        tables = sb("tables", NTAB)
        gate_w = sb("gate_w", KD, 56)
        w2 = sb("w2", P + 64)
        ssum = sb("ssum", T)
        var = sb("var", T)
        rinv = sb("rinv", T)
        silu = sb("silu", 3, T)
        qs = sb("qs", 2, T)
        ks = sb("ks", 2, T)
        vs = sb("vs", T)
        PT = sb("PT", TT, T)
        sc = sb("sc", 2, T)
        ex = sb("ex", 3, T)
        lanes = sb("lanes", 64)
        hp = sb("hp", 16)
        gates = sb("gates", TT, 48)
        ggate = sb("ggate", TT, 12)
        ifp = sb("ifp", TT, 8)
        lf = sb("lf", 4, TT, 4)
        acol = sb("acol", HEADS, TT)
        kc2 = sb("kc2", CMP_N)
        vb = sb("vb", 2, P)
        pc = sb("pc", 4, 32)
        o_sb = sb("o_sb", 2, T)

        big8 = big[:, :].rearrange("p (k t) -> p k t", k=KD)
        w1c = big[:, :].rearrange("p (l h) -> p l h", l=CMP_L)
        sq = sc
        xp = ex[:, :, :].rearrange("p a t -> p (a t)")[:, 0:2 * (T + 3)].rearrange("p (c t) -> p c t", c=2)
        h32 = hid[:, 8:16, :]
        strip = hid[:, 19, :]
        sqh = silu[:, 1:3, :]
        PTc = o_sb[:, 1, :]
        kvc = hid[:, 8:13, :]
        kc_all = hid[:, 15, 0:GROUPS * CMP_N]
        hidk = hid[:, 13, 0:GROUPS * CMP_N]
        hidv = hid[:, 14, :].rearrange("p (g a b) -> p g a b", g=GROUPS, a=4)
        vb_all = hid[:, 16:18, :].rearrange("p a (b c) -> p (a b) c", c=2 * P)
        rows = hid[:, 18:22, :]
        negM, emb = big8[:, 0:HEADS, :], big8[:, HEADS:2 * HEADS, :]
        ident, ones, blocks64 = consts[:, K_ID:K_ID + P], consts[:, K_ONE:K_ONE + P], consts[:, K_BLK:K_BLK + P]
        negmax, esum = lanes[:, 0:2], lanes[:, 4:7]
        nlam, dn_gain, rsm = lanes[:, 8:9], lanes[:, 9:10], lanes[:, 10:13]
        pebias = lanes[:, 14:16]
        le = lanes[:, 16:18]
        lprod = lanes[:, 18:20]
        maxs = lanes[:, 20:22]
        nought = lanes[:, 53:54]
        cmx, csum, cgate = lanes[:, 24:28], lanes[:, 28:32], lanes[:, 32:36]

        x_loaded = sem("x_loaded")
        params_loaded = sem("params_loaded")
        consts_loaded = sem("consts_loaded")
        tables_loaded = sem("tables_loaded")
        mem_loaded = sem("mem_loaded")
        cmp_loaded = sem("cmp_loaded")
        loaded = [sem(f"slot{s}_loaded") for s in range(SLOTS)]
        strips = sem("head_strip_loaded")
        twins = sem("key_twins_copied")
        stored = sem("stored")
        free = [sem(f"bank{b}_free") for b in range(8)]
        products = sem("panel_products")
        stats = sem("sums_over_partitions")
        scores = sem("scores_made")
        turned = sem("probs_turned")
        outs = sem("attention_out")
        gates_made = sem("gates_made")
        rcp = sem("reciprocal_mean_square")
        h32s = sem("h_tiles")
        hlos = sem("h_low_parts")
        xs = sem("x_tiles")
        negmaxs = sem("negated_maxima")
        probs = sem("probabilities")
        cmps = sem("shifted_compressed_scores")
        cats = sem("head_outputs")
        mems = sem("memory_normed")
        pads = sem("padding_zeroed")
        dves = sem("vector_steps")
        rinvs = sem("inverse_rms")
        squares = sem("squares")
        sqs = sem("head_squares")
        hhis = sem("h_high_parts")
        exps = sem("exponentials")
        convs = sem("conv_silus")
        acts = sem("scalar_steps")
        sums = sem("square_sums")
        cleared = sem("sum_cleared")
        highs = sem("panel_high_parts")
        splits = sem("panels_split")
        heads = sem("head_tables")
        zeros_set = sem("zeros_set")

        block = ctx.enter_context(nc.Block())

        @block.sync
        def _(sp):
            n = Counts()
            panel = {8: 0, 6: 0, 4: 0}
            source = {8: w8, 6: w6, 4: w4}
            before = RING
            for phase, (turns, events, ktiles) in enumerate(STREAM):
                c = slots_used(len(ktiles))
                per = {k: ktiles.count(k) for k in set(ktiles)}
                first = 0
                if phase == 0:
                    for j in range(c):
                        sp.dma_start(slot[j][:, 0:8, :], w8[j]).then_inc(loaded[j], 16)
                    n.past(events)
                    panel[8] += c
                    first = 1
                with n.turns(sp, turns - first, events) as i:
                    for j, k in enumerate(ktiles):
                        s = j % c
                        sp.wait_ge(products, n.at("products", j + 1 - min(c, before)))
                        at = panel[k] + ktiles[:j].count(k) + i * per[k]
                        src = source[k][bass.ds(at, 1)].rearrange("a p k c -> p (a k) c")
                        sp.dma_start(slot[s][:, 0:k, :], src).then_inc(loaded[s], 16)
                for k in per:
                    panel[k] += per[k] * (turns - first)
                before = c
            n.past(ADD_Z_LAST)
            done = TOTAL["xs"] - KD
            for k in range(KD):
                sp.wait_ge(xs, done + k + 1)
                sp.dma_start(outT[k], x[:, k, :]).then_inc(stored, 16)
            sp.wait_ge(stored, 16 * KD)

        @block.gpsimd
        def _(pool):
            n = Counts()
            for z in (pc[:, :, :], nought):
                last = pool.memset(z, 0.0)
            last.then_inc(zeros_set, 1)

            def clear_sum(stat):
                pool.wait_ge(stats, n.at("stats", stat))
                pool.memset(ssum[:, :], 0.0).then_inc(cleared, 1)

            def add_square(k, parity, width=T):
                pool.wait_ge(squares, n.at("squares", k + 1))
                pool.wait_ge(sums, n.at("sums", k))
                pool.tensor_tensor(ssum[:, 0:width], ssum[:, 0:width], sq[:, parity, 0:width],
                                   ALU.add).then_inc(sums, 1)

            def sum_tiles(stat, width=T):
                clear_sum(stat)
                pool.wait_ge(cleared, n.at("cleared", 1))
                for k in range(KD):
                    add_square(k, k % 2, width)

            def sum_in_turns(turns, events, per):
                with n.turns(pool, turns, events):
                    for k in range(per):
                        add_square(k, k % 2)

            def split(nth, j, product=None):
                if product != "act":
                    pool.wait_ge(loaded[j], 16 * n.at(f"loads{j}", 1))
                    pool.wait_ge(products, n.at("products", product))
                w, (high, low) = slot[j][:, 0:KD, :], (parts[nth % 2][:, c, :, :] for c in range(2))
                if product != "act":
                    pool.tensor_tensor(high, w, nought.unsqueeze(2).to_broadcast([P, KD, P]), ALU.add).then_inc(highs, 1)
                pool.wait_ge(highs, n.at("highs", nth + 1))
                pool.tensor_tensor(low, w, high.bitcast(F32), ALU.subtract).then_inc(splits, 1)

            def split_turns(turns, events, panels, last=None, between=None):
                with n.turns(pool, turns, events) as i:
                    for nth, j in enumerate(panels):
                        split(nth, j, "act" if last is None else last[nth] if nth < 2 else panels[nth - 2] + 1)
                        if nth == 1 and between is not None:
                            between(i)

            def cleared_before_turns():
                clear_sum(0)
                n.past(CLEAR)
                pool.wait_ge(cleared, n.at("cleared"))

            def ffn(down, memory=False):
                if memory:
                    for j in range(4):
                        if j == 2:
                            sum_tiles(0, M)
                            n.past(SQUARES)
                        split(j, j, "act")
                    n.past(FFN_UP)
                split_turns(KF // 2 - memory, FFN_UP, range(4))
                if memory:
                    n.past(MEM_NORM)
                cleared_before_turns()
                sum_in_turns(2, down, 4)

            sum_tiles(0)
            n.past(SQUARES)
            n.past(NORM)
            ffn(FFN_DOWN, True)
            n.past(NORM)
            split_turns(HEADS, RET, range(4), (-1, 0))
            n.past(LAM)
            split_turns(HEADS, DIFF, range(3), (0, 0))
            cleared_before_turns()
            sum_in_turns(2, OUT_X, 4)
            n.past(NORM)
            split_turns(HEADS, MEM1, (4, 5), (-1, 0))
            cleared_before_turns()
            sum_in_turns(2, OUT_X, 4)
            n.past(NORM)
            ffn(FFN_DOWN, True)
            sum_tiles(1)
            n.past(RESCALE)
            n.past(NORM)
            n.past(GATES)
            for j in range(4):
                split(j, j, j - 1 if j >= 2 else 0)
            n.past(CMP)
            pool.wait_ge(free[3], n.at("free3"))
            pool.wait_ge(free[6], n.at("free6"))

            def group_gates(i):
                pool.wait_ge(outs, n.at("outs"))
                pool.wait_ge(probs, n.at("probs"))
                pool.wait_ge(acts, n.at("acts"))
                pool.tensor_copy(kc2[:, :], kc_all.rearrange("p (g b) -> p g b", g=GROUPS)[:, bass.ds(i, 1), :].rearrange("p a b -> p (a b)"))
                pool.tensor_copy(vb[:, :, :].rearrange("p a b -> p (a b)"),
                                 vb_all[:, bass.ds(i, 1), :].rearrange("p a b -> p (a b)"))
                pool.tensor_copy(ggate[:, :, :], gates[:, :, bass.ds(i * 12, 12)]).then_inc(heads, 1)

            split_turns(GROUPS, NSA, range(4), (-1, 0), group_gates)
            n.past(SPREAD)

            def head_params(i):
                pool.wait_ge(cats, n.at("cats"))
                pool.tensor_copy(hp[:, 12:16], acol[:, bass.ds(i, 1), :].rearrange("p a t -> p (a t)"))
                pool.tensor_copy(hp[:, 0:C_HEADN],
                                 params[:, bass.ds(C_HEAD + i * C_HEADN, C_HEADN)]).then_inc(heads, 1)

            split_turns(HEADS, ML, range(4), (0, 0), head_params)
            with n.turns(pool, HEADS, MEM2):
                split(0, 0, -1)
            split_turns(KD, MERGE, (0, 2, 4))
            cleared_before_turns()
            sum_in_turns(2, OUT_Z, 4)
            sum_tiles(1)
            n.past(ADD_Z)
            n.past(NORM)
            ffn(FFN_DOWN_Z)

        @block.tensor
        def _(pe):
            n = Counts()

            def panel(j, out, moving, stationary_tokens=False, k0=0, ks_=KD, start=True, stop=True, load=1):
                pe.wait_ge(loaded[j], 16 * n.at(f"loads{j}", load))
                if stationary_tokens:
                    for t in range(moving.shape[2] // P):
                        for k in range(ks_):
                            mm = pe.matmul(out(t), moving[:, k, t * P:(t + 1) * P], slot[j][:, k, :],
                                           start=(k == 0), stop=(k == ks_ - 1))
                else:
                    for k in range(ks_):
                        mm = pe.matmul(out, slot[j][:, k, :], moving[:, k0 + k, :],
                                       start=(start and k == 0), stop=(stop and k == ks_ - 1))
                mm.then_inc(products, 1)

            def h_panel(nth, out, stationary_tokens=False, ready=None):
                high, low = (parts[nth % 2][:, c, :, :] for c in range(2))
                pe.wait_ge(splits, n.at("splits", nth + 1))
                if stationary_tokens:
                    for t in range(TT):
                        tokens = slice(t * P, (t + 1) * P)
                        for k in range(KD):
                            pe.matmul(out(t), hhi[:, k, tokens], high[:, k, :], start=(k == 0), stop=False)
                            pe.matmul(out(t), hhi[:, k, tokens], low[:, k, :], start=False, stop=False)
                            mm = pe.matmul(out(t), hlo[:, k, tokens], high[:, k, :], start=False, stop=(k == KD - 1))
                else:
                    for k in range(KD):
                        if ready is not None:
                            pe.wait_ge(hhis, ready - KD + k + 1)
                        pe.matmul(out, high[:, k, :], hhi[:, k, :], start=(k == 0), stop=False)
                        pe.matmul(out, low[:, k, :], hhi[:, k, :], start=False, stop=False)
                    for k in range(KD):
                        if ready is not None:
                            pe.wait_ge(hlos, ready - KD + k + 1)
                        mm = pe.matmul(out, high[:, k, :], hlo[:, k, :], start=False, stop=(k == KD - 1))
                mm.then_inc(products, 1)

            def emptied(b, more=0):
                pe.wait_ge(free[b], n.at(f"free{b}", more))

            def stat(k, matrix, *sources):
                emptied(3, k)
                width = sources[0].shape[1]
                for a, s in enumerate(sources):
                    mm = pe.matmul(bank[3][:, 0:width], matrix, s, start=(a == 0),
                                   stop=(a == len(sources) - 1))
                mm.then_inc(stats, 1)

            def norm(width=T):
                pe.wait_ge(sums, n.at("sums"))
                stat(0, ones, ssum[:, 0:width])

            def ffn(down, memory=False):
                h_done = n.at("hlos")
                if memory:
                    n.past(SQUARES)
                with n.turns(pe, KF // 2, FFN_UP):
                    for u in range(2):
                        emptied(0, u)
                        h_panel(2 * u, bank[0][:, :], ready=h_done if u == 0 else None)
                        emptied(1, u)
                        h_panel(2 * u + 1, bank[1][:, :])
                hidden_done = n.at("free1")
                if memory:
                    norm(M)
                    n.past(MEM_NORM)
                out_product(down, hid, free[1], hidden_done, DOWN)

            def out_product(events, moving, ready_sem, ready, ktiles=(KD,)):
                c = len(ktiles)
                with n.turns(pe, 2, events):
                    for j in range(4):
                        if "xs" in events:
                            pe.wait_ge(xs, n.at("xs", j - 1))
                        else:
                            emptied(j % 2, j // 2)
                        pe.wait_ge(ready_sem, ready)
                        for a, k in enumerate(ktiles):
                            at = j * c + a
                            panel(at % RING, bank[j % 2][:, :], moving, k0=sum(ktiles[:a]), ks_=k,
                                  start=(a == 0), stop=(a == c - 1), load=at // RING + 1)

            def scores_of(k, lhs, rhs, width):
                b = 4 + k % 2
                emptied(b, k // 2)
                for a in range(len(lhs)):
                    mm = pe.matmul(bank[b][:, 0:width], lhs[a], rhs[a], start=(a == 0), stop=(a == len(lhs) - 1))
                mm.then_inc(scores, 1)

            def turn_probs(k, tile, source, p):
                pe.wait_ge(probs, n.at("probs", p))
                emptied(6, k)
                for b in range(tile):
                    mm = pe.transpose(bank[6][:, b * P:(b + 1) * P], source[:, b * P:(b + 1) * P], ident)
                mm.then_inc(turned, 1)

            def causal_out(out, values, start=True):
                for j in range(TT):
                    mm = pe.matmul(out[:, j * P:T], values(j), PT[:, j, j * P:T], start=(start and j == 0),
                                   stop=(start and j == TT - 1), skip_group_check=not start)
                return mm

            pe.wait_ge(consts_loaded, 16)
            n.past(SQUARES)
            norm()
            n.past(NORM)
            ffn(FFN_DOWN, True)
            norm()
            n.past(NORM)

            h_done = n.at("hlos")
            with n.turns(pe, HEADS, RET):
                emptied(0)
                h_panel(0, bank[0][:, :], ready=h_done)
                emptied(1)
                h_panel(1, bank[1][:, :])
                emptied(2)
                h_panel(2, lambda t: bank[2][:, t * P:(t + 1) * P], True)
                emptied(0, 1)
                h_panel(3, bank[0][:, :])
                emptied(1, 1)
                emptied(2, 1)
                emptied(7)
                for j in range(TT + 1):
                    if j < TT:
                        scores_of(j, [ks[:, 0, j * P:(j + 1) * P]], [qs[:, 0, j * P:T]], T - j * P)
                    if j >= 1:
                        emptied(4 + (j - 1) % 2, (j - 1) // 2 + 1)
                        mm = pe.matmul(bank[7][:, (j - 1) * P:T], vs[:, (j - 1) * P:j * P],
                                       PT[:, j - 1, (j - 1) * P:T], start=(j == 1), stop=(j == TT))
                mm.then_inc(outs, 1)
                emptied(7, 1)
                stat(0, ones, o_sb[:, 0, :])
                pe.wait_ge(sqs, n.at("sqs", 1))
                stat(1, ones, sqh[:, 0, :])

            pe.wait_ge(dves, n.at("dve", 1))
            emptied(3)
            pe.matmul(bank[3][:, 0:2], ones[0:64, :], lprod[0:64, :], start=True, stop=True).then_inc(stats, 1)
            n.past(LAM)

            with n.turns(pe, HEADS, DIFF):
                emptied(0)
                h_panel(0, bank[0][:, :])
                emptied(1)
                h_panel(1, bank[1][:, :])
                pe.wait_ge(sqs, n.at("sqs", 1))
                stat(0, blocks64, sqh[:, 0, :])
                emptied(2)
                h_panel(2, lambda t: bank[2][:, t * P:(t + 1) * P], True)
                pe.wait_ge(sqs, n.at("sqs", 2))
                stat(1, blocks64, sqh[:, 1, :])
                emptied(0, 1)
                emptied(1, 1)
                emptied(2, 1)
                for s in range(8 + 2):
                    if s < 8:
                        i, m = s // 2, s % 2
                        half = slice(64 * m, 64 * m + 64)
                        scores_of(s, [qs[half, 0, i * P:(i + 1) * P]], [ks[half, 0, 0:(i + 1) * P]], (i + 1) * P)
                    if s >= 2 and s % 2 == 1:
                        i = (s - 2) // 2
                        turn_probs(i, i + 1, o_sb[:, i % 2, :], i + 1)
                emptied(6, 4)
                emptied(7)
                causal_out(bank[7], lambda j: vs[:, j * P:(j + 1) * P]).then_inc(outs, 1)
                pe.wait_ge(sqs, n.at("sqs", 3))
                stat(2, ones, sqh[:, 0, :])
            out_product(OUT_X, hid, cats, n.at("cats"))
            norm()
            n.past(NORM)

            h_done = n.at("hlos")
            with n.turns(pe, HEADS, MEM1):
                pe.wait_ge(mems, n.at("mems"))
                for c in range(2):
                    emptied(c)
                    panel(c, bank[c][:, 0:M], memh)
                emptied(2)
                for c in range(2):
                    panel(2 + c, lambda t: bank[2][:, t * M + c * P:t * M + (c + 1) * P], memh, True)
                    if c == 0:
                        pe.wait_ge(sqs, n.at("sqs", 1))
                        stat(0, ones, sqh[:, 0, 0:M], sqh[:, 1, 0:M])
                for c in range(2):
                    emptied(c, 1)
                    h_panel(c, bank[c][:, :], ready=h_done)
                pe.wait_ge(sqs, n.at("sqs", 2))
                stat(1, ones, sqh[:, 0, :], sqh[:, 1, :])
                emptied(2, 1)
                for c in range(2):
                    emptied(c, 2)
                for s in range(TT + 2):
                    if s < TT:
                        scores_of(s, [qs[:, c, s * P:(s + 1) * P] for c in range(2)],
                                  [ks[:, c, 0:M] for c in range(2)], M)
                    if s >= 2:
                        turn_probs(s - 2, MT, ex[:, (s - 2) % 3, :], s - 1)
                emptied(6, 4)
                for c in range(2):
                    emptied(7, c)
                    for j in range(MT):
                        mm = pe.matmul(bank[7][:, :], vs[:, j * M + c * P:j * M + (c + 1) * P], PT[:, j, :],
                                       start=(j == 0), stop=(j == MT - 1))
                    mm.then_inc(outs, 1)
            out_product(OUT_X, hid, free[7], n.at("free7"))
            norm()
            n.past(NORM)
            ffn(FFN_DOWN, True)
            norm()
            n.past(RESCALE)
            norm()
            n.past(NORM)

            pe.wait_ge(tables_loaded, 16)
            pe.wait_ge(params_loaded, 16)
            pe.wait_ge(cmp_loaded, 48)
            pe.wait_ge(h32s, n.at("h32s"))
            emptied(2)
            for t in range(TT):
                for k in range(KD):
                    mm = pe.matmul(bank[2][:, t * 56:(t + 1) * 56], h32[:, k, t * P:(t + 1) * P], gate_w[:, k, :],
                                   start=(k == 0), stop=(k == KD - 1))
            mm.then_inc(gates_made, 1)
            pe.wait_ge(dves, n.at("dve", 3))
            emptied(3)
            for t in range(TT):
                mm = pe.matmul(bank[3][0:4, t * P:T], lf[:, 1, t, :], tables[:, K_CUM:K_CUM + T - t * P],
                               start=(t == 0), stop=(t == TT - 1))
            mm.then_inc(stats, 1)
            emptied(6)
            for t in range(TT):
                pe.matmul(bank[6][0:4, t * P:T], lf[:, 2, t, :], tables[:, K_CUM:K_CUM + T - t * P],
                          start=(t == 0), stop=False)
            for t in range(TT):
                mm = pe.matmul(bank[6][0:4, t * P:(t + 1) * P], ifp[:, t, 0:4], ident, start=False,
                               stop=(t == TT - 1))
            mm.then_inc(turned, 1)
            emptied(6, 1)
            emptied(3, 1)
            for t in range(TT):
                mm = pe.matmul(bank[3][:, 4 * t:4 * t + 4], rows[0:4, 0, t * P:(t + 1) * P], ident[0:4, 0:4],
                               start=True, stop=True)
            mm.then_inc(stats, 1)
            n.past(GATES)

            for g in range(GROUPS):
                emptied(g % 2, g // 2)
                h_panel(g, bank[g % 2][:, :])
            emptied(0, 2)
            emptied(1, 2)
            pe.wait_ge(dves, n.at("dve", 1))
            width = (GROUPS + 1) * CMP_N
            for row, b, done in ((slice(0, 64), 3, stats), (slice(64, P), 6, turned)):
                emptied(b)
                for l in range(CMP_L):
                    mm = pe.matmul(bank[b][:, 0:width].rearrange("p (g b) -> p g b", b=CMP_N), w1c[row, l, :],
                                   kvc[row, :, l:l + CMP_S * (CMP_N - 1) + 1:CMP_S],
                                   start=(l == 0), stop=(l == CMP_L - 1))
                mm.then_inc(done, 1)
            emptied(3, 1)
            pe.matmul(bank[3][:, 0:GROUPS * CMP_N], w2[:, 0:P], hidk, start=True, stop=True).then_inc(stats, 1)
            emptied(6, 1)
            for g in range(GROUPS):
                mm = pe.matmul(bank[6][:, 64 * g:64 * (g + 1)], hidv[:, g, :, :].rearrange("p a b -> p (a b)"),
                               w2[:, P:P + 64], start=True, stop=True)
            mm.then_inc(turned, 1)
            n.past(CMP)

            with n.turns(pe, GROUPS, NSA):
                emptied(0)
                h_panel(0, bank[0][:, :])
                emptied(1)
                h_panel(1, bank[1][:, :])
                emptied(3)
                h_panel(2, bank[3][:, :])
                emptied(2)
                h_panel(3, lambda t: bank[2][:, t * P:(t + 1) * P], True)
                emptied(0, 1)
                emptied(1, 1)
                pe.wait_ge(heads, n.at("heads", 1))
                for i in range(TT + 1):
                    if i < TT:
                        for odd in range(2):
                            half = slice(64 * odd, 64 * odd + 64)
                            emptied(4 + odd, i)
                            for pair in range(2):
                                mm = pe.matmul(bank[4 + odd][:, pair * 32:pair * 32 + CMP_N],
                                               qs[half, pair, i * P:(i + 1) * P], kc2[half, :],
                                               start=True, stop=True)
                            mm.then_inc(scores, 1)
                    if i >= 1:
                        pe.wait_ge(probs, n.at("probs", i))
                        emptied(6, i - 1)
                        pe.transpose(bank[6][:, 0:P], pc[:, :, :].rearrange("p a b -> p (a b)"), ident).then_inc(turned, 1)
                pe.wait_ge(twins, 32 * n.at("twins", 1))
                emptied(2, 1)
                for s in range(NJ + 3):
                    if s < NJ:
                        head, br, i = s // 8, s // 4 % 2, s % 4
                        half = slice(64 * (head % 2), 64 * (head % 2) + 64)
                        b = 4 + s % 2
                        emptied(b, 4 + s // 2)
                        pe.matmul(bank[b][:, 0:(i + 1) * P], qs[half, head // 2, i * P:(i + 1) * P],
                                  ks[half, br, 0:(i + 1) * P], start=True, stop=True).then_inc(scores, 1)
                    if s >= 3 and (s - 3) % 4 == 3:
                        head, br = (s - 3) // 8, (s - 3) // 4 % 2
                        emptied(6, 4 + s - 2)
                        if head % 2 == 0 and br == 0:
                            emptied(7, head // 2)
                            pe.matmul(bank[7][:, :], vb[:, head // 2, :], PTc, start=True, stop=True)
                        half = slice(64 * (head % 2), 64 * (head % 2) + 64)
                        mm = causal_out(bank[7][half, :], lambda j: vs[:, j * P + 64 * br:j * P + 64 * br + 64],
                                        start=False)
                        if head % 2 == 1 and br == 1:
                            mm.then_inc(outs, 1)
                    if 2 <= s < NJ + 2:
                        turn_probs(4 + s - 2, (s - 2) % 4 + 1, ex[:, (s - 2) % 3, :], 4 + s - 1)

            pe.wait_ge(dves, n.at("dve"))
            pe.wait_ge(acts, n.at("acts"))
            for s in range(8):
                scores_of(s, [ident[0:4, s % 4:s % 4 + 1].to_broadcast([4, P])],
                          [rows[0:4, 1 if s < 4 else 3, :]], T)
            n.past(SPREAD)
            with n.turns(pe, HEADS, ML):
                emptied(0)
                h_panel(0, bank[0][:, :])
                emptied(1)
                h_panel(1, bank[1][:, :])
                emptied(0, 1)
                h_panel(2, bank[0][:, :])
                emptied(2)
                h_panel(3, lambda t: bank[2][:, t * P:(t + 1) * P], True)
                pe.wait_ge(convs, n.at("convs", 2))
                emptied(2, 1)
                emptied(7)
                emptied(6)
                for j in range(TT + 1):
                    if j < TT:
                        scores_of(j, [ks[:, 0, j * P:(j + 1) * P]], [qs[:, 0, j * P:T]], T - j * P)
                    if j >= 1:
                        a = j - 1
                        emptied(4 + a % 2, a // 2 + 1)
                        mm = pe.matmul(bank[7][:, a * P:T], vs[:, a * P:j * P], PT[:, a, a * P:T],
                                       start=(a == 0), stop=(j == TT))
                        if j == TT:
                            mm.then_inc(outs, 1)
                        mm = pe.matmul(bank[6][:, a * P:T], ones, PT[:, a, a * P:T],
                                       start=(a == 0), stop=(j == TT))
                mm.then_inc(turned, 1)
                pe.wait_ge(sqs, n.at("sqs", 1))
                stat(0, ones, sqh[:, 0, :])

            pe.wait_ge(mems, n.at("mems"))
            with n.turns(pe, HEADS, MEM2):
                emptied(0)
                h_panel(0, bank[0][:, :])
                emptied(1)
                panel(1, bank[1][:, 0:M], memh)
                emptied(2)
                panel(2, lambda t: bank[2][:, t * P:(t + 1) * P], memh, True)
                emptied(0, 1)
                emptied(1, 1)
                emptied(2, 1)
                for s in range(TT + 2):
                    if s < TT:
                        scores_of(s, [qs[:, 0, s * P:(s + 1) * P]], [ks[:, 0, 0:M]], M)
                    if s >= 2:
                        turn_probs(s - 2, MT, ex[:, (s - 2) % 3, :], s - 1)
                emptied(6, 4)
                emptied(7)
                for j in range(MT):
                    mm = pe.matmul(bank[7][:, :], vs[:, j * P:(j + 1) * P], PT[:, j, :],
                                   start=(j == 0), stop=(j == MT - 1))
                mm.then_inc(outs, 1)

            branches_done = (n.at("cats"), n.at("free7"))
            with n.turns(pe, KD, MERGE):
                for j, (k0, kt) in enumerate(((0, 8), (8, 4), (12, 4))):
                    emptied(0, j)
                    h_panel(j, bank[0][:, :])
                    emptied(1, j)
                    pe.wait_ge(cats, branches_done[0])
                    pe.wait_ge(free[7], branches_done[1])
                    panel(2 * j + 1, bank[1][:, :], hid, k0=k0, ks_=kt)
            out_product(OUT_Z, big8, dves, n.at("dve"))
            norm()
            n.past(ADD_Z)
            norm()
            n.past(NORM)
            ffn(FFN_DOWN_Z)
            norm()
            n.past(ADD_Z_LAST)

        @block.scalar
        def _(act):
            n = Counts()
            act.dma_start(params[:, :], par).then_inc(params_loaded, 16)
            act.dma_start(x[:, :, :], xT).then_inc(x_loaded, 16)
            act.dma_start(consts[:, :], con).then_inc(consts_loaded, 16)
            act.dma_start(memh[:, :, :], memT).then_inc(mem_loaded, 16)
            act.dma_start(tables[:, :], tab).then_inc(tables_loaded, 16)
            act.dma_start(gate_w[:, :, :], gatew).then_inc(cmp_loaded, 16)
            act.dma_start(w1c[:, :, :], cmpw1).then_inc(cmp_loaded, 16)
            act.dma_start(w2[:, :], cmpw2).then_inc(cmp_loaded, 16)

            def square(k, parity, source, first=False):
                if not (first and k < 2):
                    act.wait_ge(sums, n.at("sums", k - 1))
                act.activation(sq[:, parity, 0:source.shape[1]], source, ACT.Square).then_inc(squares, 1)

            def root(k):
                act.wait_ge(rcp, n.at("rcp", k + 1))
                act.activation(rinv[:, :], var[:, :], ACT.Sqrt).then_inc(rinvs, 1)

            def head_square(k, half, source, read):
                act.wait_ge(stats, n.at("stats", read))
                act.activation(sqh[:, half, 0:source.shape[1]], source, ACT.Square).then_inc(sqs, 1)

            def copy(out, source, b, scale=1.0):
                act.activation(out, source, ACT.Copy, scale=scale).then_inc(free[b], 1)

            def x_squares(turns, events, per):
                with n.turns(act, turns, events) as i:
                    for k in range(per):
                        act.wait_ge(xs, n.at("xs", k + 1))
                        square(k, k % 2, x[:, bass.ds(i * per + k, 1), :].rearrange("p a t -> p (a t)"))

            def z_squares(turns, events, per, z, panels_each):
                with n.turns(act, turns, events) as i:
                    for k in range(per):
                        b = k % 2
                        act.wait_ge(products, n.at("products", panels_each * (k + 1)))
                        square(k, k % 2, bank[b][:, :])
                        copy(z[:, bass.ds(i * per + k, 1), :].rearrange("p a t -> p (a t)"), bank[b][:, :], b)

            def high_part(nth, j, product, load=1):
                act.wait_ge(loaded[j], 16 * n.at(f"loads{j}", load))
                if product is not None:
                    act.wait_ge(products, n.at("products", product))
                act.activation(parts[nth % 2][:, 0, :, :], slot[j][:, 0:KD, :], ACT.Copy).then_inc(highs, 1)

            def norm(ffn=False):
                if ffn:
                    for u in range(2):
                        high_part(u, u, u - RING if n.base.get("products", 0) else None)
                root(0)
                for k in range(KD):
                    act.wait_ge(h32s, n.at("h32s", k + 1))
                    act.activation(hhi[:, k, :], h32[:, k, :], ACT.Copy).then_inc(hhis, 1)
                n.past(NORM)

            def ffn_up():
                for last in (False, True):
                    with n.turns(act, 1 if last else KF // 2 - 1, FFN_UP):
                        for u in range(2):
                            if u == 0:
                                high_part(2, 2, 1)
                            elif not last:
                                high_part(4, 0, 3, load=2)
                            act.wait_ge(products, n.at("products", 2 * u + 1))
                            act.wait_ge(free[1], n.at("free1", u - 1) if u else n.at("free1"))
                            act.activation(silu[:, u, :], bank[0][:, :], ACT.Silu).then_inc(free[0], 1)
                            if u == 0:
                                high_part(3, 3, 2)
                            elif not last:
                                high_part(5, 1, 4, load=2)

            def ffn_of_memory(loads):
                act.wait_ge(mem_loaded, 16 * loads)
                for k in range(KD):
                    square(k, k % 2, memh[:, k, :])
                n.past(SQUARES)
                ffn_up()
                root(0)
                n.past(MEM_NORM)
                n.past(CLEAR)
                x_squares(2, FFN_DOWN, 4)

            def exponential(k, width):
                act.wait_ge(negmaxs, n.at("negmax", k + 1))
                act.activation(ex[:, k % 3, 0:width], sc[:, k % 2, 0:width], ACT.Exp, bias=negmax[:, k % 2:k % 2 + 1],
                               accum_out=esum[:, k % 3:k % 3 + 1]).then_inc(exps, 1)

            def place_turned(k, i, blocks):
                act.wait_ge(turned, n.at("turned", k + 1))
                copy(PT[:, 0:blocks, i * P:(i + 1) * P],
                     bank[6][:, 0:blocks * P].rearrange("p (a b) -> p a b", a=blocks), 6)

            act.wait_ge(x_loaded, 16)
            for k in range(KD):
                square(k, k % 2, x[:, k, :], first=True)
            n.past(SQUARES)
            norm(ffn=True)
            ffn_of_memory(1)
            norm()

            def load_strip(i):
                act.wait_ge(cats, n.at("cats"))
                act.dma_start(strip[:, :], headtab[bass.ds(i, 1)].rearrange("a p t -> p (a t)")).then_inc(strips, 16)

            with n.turns(act, HEADS, RET) as i:
                load_strip(i)
                act.wait_ge(products, n.at("products", 1))
                copy(qs[:, 0, :], bank[0][:, :], 0)
                act.wait_ge(products, n.at("products", 3))
                copy(vs[:, :], bank[2][:, :], 2)
                act.wait_ge(products, n.at("products", 4))
                act.wait_ge(cats, n.at("cats"))
                act.activation(silu[:, 0, :], bank[0][:, :], ACT.Silu).then_inc(free[0], 1)
                act.wait_ge(outs, n.at("outs", 1))
                copy(o_sb[:, 0, :], bank[7][:, :], 7)
                act.wait_ge(free[3], n.at("free3", 1))
                head_square(0, 0, o_sb[:, 1, :], 1)
                root(0)

            act.wait_ge(stats, n.at("stats", 1))
            act.activation(le, bank[3][:, 0:2], ACT.Exp).then_inc(free[3], 1)
            n.past(LAM)

            with n.turns(act, HEADS, DIFF) as i:
                load_strip(i + HEADS)
                for c in range(2):
                    act.wait_ge(products, n.at("products", c + 1))
                    head_square(c, c, bank[c][:, :], 0)
                root(0)
                root(1)
                act.wait_ge(products, n.at("products", 3))
                copy(vs[:, :], bank[2][:, :], 2)
                for s in range(8 + 4):
                    if s < 8:
                        exponential(s, (s // 2 + 1) * P)
                    if s >= 4 and s % 2 == 1:
                        i = (s - 4) // 2
                        place_turned(i, i, i + 1)
                act.wait_ge(outs, n.at("outs", 1))
                head_square(2, 0, bank[7][:, :], 2)
                root(2)
            n.past(CLEAR)
            x_squares(2, OUT_X, 4)
            norm()

            with n.turns(act, HEADS, MEM1) as i:
                for c in range(2):
                    act.wait_ge(products, n.at("products", c + 1))
                    act.wait_ge(stats, n.at("stats"))
                    mm = act.activation(sqh[:, c, 0:M], bank[c][:, 0:M], ACT.Square)
                mm.then_inc(sqs, 1)
                root(0)
                act.wait_ge(products, n.at("products", 4))
                copy(vs[:, :], bank[2][:, :], 2)
                for c in range(2):
                    act.wait_ge(products, n.at("products", c + 5))
                    act.wait_ge(stats, n.at("stats", 1))
                    mm = act.activation(sqh[:, c, :], bank[c][:, :], ACT.Square)
                mm.then_inc(sqs, 1)
                root(1)
                for s in range(TT + 2):
                    if s < TT:
                        exponential(s, M)
                    if s >= 2:
                        place_turned(s - 2, s - 2, MT)
                for c in range(2):
                    act.wait_ge(outs, n.at("outs", c + 1))
                    copy(hid[:, bass.ds(i * 2 + c, 1), :].rearrange("p a t -> p (a t)"), bank[7][:, :], 7)
            act.dma_start(memh[:, :, :], mem2T).then_inc(mem_loaded, 16)
            n.past(CLEAR)
            x_squares(2, OUT_X, 4)
            norm(ffn=True)
            ffn_of_memory(2)
            root(0)
            for k in range(KD):
                act.wait_ge(xs, n.at("xs", k + 1))
                square(k, k % 2, x[:, k, :])
            n.past(RESCALE)
            norm()

            act.wait_ge(gates_made, 1)
            g4 = bank[2][:, 0:TT * 56].rearrange("p (t c) -> p t c", t=TT)
            act.activation(gates[:, :, :], g4[:, :, 0:48], ACT.Sigmoid).then_inc(acts, 1)
            act.wait_ge(free[2], n.at("free2", 1))
            act.activation(lf[:, 3, :, :], ifp[:, :, 4:8], ACT.Abs).then_inc(acts, 1)
            act.wait_ge(acts, 2)
            act.activation(lf[:, 3, :, :], lf[:, 3, :, :], ACT.Exp, scale=-1.0).then_inc(acts, 1)
            act.wait_ge(acts, 3)
            act.activation(lf[:, 3, :, :], lf[:, 3, :, :], ACT.Ln, bias=1.0).then_inc(acts, 1)
            act.wait_ge(free[3], n.at("free3", 1))
            act.activation(rows[0:4, 3, :], rows[0:4, 2, :], ACT.Exp, scale=-1.0).then_inc(acts, 1)
            n.past(GATES)
            for g in range(GROUPS):
                act.wait_ge(products, n.at("products", g + 1))
                copy(kvc[:, g, :], bank[g % 2][:, :], g % 2)
            all_n, bias_at = GROUPS * CMP_N, GROUPS * CMP_N
            act.wait_ge(stats, n.at("stats", 1))
            act.activation(pebias[:, 0:1], bank[3][:, bias_at:bias_at + 1], ACT.Copy).then_inc(acts, 1)
            act.wait_ge(acts, n.at("acts", 1))
            act.activation(hidk, bank[3][:, 0:all_n], ACT.Silu, bias=pebias[:, 0:1]).then_inc(free[3], 1)
            act.wait_ge(turned, n.at("turned", 1))
            act.activation(pebias[:, 1:2], bank[6][:, bias_at:bias_at + 1], ACT.Copy).then_inc(acts, 1)
            act.wait_ge(acts, n.at("acts", 2))
            act.wait_ge(dves, n.at("dve", 2))
            for a in range(4):
                mm = act.activation(hidv[:, :, a, 0:CMP_N], bank[6][:, 0:all_n].rearrange("p (g b) -> p g b", g=GROUPS),
                                    ACT.Silu, bias=pebias[:, 1:2])
            mm.then_inc(free[6], 1)
            act.wait_ge(stats, n.at("stats", 2))
            copy(kc_all, bank[3][:, 0:all_n], 3)
            n.past(CMP)

            act.wait_ge(zeros_set, 1)
            with n.turns(act, GROUPS, NSA) as i:
                act.wait_ge(products, n.at("products", 1))
                copy(qs[:, 0, :], bank[0][:, :], 0, 64 ** -0.5)
                act.wait_ge(products, n.at("products", 2))
                copy(qs[:, 1, :], bank[1][:, :], 1, 64 ** -0.5)
                act.wait_ge(products, n.at("products", 3))
                act.activation(ks[0:64, 0, :], bank[3][0:64, :], ACT.Copy)
                copy(ks[64:P, 1, :], bank[3][64:P, :], 3)
                act.wait_ge(free[3], n.at("free3", 1))
                act.dma_start(ks[64:P, 0, :], ks[0:64, 0, :]).then_inc(twins, 16)
                act.dma_start(ks[0:64, 1, :], ks[64:P, 1, :]).then_inc(twins, 16)
                act.wait_ge(products, n.at("products", 4))
                copy(vs[:, :], bank[2][:, :], 2)
                for s in range(TT + 1):
                    if s < TT:
                        act.wait_ge(cmps, n.at("cmps", s + 1))
                        c4 = sc[:, s % 2, 0:P].rearrange("p (a b) -> p a b", a=4)[:, :, 0:CMP_N]
                        e4 = ex[:, s % 2, 0:P].rearrange("p (a b) -> p a b", a=4)[:, :, 0:CMP_N]
                        act.activation(e4, c4, ACT.Exp).then_inc(exps, 1)
                    if s >= 1:
                        act.wait_ge(turned, n.at("turned", s))
                        copy(PTc[:, (s - 1) * P:s * P], bank[6][:, 0:P], 6)
                for s in range(NJ + 2):
                    if s < NJ:
                        act.wait_ge(negmaxs, n.at("negmax", s + 1))
                        width = (s % 4 + 1) * P
                        act.activation(ex[:, s % 3, 0:width], sc[:, s % 2, 0:width], ACT.Exp,
                                       bias=negmax[:, s % 2:s % 2 + 1],
                                       accum_out=esum[:, s % 3:s % 3 + 1]).then_inc(exps, 1)
                    if s >= 2:
                        place_turned(4 + s - 2, (s - 2) % 4, (s - 2) % 4 + 1)
                    if s >= 3 and (s - 3) % 16 == 15:
                        pair = (s - 3) // 16
                        act.wait_ge(outs, n.at("outs", pair + 1))
                        copy(hid[:, bass.ds(i * 2 + pair, 1), :].rearrange("p a t -> p (a t)"), bank[7][:, :], 7)
                act.wait_ge(outs, n.at("outs", 2))
                copy(hid[:, bass.ds(i * 2 + 1, 1), :].rearrange("p a t -> p (a t)"), bank[7][:, :], 7)

            for s in range(8):
                act.wait_ge(scores, n.at("scores", s + 1))
                copy((negM if s < 4 else emb)[:, s % 4, :], bank[4 + s % 2][:, :], 4 + s % 2,
                     -1.0 if s < 4 else 1.0)
            n.past(SPREAD)
            act.wait_ge(pads, 1)
            with n.turns(act, HEADS, ML):
                act.wait_ge(heads, n.at("heads", 1))
                for c in range(2):
                    act.wait_ge(products, n.at("products", c + 1))
                    copy(xp[:, c, 3:T + 3], bank[c][:, :], c)
                for c, dst in ((0, qs), (1, ks)):
                    act.wait_ge(dves, n.at("dve", 4 * c + 4))
                    act.activation(dst[:, 0, :], o_sb[:, c, :], ACT.Silu, bias=hp[:, 8 + c:9 + c]).then_inc(convs, 1)
                act.wait_ge(products, n.at("products", 3))
                act.wait_ge(cats, n.at("cats"))
                act.activation(silu[:, 0, :], bank[0][:, :], ACT.Sigmoid).then_inc(free[0], 1)
                act.wait_ge(products, n.at("products", 4))
                copy(vs[:, :], bank[2][:, :], 2)
                for j in range(TT):
                    act.wait_ge(dves, n.at("dve", 9 + j))
                    act.activation(hid[:, 18 + j, 0:T - j * P], hid[:, 18 + j, 0:T - j * P], ACT.Exp).then_inc(exps, 1)
                act.wait_ge(turned, n.at("turned", 1))
                act.activation(var[:, :], bank[6][:, :], ACT.Abs).then_inc(free[6], 1)
                act.wait_ge(free[7], n.at("free7", 1))
                head_square(0, 0, o_sb[:, 0, :], 0)
                root(0)

            with n.turns(act, HEADS, MEM2) as i:
                act.wait_ge(products, n.at("products", 1))
                copy(qs[:, 0, :], bank[0][:, :], 0, P ** -0.5)
                act.wait_ge(products, n.at("products", 2))
                copy(ks[:, 0, 0:M], bank[1][:, 0:M], 1)
                act.wait_ge(products, n.at("products", 3))
                copy(vs[:, 0:MT * P], bank[2][:, 0:MT * P], 2)
                for s in range(TT + 2):
                    if s < TT:
                        exponential(s, M)
                    if s >= 2:
                        place_turned(s - 2, s - 2, MT)
                act.wait_ge(outs, n.at("outs", 1))
                copy(hid[:, bass.ds(i + 12, 1), :].rearrange("p a t -> p (a t)"), bank[7][:, :], 7)

            with n.turns(act, KD, MERGE):
                high_part(0, 0, -1)
                high_part(1, 2, -3)
                for j in range(3):
                    if j == 1:
                        high_part(2, 4, 1)
                    act.wait_ge(products, n.at("products", 2 * j + 1))
                    act.wait_ge(free[1], n.at("free1", j) if j < 1 else n.at("free1", j - 1))
                    act.activation(silu[:, j, :], bank[0][:, :], ACT.Sigmoid).then_inc(free[0], 1)
            n.past(CLEAR)
            z_squares(2, OUT_Z, 4, hid, 1)
            root(0)
            for k in range(KD):
                act.wait_ge(xs, n.at("xs", k + 1))
                square(k, k % 2, x[:, k, :])
            n.past(ADD_Z)
            norm(ffn=True)
            ffn_up()
            n.past(CLEAR)
            z_squares(2, FFN_DOWN_Z, 4, big8, 3)
            root(0)
            n.past(ADD_Z_LAST)

        @block.vector
        def _(dve):
            n = Counts()

            def reciprocal_mean(k, r, scale, eps, width=T):
                dve.wait_ge(stats, n.at("stats", k + 1))
                dve.tensor_scalar(var[:, 0:width], bank[3][:, 0:width], scale, eps, ALU.mult, ALU.add).then_inc(free[3], 1)
                dve.wait_ge(free[3], n.at("free3", k + 1))
                dve.reciprocal(var[:, 0:width], var[:, 0:width]).then_inc(rcp, 1)
                dve.wait_ge(rinvs, n.at("rinv", r + 1))

            def scaled(out, source, gain, width=T):
                return dve.scalar_tensor_tensor(out, source, gain, rinv[:, 0:width], ALU.mult, ALU.mult)

            def apply_norm(g):
                for k in range(KD + 2):
                    if k < KD:
                        scaled(h32[:, k, :], x[:, k, :], params[:, g + k:g + k + 1]).then_inc(h32s, 1)
                    if k >= 2:
                        a = k - 2
                        dve.wait_ge(hhis, n.at("hhis", a + 1))
                        dve.tensor_tensor(hlo[:, a, :], h32[:, a, :], hhi[:, a, :].bitcast(F32),
                                          ALU.subtract).then_inc(hlos, 1)

            def norm(g):
                reciprocal_mean(0, 0, 1.0 / D, EPS)
                apply_norm(g)
                n.past(NORM)

            def tile(a, k):
                return a[:, bass.ds(k, 1), :].rearrange("p a t -> p (a t)")

            def ffn_up():
                with n.turns(dve, KF // 2, FFN_UP) as i:
                    for u in range(2):
                        dve.wait_ge(free[0], n.at("free0", u + 1))
                        dve.wait_ge(products, n.at("products", 2 * u + 2))
                        dve.tensor_tensor(tile(hid, i * 2 + u), silu[:, u, :], bank[1][:, :],
                                          ALU.mult).then_inc(free[1], 1)

            def norm_memory(g):
                reciprocal_mean(0, 0, 1.0 / D, EPS, M)
                for k in range(KD):
                    last = scaled(memh[:, k, :], memh[:, k, :], params[:, g + k:g + k + 1], M)
                last.then_inc(mems, 1)
                n.past(MEM_NORM)

            def ffn_down():
                n.past(CLEAR)
                with n.turns(dve, 2, FFN_DOWN) as i:
                    for u in range(4):
                        dve.wait_ge(products, n.at("products", len(DOWN) * (u + 1)))
                        dve.scalar_tensor_tensor(tile(x, i * 4 + u), bank[u % 2][:, :], 0.5, tile(x, i * 4 + u),
                                                 ALU.mult, ALU.add).then_inc(xs, 1)

            def out_x():
                n.past(CLEAR)
                with n.turns(dve, 2, OUT_X) as i:
                    for k in range(4):
                        dve.wait_ge(products, n.at("products", k + 1))
                        dve.tensor_tensor(tile(x, i * 4 + k), bank[k % 2][:, :], tile(x, i * 4 + k),
                                          ALU.add).then_inc(xs, 1)

            def masked_scores(k, width, mask, b_more=0, s_more=0):
                b = 4 + k % 2
                dve.wait_ge(scores, n.at("scores", s_more + k + 1))
                dve.memset(lanes[:, 42:43], 0.0)
                dve.tensor_tensor_reduce(sc[:, k % 2, 0:width], bank[b][:, 0:width], mask, 1.0, -3e38,
                                         ALU.add, ALU.max, maxs[:, k % 2:k % 2 + 1]).then_inc(free[b], 1)
                dve.wait_ge(free[b], n.at(f"free{b}", b_more + k // 2 + 1))
                dve.tensor_scalar(negmax[:, k % 2:k % 2 + 1], maxs[:, k % 2:k % 2 + 1], -1.0, None,
                                  ALU.mult).then_inc(negmaxs, 1)

            def normalise(k, width, gate=None, d_more=0, e_more=0):
                dve.wait_ge(exps, n.at("exps", e_more + k + 1))
                dve.reciprocal(rsm[:, k % 3:k % 3 + 1], esum[:, k % 3:k % 3 + 1]).then_inc(dves, 1)
                dve.wait_ge(dves, n.at("dve", d_more + k + 1))
                e = ex[:, k % 3, 0:width]
                if gate is None:
                    dve.tensor_scalar(e, e, rsm[:, k % 3:k % 3 + 1], None, ALU.mult).then_inc(probs, 1)
                else:
                    dve.tensor_scalar(e, e, rsm[:, k % 3:k % 3 + 1], gate, ALU.mult, ALU.mult).then_inc(probs, 1)

            no_mask = tables[:, K_CAUS:K_CAUS + M]

            for s in (*free, cats, xs):
                dve.sem_inc(s, 1)
            dve.wait_ge(params_loaded, 16)
            dve.wait_ge(tables_loaded, 16)
            n.past(SQUARES)
            norm(G_FFN1)
            n.past(SQUARES)
            ffn_up()
            norm_memory(G_MEMKV)
            ffn_down()
            norm(G_MIX)

            with n.turns(dve, HEADS, RET) as i:
                dve.wait_ge(products, n.at("products", 2))
                dve.tensor_copy(ks[:, 0, :], bank[1][:, :]).then_inc(free[1], 1)
                dve.wait_ge(strips, 16 * n.at("strips", 1))
                for j in range(TT):
                    b = 4 + j % 2
                    dve.wait_ge(scores, n.at("scores", j + 1))
                    dve.tensor_tensor(PT[:, j, j * P:T], bank[b][:, 0:T - j * P], strip[:, 0:T - j * P],
                                      ALU.mult).then_inc(free[b], 1)
                dve.wait_ge(stats, n.at("stats", 1))
                dve.wait_ge(free[7], n.at("free7", 1))
                dve.scalar_tensor_tensor(o_sb[:, 1, :], bank[3][:, :], -1.0 / P, o_sb[:, 0, :],
                                         ALU.mult, ALU.add).then_inc(free[3], 1)
                reciprocal_mean(1, 0, 1.0 / P, EPS)
                scaled(o_sb[:, 1, :], o_sb[:, 1, :], params[:, C_RET:C_RET + 1]).then_inc(dves, 1)
                dve.wait_ge(dves, n.at("dve", 1))
                dve.wait_ge(free[0], n.at("free0", 2))
                dve.tensor_tensor(tile(hid, i), o_sb[:, 1, :], silu[:, 0, :], ALU.mult).then_inc(cats, 1)

            dve.tensor_tensor(lprod[0:64, :], params[0:64, C_LAM:C_LAM + 2], params[0:64, C_LAM + 2:C_LAM + 4],
                              ALU.mult).then_inc(dves, 1)
            dve.tensor_scalar(dn_gain, params[:, C_DN:C_DN + 1], 1.0 - LAM_INIT, None, ALU.mult).then_inc(dves, 1)
            dve.wait_ge(free[3], n.at("free3", 1))
            dve.tensor_scalar(nlam, le[:, 1:2], le[:, 0:1], -LAM_INIT, ALU.subtract, ALU.add).then_inc(dves, 1)
            n.past(LAM)
            dve.wait_ge(dves, n.at("dve"))

            with n.turns(dve, HEADS, DIFF) as i:
                reciprocal_mean(0, 0, 1.0, 64 * EPS)
                scaled(qs[:, 0, :], bank[0][:, :], params[:, C_DQ:C_DQ + 1]).then_inc(free[0], 1)
                reciprocal_mean(1, 1, 1.0 / 64, EPS)
                scaled(ks[:, 0, :], bank[1][:, :], params[:, C_DK:C_DK + 1]).then_inc(free[1], 1)
                dve.wait_ge(strips, 16 * n.at("strips", 1))
                for s in range(8 + 1):
                    if s < 8:
                        width = (s // 2 + 1) * P
                        masked_scores(s, width, strip[:, T - width:T])
                    if s >= 1:
                        a, row, m = s - 1, (s - 1) // 2, (s - 1) % 2
                        width = (row + 1) * P
                        r, e = rsm[:, a % 3:a % 3 + 1], ex[:, a % 3, 0:width]
                        dve.wait_ge(exps, n.at("exps", a + 1))
                        dve.reciprocal(r, esum[:, a % 3:a % 3 + 1]).then_inc(dves, 1)
                        dve.wait_ge(dves, n.at("dve", 2 * a + 1))
                        if m == 0:
                            dve.tensor_scalar(e, e, r, None, ALU.mult).then_inc(dves, 1)
                        else:
                            dve.tensor_scalar(r, r, nlam, None, ALU.mult).then_inc(dves, 1)
                            dve.wait_ge(dves, n.at("dve", 2 * a + 2))
                            dve.scalar_tensor_tensor(o_sb[:, row % 2, 0:width], e, r, ex[:, (a - 1) % 3, 0:width],
                                                     ALU.mult, ALU.add).then_inc(probs, 1)
                reciprocal_mean(2, 2, 1.0 / P, EPS)
                scaled(tile(hid, i + HEADS), bank[7][:, :], dn_gain).then_inc(free[7], 1)
                dve.wait_ge(free[7], n.at("free7", 1))
                dve.tensor_copy(lanes[:, 40:41], lanes[:, 8:9]).then_inc(cats, 1)
            out_x()
            norm(G_MEMQ)

            with n.turns(dve, HEADS, MEM1):
                reciprocal_mean(0, 0, 1.0 / M, EPS, M)
                for c in range(2):
                    scaled(ks[:, c, 0:M], bank[c][:, 0:M], params[:, C_MK + c:C_MK + c + 1], M).then_inc(free[c], 1)
                reciprocal_mean(1, 1, 1.0, M * EPS)
                for c in range(2):
                    scaled(qs[:, c, :], bank[c][:, :], params[:, C_MQ + c:C_MQ + c + 1]).then_inc(free[c], 1)
                for s in range(TT + 1):
                    if s < TT:
                        masked_scores(s, M, no_mask)
                    if s >= 1:
                        normalise(s - 1, M)
            out_x()
            norm(G_FFN2)
            n.past(SQUARES)
            ffn_up()
            norm_memory(G_MEM2)
            ffn_down()
            reciprocal_mean(0, 0, 1.0 / D, EPS)
            for k in range(KD):
                scaled(x[:, k, :], x[:, k, :], params[:, G_OUT + k:G_OUT + k + 1]).then_inc(xs, 1)
            n.past(RESCALE)
            norm(G_PRE2)

            dve.wait_ge(acts, 1)
            g4 = bank[2][:, 0:TT * 56].rearrange("p (t c) -> p t c", t=TT)
            dve.tensor_tensor(ifp[:, :, :], g4[:, :, 48:56],
                              params[:, C_GATEB:C_GATEB + 8].unsqueeze(1).to_broadcast([P, TT, 8]),
                              ALU.add).then_inc(free[2], 1)
            dve.wait_ge(free[2], n.at("free2", 1))
            dve.tensor_scalar(lf[:, 0, :, :], ifp[:, :, 4:8], 0.0, None, ALU.min).then_inc(dves, 1)
            dve.wait_ge(dves, n.at("dve", 1))
            dve.wait_ge(acts, 4)
            dve.tensor_tensor(lf[:, 1, :, :], lf[:, 0, :, :], lf[:, 3, :, :], ALU.subtract).then_inc(dves, 1)
            dve.tensor_tensor(lf[:, 2, :, :], lf[:, 3, :, :], lf[:, 0, :, :], ALU.subtract).then_inc(dves, 1)
            dve.wait_ge(turned, n.at("turned", 1))
            dve.tensor_copy(rows[0:4, 0, :], bank[6][0:4, :]).then_inc(free[6], 1)
            dve.wait_ge(free[6], n.at("free6", 1))
            dve.tensor_tensor_scan(rows[0:4, 1, :], rows[0:4, 0, :], rows[0:4, 0, :], 0.0, ALU.max,
                                   ALU.max).then_inc(dves, 1)
            dve.wait_ge(dves, n.at("dve", 4))
            dve.wait_ge(stats, n.at("stats", 1))
            dve.tensor_tensor(rows[0:4, 2, :], bank[3][0:4, :], rows[0:4, 1, :], ALU.add).then_inc(free[3], 1)
            dve.wait_ge(stats, n.at("stats", 2))
            dve.tensor_copy(acol[:, :, :], bank[3][:, 0:16].rearrange("p (t h) -> p h t", t=TT)).then_inc(free[3], 1)
            n.past(GATES)
            dve.wait_ge(gates_made, 1)
            dve.tensor_copy(kvc[:, GROUPS, 0:CMP_L], params[:, C_PE:C_PE + CMP_L]).then_inc(dves, 1)
            dve.memset(vb_all, 0.0)
            dve.memset(hidv, 0.0).then_inc(dves, 1)
            dve.wait_ge(dves, n.at("dve", 2))
            dve.wait_ge(turned, n.at("turned", 2))
            for a in range(4):
                rows_a, at = slice(32 * a, 32 * a + 32), a // 2 * P + 64 * (a % 2)
                last = dve.tensor_copy(vb_all[rows_a, :, at:at + 64],
                                       bank[6][rows_a, 0:GROUPS * 64].rearrange("p (g b) -> p g b", g=GROUPS))
            last.then_inc(free[6], 1)
            n.past(CMP)

            with n.turns(dve, GROUPS, NSA):
                dve.wait_ge(heads, n.at("heads", 1))
                for s in range(TT + 1):
                    if s < TT:
                        c4 = sc[:, s % 2, 0:P].rearrange("p (a b) -> p a b", a=4)[:, :, 0:CMP_N]
                        add = tables[:, K_CADD + s * CMP_N:K_CADD + (s + 1) * CMP_N]
                        for odd in range(2):
                            dve.wait_ge(scores, n.at("scores", 2 * s + odd + 1))
                            dve.tensor_tensor(c4[:, odd::2, :],
                                              bank[4 + odd][:, 0:64].rearrange("p (a b) -> p a b", a=2)[:, :, 0:CMP_N],
                                              add.unsqueeze(1).to_broadcast([P, 2, CMP_N]),
                                              ALU.add).then_inc(free[4 + odd], 1)
                        dve.wait_ge(free[5], n.at("free5", s + 1))
                        dve.tensor_reduce(cmx, c4, AX.X, ALU.max).then_inc(dves, 1)
                        dve.wait_ge(dves, n.at("dve", 5 * s + 1))
                        dve.tensor_tensor(c4, c4, cmx.unsqueeze(2).to_broadcast([P, 4, CMP_N]),
                                          ALU.subtract).then_inc(cmps, 1)
                        e4 = ex[:, s % 2, 0:P].rearrange("p (a b) -> p a b", a=4)[:, :, 0:CMP_N]
                        mul = tables[:, K_CMUL + s * CMP_N:K_CMUL + (s + 1) * CMP_N]
                        dve.wait_ge(exps, n.at("exps", s + 1))
                        dve.tensor_reduce(csum, e4, AX.X, ALU.add).then_inc(dves, 1)
                        dve.wait_ge(dves, n.at("dve", 5 * s + 2))
                        dve.reciprocal(cgate, csum).then_inc(dves, 1)
                        dve.wait_ge(dves, n.at("dve", 5 * s + 3))
                        dve.tensor_tensor(cgate, cgate, ggate[:, s, 0::3], ALU.mult).then_inc(dves, 1)
                        dve.tensor_tensor(e4, e4, mul.unsqueeze(1).to_broadcast([P, 4, CMP_N]),
                                          ALU.mult).then_inc(dves, 1)
                        dve.wait_ge(dves, n.at("dve", 5 * s + 5))
                        if s >= 1:
                            dve.wait_ge(turned, n.at("turned", s))
                        dve.tensor_tensor(pc[:, :, 0:CMP_N], e4, cgate.unsqueeze(2).to_broadcast([P, 4, CMP_N]),
                                          ALU.mult).then_inc(probs, 1)
                for s in range(NJ + 1):
                    if s < NJ:
                        width = (s % 4 + 1) * P
                        masked_scores(s, width, tables[:, K_CAUS + T - width:K_CAUS + T], 4, 8)
                    if s >= 1:
                        a = s - 1
                        head, br, row = a // 8, a // 4 % 2, a % 4
                        normalise(a, (row + 1) * P, ggate[:, row, head * 3 + 1 + br:head * 3 + 2 + br], 20, 4)
            n.past(SPREAD)

            dve.wait_ge(turned, n.at("turned"))
            dve.memset(xp[:, :, 0:3], 0.0).then_inc(pads, 1)
            with n.turns(dve, HEADS, ML) as i:
                dve.wait_ge(heads, n.at("heads", 1))
                for c in range(2):
                    dve.wait_ge(free[c], n.at(f"free{c}", 1))
                    y = o_sb[:, c, :]
                    for tap in range(4):
                        w = hp[:, 4 * c + tap:4 * c + tap + 1]
                        if tap == 0:
                            dve.tensor_scalar(y, xp[:, c, 0:T], w, None, ALU.mult).then_inc(dves, 1)
                        else:
                            dve.wait_ge(dves, n.at("dve", 4 * c + tap))
                            dve.scalar_tensor_tensor(y, xp[:, c, tap:tap + T], w, y, ALU.mult, ALU.add).then_inc(dves, 1)
                for j in range(TT):
                    w = T - j * P
                    dve.scalar_tensor_tensor(hid[:, 18 + j, 0:w], negM[:, bass.ds(i, 1), j * P:T].rearrange("p a t -> p (a t)"),
                                             hp[:, 12 + j:13 + j], tables[:, K_CAUST:K_CAUST + w],
                                             ALU.add, ALU.add).then_inc(dves, 1)
                for j in range(TT):
                    b, w = 4 + j % 2, T - j * P
                    dve.wait_ge(exps, n.at("exps", j + 1))
                    dve.wait_ge(scores, n.at("scores", j + 1))
                    dve.scalar_tensor_tensor(PT[:, j, j * P:T], bank[b][:, 0:w], P ** -0.5, hid[:, 18 + j, 0:w],
                                             ALU.mult, ALU.mult).then_inc(free[b], 1)
                dve.wait_ge(free[6], n.at("free6", 1))
                dve.tensor_tensor(var[:, :], var[:, :], tile(emb, i), ALU.max).then_inc(dves, 1)
                dve.wait_ge(dves, n.at("dve", 13))
                dve.reciprocal(var[:, :], var[:, :]).then_inc(dves, 1)
                dve.wait_ge(dves, n.at("dve", 14))
                dve.wait_ge(outs, n.at("outs", 1))
                dve.tensor_tensor(o_sb[:, 0, :], bank[7][:, :], var[:, :], ALU.mult).then_inc(free[7], 1)
                reciprocal_mean(0, 0, 1.0 / P, EPS)
                scaled(o_sb[:, 1, :], o_sb[:, 0, :], hp[:, 10:11]).then_inc(dves, 1)
                dve.wait_ge(dves, n.at("dve", 15))
                dve.wait_ge(free[0], n.at("free0", 2))
                dve.tensor_tensor(tile(hid, i + 8), o_sb[:, 1, :], silu[:, 0, :], ALU.mult).then_inc(cats, 1)

            with n.turns(dve, HEADS, MEM2):
                for s in range(TT + 1):
                    if s < TT:
                        masked_scores(s, M, no_mask)
                    if s >= 1:
                        normalise(s - 1, M)

            with n.turns(dve, KD, MERGE) as i:
                for j in range(3):
                    dve.wait_ge(free[0], n.at("free0", j + 1))
                    dve.wait_ge(products, n.at("products", 2 * j + 2))
                    dve.tensor_tensor(ex[:, j, :], silu[:, j, :], bank[1][:, :], ALU.mult).then_inc(free[1], 1)
                    if j == 1:
                        dve.wait_ge(free[1], n.at("free1", 2))
                        dve.tensor_tensor(sc[:, 0, :], ex[:, 0, :], ex[:, 1, :], ALU.add).then_inc(dves, 1)
                dve.wait_ge(free[1], n.at("free1", 3))
                dve.wait_ge(dves, n.at("dve", 1))
                dve.tensor_tensor(tile(big8, i), sc[:, 0, :], ex[:, 2, :], ALU.add).then_inc(dves, 1)

            def add_z(z, g, events):
                reciprocal_mean(0, 0, 1.0 / D, EPS)
                for k in range(KD + 1):
                    if k < KD:
                        scaled(z[:, k, :], z[:, k, :], params[:, g + k:g + k + 1]).then_inc(dves, 1)
                    if k >= 1:
                        dve.wait_ge(dves, n.at("dve", k))
                        dve.tensor_tensor(x[:, k - 1, :], x[:, k - 1, :], z[:, k - 1, :], ALU.add).then_inc(xs, 1)
                n.past(events)

            n.past(CLEAR)
            n.past(OUT_Z, 2)
            add_z(hid, G_POST2, ADD_Z)
            norm(G_PREF2)
            ffn_up()
            n.past(CLEAR)
            n.past(FFN_DOWN_Z, 4)
            add_z(big8, G_POSTF2, ADD_Z_LAST)


TOTAL = {"xs": 1 + 2 * 8 + 2 * 8 + 8 + 8 + 8}


def _panels(np_, w, cols, k0=0, k1=None):
    w = w[k0:k1]
    a = w.reshape(w.shape[0] // P, P, w.shape[1])
    return [np_.ascontiguousarray(a[:, :, c].transpose(1, 0, 2)) for c in cols]


def _tables():
    r = np.arange(P)
    con = np.zeros((P, K_BASE), np.float32)
    con[:, K_ID:K_ID + P] = np.eye(P)
    con[:, K_ONE:K_ONE + P] = 1
    con[:, K_BLK:K_BLK + P] = (r[:, None] // 64 == r[None, :] // 64)
    tab = np.zeros((P, NTAB), np.float32)
    tab[:, K_CAUS + T - P:K_CAUS + T] = np.where(r[None, :] <= r[:, None], 0, NEG)
    tab[:, K_CAUST:K_CAUST + P] = np.where(r[None, :] >= r[:, None], 0, NEG)
    c = np.arange(T)
    tab[:, K_CUM:K_CUM + T] = c[None, :] >= r[:, None]
    for t in range(TT):
        ok = (np.arange(CMP_N)[None, :] * CMP_S + CMP_L - 1) <= (t * P + r)[:, None]
        tab[:, K_CADD + t * CMP_N:K_CADD + (t + 1) * CMP_N] = np.where(ok, 0, NEG)
        tab[:, K_CMUL + t * CMP_N:K_CMUL + (t + 1) * CMP_N] = ok
    headtab = np.zeros((2 * HEADS, P, T), np.float32)
    for hd in range(HEADS):
        gamma = np.log1p(-2.0 ** (-5.0 - hd))
        rel = c[None, :] - r[:, None]
        headtab[hd] = np.where(rel >= 0, np.exp(gamma * np.maximum(rel, 0)), 0) * P ** -0.5
        slope = 2.0 ** (-8.0 * (hd + 1) / HEADS)
        dist = r[:, None] - (c[None, :] - (T - P))
        headtab[HEADS + hd] = np.where(dist >= 0, -slope * dist, NEG)
    return con, tab, headtab


def kernel(**inputs):
    import numpy as _np
    import concourse.bacc as _bacc
    from concourse import mybir as _mybir
    from concourse.bass_utils import run_bass_kernel_spmd as _run

    I = {k: _np.asarray(v) for k, v in inputs.items()}

    def W(name):
        return I[name][0]

    def cols(start, width=P):
        return slice(start, start + width)

    def two(a, b, width=64):
        return _np.r_[a:a + width, b:b + width]

    w8, w6, w4 = [], [], []

    def ffn(w1, w3, w2, off3=0):
        for f in range(KF):
            w8.extend(_panels(_np, w1, [cols(f * P)]))
            w8.extend(_panels(_np, w3, [cols(off3 + f * P)]))
        for m in range(KD):
            k0 = 0
            for k in DOWN:
                {8: w8, 6: w6}[k].extend(_panels(_np, w2, [cols(m * P)], k0 * P, (k0 + k) * P))
                k0 += k

    ffn(W("ffn1_w1"), W("ffn1_w3"), W("ffn1_w2"))
    win = W("w_in")
    for hd in range(HEADS):
        w8.extend(_panels(_np, win, [cols(b * 512 + hd * P) for b in range(4)]))
    for hd in range(HEADS):
        w8.extend(_panels(_np, win, [cols(2048 + b * 512 + hd * P) for b in range(3)]))
    w8.extend(_panels(_np, W("w_out"), [cols(m * P) for m in range(KD)]))
    for hd in range(HEADS):
        w8.extend(_panels(_np, W("mem_w_kv"), [cols(b * D + hd * M + c * P) for b in range(2) for c in range(2)]))
        w8.extend(_panels(_np, W("mem_w_q"), [cols(hd * M + c * P) for c in range(2)]))
    w8.extend(_panels(_np, W("mem_w_o"), [cols(m * P) for m in range(KD)]))
    ffn(W("ffn2_w1"), W("ffn2_w3"), W("ffn2_w2"))
    win = W("w_in_2")
    kv0 = 1024

    def kv(b, g):
        return kv0 + b * 256 + g * 64

    w8.extend(_panels(_np, win, [two(kv(0, g), kv(1, g)) for g in range(GROUPS)]))
    for g in range(GROUPS):
        w8.extend(_panels(_np, win, [cols(g * 256), cols(g * 256 + P), two(kv(2, g), kv(4, g)),
                                     two(kv(3, g), kv(5, g))]))
    ml0 = 1024 + 1536 + 48
    if0 = ml0 + 1536
    o0 = if0 + 8
    mq0 = o0 + 512
    gm0 = mq0 + 512
    for hd in range(HEADS):
        w8.extend(_panels(_np, win, [cols(ml0 + hd * P), cols(ml0 + 512 + hd * P), cols(o0 + hd * P),
                                     cols(ml0 + 1024 + hd * P)]))
    mkv = W("w_mem_kv_2")
    for hd in range(HEADS):
        w8.extend(_panels(_np, win, [cols(mq0 + hd * P)]))
        w8.extend(_panels(_np, mkv, [cols(hd * P), cols(512 + hd * P)]))
    for m in range(KD):
        w8.extend(_panels(_np, win, [cols(gm0 + m * P)]))
        w8.extend(_panels(_np, W("w_proj_nsa_2"), [cols(m * P)]))
        w8.extend(_panels(_np, win, [cols(gm0 + D + m * P)]))
        w4.extend(_panels(_np, W("w_proj_ml_2"), [cols(m * P)]))
        w8.extend(_panels(_np, win, [cols(gm0 + 2 * D + m * P)]))
        w4.extend(_panels(_np, W("w_proj_mem_2"), [cols(m * P)]))
    w8.extend(_panels(_np, W("w_out_2"), [cols(m * P) for m in range(KD)]))
    ffn(W("w_ffn_in_2"), W("w_ffn_in_2"), W("w_ffn_down_2"), FF)

    gatew = _np.concatenate([win[:, 2560:2608], win[:, if0:if0 + 8]], 1).reshape(KD, P, 56).transpose(1, 0, 2)
    cw1 = _np.concatenate([W("cmp_w1_k_2").transpose(1, 0, 2), W("cmp_w1_v_2").transpose(1, 0, 2)], 0)
    cw2 = _np.concatenate([W("cmp_w2_k_2"), W("cmp_w2_k_2"), W("cmp_w2_v_2")], 1)

    par = [W(k).reshape(KD, P).T for k in ("norm_ffn1", "norm_mix", "norm_mem_q", "norm_mem_kv", "norm_ffn2",
                                           "norm_out", "g_pre_mix_2", "g_mem_2", "g_post_mix_2", "g_pre_ffn_2",
                                           "g_post_ffn_2")]
    twice = lambda v: _np.concatenate([v, v])[:, None]
    par += [W("ret_norm")[:, None], twice(W("diff_q_norm")), twice(W("diff_k_norm")), W("diff_norm")[:, None],
            W("mem_q_norm").reshape(2, P).T, W("mem_k_norm").reshape(2, P).T,
            twice(W("lambda_q1")), twice(W("lambda_q2")), twice(W("lambda_k1")), twice(W("lambda_k2"))]
    cw, cb, hg = W("ml_conv_w_2"), W("ml_conv_b_2"), W("ml_head_g_2")
    for hd in range(HEADS):
        a, b = hd * P, 512 + hd * P
        par += [cw[:, a:a + P].T, cw[:, b:b + P].T, cb[a:a + P, None], cb[b:b + P, None], hg[a:a + P, None]]
    par += [_np.repeat(W("ml_gate_b_2")[None, :], P, 0),
            _np.concatenate([W("cmp_pe_k_2").T, W("cmp_pe_v_2").T], 0)]
    con, tab, headtab = _tables()

    arrays = {
        "xT": I["x"][0].T.reshape(KD, P, T).transpose(1, 0, 2),
        "memT": I["mem"][0].T.reshape(KD, P, M).transpose(1, 0, 2),
        "mem2T": I["mem_2"][0].T.reshape(KD, P, M).transpose(1, 0, 2),
        "par": _np.concatenate(par, 1), "con": con, "tab": tab, "headtab": headtab,
        "w8": _np.stack(w8), "w6": _np.stack(w6), "w4": _np.stack(w4),
        "gatew": gatew, "cmpw1": cw1, "cmpw2": cw2,
    }
    arrays = {k: _np.ascontiguousarray(v) for k, v in arrays.items()}
    nc = _bacc.Bacc("TRN2", target_bir_lowering=False, num_devices=1)
    args = [nc.dram_tensor(k, a.shape, _mybir.dt.from_np(a.dtype), kind="ExternalInput").ap() for k, a in arrays.items()]
    args.append(nc.dram_tensor("outT", (KD, P, T), _mybir.dt.float32, kind="ExternalOutput").ap())
    build(nc, *args)
    r = _run(nc, [arrays], core_ids=[0])
    return _np.ascontiguousarray(r.results[0]["outT"].reshape(D, T).T)[None]
```

```python
from contextlib import ExitStack, contextmanager

import numpy as np

import concourse.bass as bass
from concourse import mybir

F32 = mybir.dt.float32
F32R = mybir.dt.float32r
ACT = mybir.ActivationFunctionType
ALU = mybir.AluOpType
AX = mybir.AxisListType

P = 128
D = 1024
T = 512
M = 256
KD = D // P
TT = T // P
MT = M // P
FF = 2816
KF = FF // P
EPS = 1e-6
NEG = -1e30
HEADS = 4
CMP_L, CMP_S, CMP_N = 32, 16, 31
GATE_COLS = 56
GROUPS = 4
LAM_INIT = 0.2
SLOTS = 6
RING = 4
CHUNKS = (4, 7, 4, 7)

G_FFN1, G_MIX, G_MEMQ, G_MEMKV, G_FFN2, G_OUT, G_PRE2, G_MEM2, G_POST2, G_PREF2, G_POSTF2 = range(0, 88, 8)
C_RET, C_DQ, C_DK, C_DN = 88, 89, 90, 91
C_MQ, C_MK = 92, 94
C_LAM = 96
C_HEAD = 100
C_HEADN = 11
C_GATEB = C_HEAD + HEADS * C_HEADN
C_PE = C_GATEB + 8
NPAR = C_PE + CMP_L

K_ID, K_ONE, K_BLK = 0, 128, 256
K_BASE = 384
K_CAUS = 0
K_CAUST = 512
K_CUM = 1024
K_CADD = 1536
K_CMUL = K_CADD + TT * CMP_N
NTAB = K_CMUL + TT * CMP_N

NORM = dict(stats=1, free3=1, rcp=1, rinv=1, h32s=KD, hhis=KD, hlos=KD)
SQUARES = dict(squares=KD, sums=KD, cleared=1)
CLEAR = dict(cleared=1)
RESCALE = dict(stats=1, free3=1, rcp=1, rinv=1, xs=KD, squares=KD, sums=KD, cleared=1)
FFN_UP = dict(products=4, splits=4, highs=4, free0=2, free1=2)
DOWN = len(CHUNKS) * KD
FFN_DOWN = dict(products=DOWN, splits=DOWN, highs=DOWN, hhis=KF, hlos=KF, squares=KD, sums=KD,
                **{f"free{b}": 1 for b in range(8)})
OUT_X = dict(products=8, splits=8, highs=8, hhis=KD, hlos=KD, xs=8, squares=8, sums=8)
OUT_Z = dict(products=8, splits=8, highs=8, hhis=KD, hlos=KD, free0=4, free1=4, squares=8, sums=8)
ADD_Z = dict(stats=1, free3=1, rcp=1, rinv=1, dve=KD, xs=KD, squares=KD, sums=KD, cleared=1)
ADD_Z_LAST = dict(stats=1, free3=1, rcp=1, rinv=1, dve=KD, xs=KD)
MEM_NORM = dict(stats=1, free3=1, rcp=1, rinv=1, mems=1)
RET = dict(products=4, splits=4, highs=4, free0=2, free1=1, free2=1, strips=1, scores=4, free4=2, free5=2, outs=1, free7=1,
           stats=2, free3=2, sqs=1, rcp=1, rinv=1, dve=1, cats=1)
LAM = dict(stats=1, free3=1, dve=3)
DIFF = dict(products=3, splits=3, highs=3, free0=1, free1=1, free2=1, strips=1, stats=3, free3=3, sqs=3, rcp=3, rinv=3,
            scores=8, free4=4, free5=4, negmax=8, exps=8, dve=16, probs=4, turned=4, free6=4,
            outs=1, free7=1, cats=1)
MEM1 = dict(products=6, splits=2, highs=2, free0=2, free1=1, free2=1, stats=2, free3=2, sqs=2, rcp=2, rinv=2,
            scores=4, free4=2, free5=2, negmax=4, exps=4, dve=4, probs=4, turned=4, free6=4,
            outs=2, free7=2)
NJ = 32
CMP = dict(products=4, splits=4, highs=4, free0=2, free1=2, dve=2, acts=2, stats=2, free3=2, turned=2, free6=2)
NSA = dict(products=4, splits=4, highs=4, free0=1, free1=1, free2=1, free3=1, heads=1, twins=1,
           scores=8 + NJ, free4=4 + NJ // 2, free5=4 + NJ // 2, cmps=4, negmax=NJ, exps=4 + NJ,
           dve=20 + NJ, probs=4 + NJ, turned=4 + NJ, free6=4 + NJ, outs=2, free7=2)
GATES = dict(outs=1, free7=1, gates=1, acts=5, free2=1, dve=4, stats=2, free3=2, turned=1, free6=1)
SPREAD = dict(scores=8, free4=4, free5=4)
ML = dict(products=4, splits=4, highs=4, free0=2, free1=1, free2=1, heads=1, dve=15, convs=2, exps=4, scores=4, free4=2,
          free5=2, outs=1, turned=1, free6=1, free7=1, sqs=1, stats=1, free3=1, rcp=1, rinv=1, cats=1)
MEM2 = dict(products=3, splits=1, highs=1, free0=1, free1=1, free2=1, scores=4, free4=2, free5=2, negmax=4, exps=4,
            dve=4, probs=4, turned=4, free6=4, outs=1, free7=1)
MERGE = dict(products=6, splits=3, highs=3, free0=3, free1=3, dve=2)

STREAM = [
    (KF // 2, FFN_UP, [8] * 4), (1, FFN_DOWN, [k for k in CHUNKS for _ in range(KD)]),
    (HEADS, RET, [8] * 4), (HEADS, DIFF, [8] * 3), (1, OUT_X, [8] * 8),
    (HEADS, MEM1, [8] * 6), (1, OUT_X, [8] * 8),
    (KF // 2, FFN_UP, [8] * 4), (1, FFN_DOWN, [k for k in CHUNKS for _ in range(KD)]),
    (1, CMP, [8] * 4), (GROUPS, NSA, [8] * 4), (HEADS, ML, [8] * 4), (HEADS, MEM2, [8] * 3),
    (KD, MERGE, [8, 8, 8, 4, 8, 4]), (1, OUT_Z, [8] * 8),
    (KF // 2, FFN_UP, [8] * 4), (1, FFN_DOWN, [k for k in CHUNKS for _ in range(KD)]),
]


def slots_used(panels):
    return panels if panels <= SLOTS else RING


def slot_loads(events):
    panels = events.get("products", 0)
    return [(s, panels // slots_used(panels)) for s in range(slots_used(panels))] if panels else []


class Counts:

    def __init__(self):
        self.base = {**{f"free{b}": 1 for b in range(8)}, "cats": 1, "xs": 1}
        self.turn, self.events = None, {}

    def at(self, name, more=0):
        value = self.base.get(name, 0) + more
        if self.turn is not None and self.events.get(name, 0):
            value = self.turn * self.events[name] + value
        return value

    def past(self, events, turns=1):
        for name, k in events.items():
            self.base[name] = self.base.get(name, 0) + k * turns
        for slot, k in slot_loads(events):
            self.base[f"loads{slot}"] = self.base.get(f"loads{slot}", 0) + k * turns

    @contextmanager
    def turns(self, engine, turns, events):
        with engine.Fori(0, turns) as i:
            self.turn = i
            self.events = {**events, **{f"loads{s}": k for s, k in slot_loads(events)}}
            yield i
        self.turn, self.events = None, {}
        self.past(events, turns)


def build(nc, xT, memT, mem2T, par, con, tab, headtab, w8, w7, w4, gatew, cmpw1, cmpw2, outT):
    with ExitStack() as ctx:
        def sb(name, *shape):
            return ctx.enter_context(nc.sbuf_tensor(name, [P, *shape], F32))

        def sbr(name, *shape):
            return ctx.enter_context(nc.sbuf_tensor(name, [P, *shape], F32R))

        def sem(name):
            return ctx.enter_context(nc.semaphore(name))

        bank = [ctx.enter_context(nc.psum_tensor(f"bank{b}", [P, 512], F32)) for b in range(8)]

        x = sb("x", KD, T)
        hhi, hlo = sbr("hhi", KD, T), sbr("hlo", KD, T)
        hid = sb("hid", KF, T)
        with nc.sbuf_tensor("bigr", [P, KD, T], F32R) as bigr:
            pass
        big = sb("big", KD * T)
        memh = sb("memh", KD, M)
        slot = [sb(f"slot{s}", KD, P) for s in range(RING)]
        slot += [hid[:, t:t + 2, :].rearrange("p a (b c) -> p (a b) c", c=P) for t in (16, 20)]
        parts = [sbr(f"parts{s}", 2, KD, P) for s in range(2)]
        params = sb("params", NPAR)
        consts = sb("consts", K_BASE)
        tables = sb("tables", NTAB)
        gate_w = sb("gate_w", KD, GATE_COLS)
        w2 = sb("w2", P + 64)
        ssum = sb("ssum", T)
        var = sb("var", T)
        rinv = sb("rinv", T)
        silu = sb("silu", 3, T)
        qs = sb("qs", 2, T)
        ks = sb("ks", 2, T)
        vs = sb("vs", T)
        PT = sb("PT", TT, T)
        sc = sb("sc", 2, T)
        ex = sb("ex", 3, T)
        lanes = sb("lanes", 64)
        hp = sb("hp", 16)
        gates = sb("gates", TT, 48)
        ggate = sb("ggate", TT, 12)
        ifp = sb("ifp", TT, 8)
        lf = sb("lf", 4, TT, 4)
        acol = sb("acol", HEADS, TT)
        kc2 = sb("kc2", CMP_N)
        vb = sb("vb", 2, P)
        pc = sb("pc", 4, 32)
        o_sb = sb("o_sb", 2, T)

        big8 = big[:, :].rearrange("p (k t) -> p k t", k=KD)
        stores = [(bigr[:, 0:4, :], bigr[:, 4:8, :]), (hhi, hlo)]
        w1c = big[:, :].rearrange("p (l h) -> p l h", l=CMP_L)
        sq = sc
        xp = ex[:, :, :].rearrange("p a t -> p (a t)")[:, 0:2 * (T + 3)].rearrange("p (c t) -> p c t", c=2)
        h32 = hid[:, 8:16, :]
        strip = hid[:, 19, :]
        sqh = silu[:, 1:3, :]
        PTc = o_sb[:, 1, :]
        exs = [ex[:, 0, :], ex[:, 1, :], ex[:, 2, :], o_sb[:, 0, :]]
        kvc = hid[:, 8:13, :]
        kc_all = hid[:, 15, 0:GROUPS * CMP_N]
        hidk = hid[:, 13, 0:GROUPS * CMP_N]
        hidv = hid[:, 14, :].rearrange("p (g a b) -> p g a b", g=GROUPS, a=4)
        gate_rows = hid[0:GATE_COLS, 17, :]
        vb_all = hid[:, 16:18, :].rearrange("p a (b c) -> p (a b) c", c=2 * P)
        rows = hid[:, 18:22, :]
        negM, emb = big8[:, 0:HEADS, :], big8[:, HEADS:2 * HEADS, :]
        ident, ones, blocks64 = consts[:, K_ID:K_ID + P], consts[:, K_ONE:K_ONE + P], consts[:, K_BLK:K_BLK + P]
        negmax, esum = lanes[:, 0:2], lanes[:, 4:8]
        nlam, dn_gain, rsm = lanes[:, 8:9], lanes[:, 9:10], lanes[:, 10:14]
        pebias = lanes[:, 14:16]
        le = lanes[:, 16:18]
        lprod = lanes[:, 18:20]
        maxs = lanes[:, 20:22]
        nought = lanes[:, 53:54]
        cmx, csum, cgate = lanes[:, 24:28], lanes[:, 28:32], lanes[:, 32:36]

        x_loaded = sem("x_loaded")
        params_loaded = sem("params_loaded")
        consts_loaded = sem("consts_loaded")
        tables_loaded = sem("tables_loaded")
        mem_loaded = sem("mem_loaded")
        cmp_loaded = sem("cmp_loaded")
        loaded = [sem(f"slot{s}_loaded") for s in range(SLOTS)]
        strips = sem("head_strip_loaded")
        twins = sem("key_twins_copied")
        stored = sem("stored")
        free = [sem(f"bank{b}_free") for b in range(8)]
        products = sem("panel_products")
        stats = sem("sums_over_partitions")
        scores = sem("scores_made")
        turned = sem("probs_turned")
        outs = sem("attention_out")
        gates_made = sem("gates_made")
        rcp = sem("reciprocal_mean_square")
        h32s = sem("h_tiles")
        hlos = sem("h_low_parts")
        xs = sem("x_tiles")
        negmaxs = sem("negated_maxima")
        probs = sem("probabilities")
        cmps = sem("shifted_compressed_scores")
        cats = sem("head_outputs")
        mems = sem("memory_normed")
        pads = sem("padding_zeroed")
        dves = sem("vector_steps")
        rinvs = sem("inverse_rms")
        squares = sem("squares")
        sqs = sem("head_squares")
        hhis = sem("h_high_parts")
        exps = sem("exponentials")
        convs = sem("conv_silus")
        acts = sem("scalar_steps")
        sums = sem("square_sums")
        cleared = sem("sum_cleared")
        highs = sem("panel_high_parts")
        splits = sem("panels_split")
        heads = sem("head_tables")
        zeros_set = sem("zeros_set")

        block = ctx.enter_context(nc.Block())

        @block.sync
        def _(sp):
            n = Counts()
            panel = {8: 0, 7: 0, 4: 0}
            source = {8: w8, 7: w7, 4: w4}
            before = RING
            for phase, (turns, events, ktiles) in enumerate(STREAM):
                c = slots_used(len(ktiles))
                per = {k: ktiles.count(k) for k in set(ktiles)}
                first = 0
                if phase == 0:
                    for j in range(c):
                        sp.dma_start(slot[j][:, 0:8, :], w8[j]).then_inc(loaded[j], 16)
                    n.past(events)
                    panel[8] += c
                    first = 1
                with n.turns(sp, turns - first, events) as i:
                    for j, k in enumerate(ktiles):
                        s = j % c
                        sp.wait_ge(products, n.at("products", j + 1 - min(c, before)))
                        at = panel[k] + ktiles[:j].count(k) + i * per[k]
                        src = source[k][bass.ds(at, 1)].rearrange("a p k c -> p (a k) c")
                        sp.dma_start(slot[s][:, 0:k, :], src).then_inc(loaded[s], 16)
                for k in per:
                    panel[k] += per[k] * (turns - first)
                before = c
            n.past(ADD_Z_LAST)
            done = TOTAL["xs"] - KD
            for k in range(KD):
                sp.wait_ge(xs, done + k + 1)
                sp.dma_start(outT[k], x[:, k, :]).then_inc(stored, 16)
            sp.wait_ge(stored, 16 * KD)

        @block.gpsimd
        def _(pool):
            n = Counts()
            for z in (pc[:, :, :], nought):
                last = pool.memset(z, 0.0)
            last.then_inc(zeros_set, 1)

            def clear_sum(stat):
                pool.wait_ge(stats, n.at("stats", stat))
                pool.memset(ssum[:, :], 0.0).then_inc(cleared, 1)

            def add_square(k, parity, width=T):
                pool.wait_ge(squares, n.at("squares", k + 1))
                pool.wait_ge(sums, n.at("sums", k))
                pool.tensor_tensor(ssum[:, 0:width], ssum[:, 0:width], sq[:, parity, 0:width],
                                   ALU.add).then_inc(sums, 1)

            def sum_tiles(stat, width=T):
                clear_sum(stat)
                pool.wait_ge(cleared, n.at("cleared", 1))
                for k in range(KD):
                    add_square(k, k % 2, width)

            def split(nth, j, product=None, kt=KD):
                if product != "act":
                    pool.wait_ge(loaded[j], 16 * n.at(f"loads{j}", 1))
                    pool.wait_ge(products, n.at("products", product))
                w, (high, low) = slot[j][:, 0:kt, :], (parts[nth % 2][:, c, 0:kt, :] for c in range(2))
                if product != "act":
                    pool.tensor_tensor(high, w, nought.unsqueeze(2).to_broadcast([P, KD, P]), ALU.add).then_inc(highs, 1)
                pool.wait_ge(highs, n.at("highs", nth + 1))
                pool.tensor_tensor(low, w, high.bitcast(F32), ALU.subtract).then_inc(splits, 1)

            def split_turns(turns, events, panels, last=None, between=None):
                with n.turns(pool, turns, events) as i:
                    for nth, j in enumerate(panels):
                        split(nth, j, "act" if last is None else last[nth] if nth < 2 else panels[nth - 2] + 1)
                        if nth == 1 and between is not None:
                            between(i)

            def cleared_before_turns():
                clear_sum(0)
                n.past(CLEAR)
                pool.wait_ge(cleared, n.at("cleared"))

            def ffn(memory=False):
                if memory:
                    for j in range(4):
                        if j == 2:
                            sum_tiles(0, M)
                            n.past(SQUARES)
                        split(j, j, "act")
                    n.past(FFN_UP)
                split_turns(KF // 2 - memory, FFN_UP, range(4))
                if memory:
                    n.past(MEM_NORM)
                for q in range(DOWN):
                    if q == 2:
                        cleared_before_turns()
                    split(q, q % RING, "act", CHUNKS[q // KD])
                    if q >= DOWN - 6:
                        add_square(q - DOWN + 6, q % 2)
                for k in range(6, KD):
                    add_square(k, k % 2)
                n.past(FFN_DOWN)

            def out_product(events):
                cleared_before_turns()
                for q in range(KD):
                    split(q, q % RING, "act")
                    if q >= 2:
                        add_square(q - 2, q % 2)
                for k in range(KD - 2, KD):
                    add_square(k, k % 2)
                n.past(events)

            sum_tiles(0)
            n.past(SQUARES)
            n.past(NORM)
            ffn(True)
            n.past(NORM)
            split_turns(HEADS, RET, range(4), (-1, 0))
            n.past(LAM)
            split_turns(HEADS, DIFF, range(3), (0, 0))
            out_product(OUT_X)
            n.past(NORM)
            split_turns(HEADS, MEM1, (2, 3), (-3, -2))
            out_product(OUT_X)
            n.past(NORM)
            ffn(True)
            sum_tiles(1)
            n.past(RESCALE)
            n.past(NORM)
            n.past(GATES)
            for j in range(4):
                split(j, j, j - 1 if j >= 2 else 0)
            n.past(CMP)
            pool.wait_ge(free[3], n.at("free3"))
            pool.wait_ge(free[6], n.at("free6"))

            def group_gates(i):
                pool.wait_ge(outs, n.at("outs"))
                pool.wait_ge(probs, n.at("probs"))
                pool.wait_ge(acts, n.at("acts"))
                pool.tensor_copy(kc2[:, :], kc_all.rearrange("p (g b) -> p g b", g=GROUPS)[:, bass.ds(i, 1), :].rearrange("p a b -> p (a b)"))
                pool.tensor_copy(vb[:, :, :].rearrange("p a b -> p (a b)"),
                                 vb_all[:, bass.ds(i, 1), :].rearrange("p a b -> p (a b)"))
                pool.tensor_copy(ggate[:, :, :], gates[:, :, bass.ds(i * 12, 12)]).then_inc(heads, 1)

            split_turns(GROUPS, NSA, range(4), (-1, 0), group_gates)
            n.past(SPREAD)

            split_turns(HEADS, ML, range(4), (0, 0))
            with n.turns(pool, HEADS, MEM2):
                split(0, 0, -1)
            split_turns(KD, MERGE, (0, 2, 4))
            out_product(OUT_Z)
            sum_tiles(1)
            n.past(ADD_Z)
            n.past(NORM)
            ffn()

        @block.tensor
        def _(pe):
            n = Counts()

            def panel(j, out, moving, stationary_tokens=False, k0=0, ks_=KD, start=True, stop=True, load=1):
                pe.wait_ge(loaded[j], 16 * n.at(f"loads{j}", load))
                if stationary_tokens:
                    for t in range(moving.shape[2] // P):
                        for k in range(ks_):
                            mm = pe.matmul(out(t), moving[:, k, t * P:(t + 1) * P], slot[j][:, k, :],
                                           start=(k == 0), stop=(k == ks_ - 1))
                else:
                    for k in range(ks_):
                        mm = pe.matmul(out, slot[j][:, k, :], moving[:, k0 + k, :],
                                       start=(start and k == 0), stop=(stop and k == ks_ - 1))
                mm.then_inc(products, 1)

            def h_panel(nth, out, stationary_tokens=False, ready=None, between=None, moving=(hhi, hlo),
                        kt=KD, start=True, stop=True):
                high, low = (parts[nth % 2][:, c, :, :] for c in range(2))
                mhi, mlo = moving
                pe.wait_ge(splits, n.at("splits", nth + 1))
                if stationary_tokens:
                    for t in range(TT):
                        tokens = slice(t * P, (t + 1) * P)
                        if t >= 1 and between is not None:
                            between(t)
                        for k in range(KD):
                            pe.matmul(out(t), mhi[:, k, tokens], high[:, k, :], start=(k == 0), stop=False)
                            pe.matmul(out(t), mhi[:, k, tokens], low[:, k, :], start=False, stop=False)
                            mm = pe.matmul(out(t), mlo[:, k, tokens], high[:, k, :], start=False, stop=(k == KD - 1))
                else:
                    for k in range(kt):
                        if ready is not None:
                            pe.wait_ge(hhis, ready - kt + k + 1)
                        pe.matmul(out, high[:, k, :], mhi[:, k, :], start=(start and k == 0), stop=False)
                        pe.matmul(out, low[:, k, :], mhi[:, k, :], start=False, stop=False)
                    if between is not None:
                        between()
                    for k in range(kt):
                        if ready is not None:
                            pe.wait_ge(hlos, ready - kt + k + 1)
                        mm = pe.matmul(out, high[:, k, :], mlo[:, k, :], start=False, stop=(stop and k == kt - 1))
                mm.then_inc(products, 1)

            def emptied(b, more=0):
                pe.wait_ge(free[b], n.at(f"free{b}", more))

            def stat(k, matrix, *sources):
                emptied(3, k)
                width = sources[0].shape[1]
                for a, s in enumerate(sources):
                    mm = pe.matmul(bank[3][:, 0:width], matrix, s, start=(a == 0),
                                   stop=(a == len(sources) - 1))
                mm.then_inc(stats, 1)

            def norm(width=T):
                pe.wait_ge(sums, n.at("sums"))
                stat(0, ones, ssum[:, 0:width])

            def ffn(memory=False):
                h_done = n.at("hlos")
                if memory:
                    n.past(SQUARES)
                with n.turns(pe, KF // 2, FFN_UP):
                    for u in range(2):
                        emptied(0, u)
                        h_panel(2 * u, bank[0][:, :], ready=h_done if u == 0 else None)
                        emptied(1, u)
                        h_panel(2 * u + 1, bank[1][:, :])
                if memory:
                    norm(M)
                    n.past(MEM_NORM)
                for c, k in enumerate(CHUNKS):
                    for m in range(KD):
                        if c == 0:
                            emptied(m)
                        h_panel(c * KD + m, bank[m][:, :], ready=None if m else n.at("hlos", sum(CHUNKS[:c + 1])),
                                moving=stores[c % 2], kt=k, start=(c == 0), stop=(c == len(CHUNKS) - 1))
                n.past(FFN_DOWN)

            def out_product(events):
                for m in range(KD):
                    if "xs" in events and m >= 2:
                        pe.wait_ge(xs, n.at("xs", m - 1))
                    elif "xs" in events:
                        emptied(m)
                    else:
                        emptied(m % 2, m // 2)
                    h_panel(m, bank[m % 2][:, :], ready=None if m else n.at("hlos", KD))
                n.past(events)

            def scores_of(k, lhs, rhs, width):
                b = 4 + k % 2
                emptied(b, k // 2)
                for a in range(len(lhs)):
                    mm = pe.matmul(bank[b][:, 0:width], lhs[a], rhs[a], start=(a == 0), stop=(a == len(lhs) - 1))
                mm.then_inc(scores, 1)

            def turn_probs(k, tile, source, p):
                pe.wait_ge(probs, n.at("probs", p))
                emptied(6, k)
                for b in range(tile):
                    mm = pe.transpose(bank[6][:, b * P:(b + 1) * P], source[:, b * P:(b + 1) * P], ident)
                mm.then_inc(turned, 1)

            def causal_out(out, values, start=True):
                for j in range(TT):
                    mm = pe.matmul(out[:, j * P:T], values(j), PT[:, j, j * P:T], start=(start and j == 0),
                                   stop=(start and j == TT - 1), skip_group_check=not start)
                return mm

            def turns_with_tails(turns, events, turn, tails):
                for none in (True, False):
                    with n.turns(pe, 1 if none else turns - 1, events):
                        turn([None] * len(tails) if none else tails)
                for tail in tails:
                    tail()

            pe.wait_ge(consts_loaded, 16)
            n.past(SQUARES)
            norm()
            n.past(NORM)
            ffn(True)
            norm()
            n.past(NORM)

            h_done = n.at("hlos")

            def output_sum():
                emptied(7)
                stat(-2, ones, o_sb[:, 0, :])

            def centred_sum():
                pe.wait_ge(sqs, n.at("sqs"))
                stat(-1, ones, sqh[:, 0, :])

            def retention_turn(tails):
                emptied(0)
                h_panel(0, bank[0][:, :], ready=h_done, between=tails[0])
                emptied(1)
                h_panel(1, bank[1][:, :], between=tails[1])
                emptied(2)
                h_panel(2, lambda t: bank[2][:, t * P:(t + 1) * P], True)
                emptied(0, 1)
                h_panel(3, bank[0][:, :])
                emptied(1, 1)
                emptied(2, 1)
                emptied(7)
                for j in range(TT + 1):
                    if j < TT:
                        scores_of(j, [ks[:, 0, j * P:(j + 1) * P]], [qs[:, 0, j * P:T]], T - j * P)
                    if j >= 1:
                        emptied(4 + (j - 1) % 2, (j - 1) // 2 + 1)
                        mm = pe.matmul(bank[7][:, (j - 1) * P:T], vs[:, (j - 1) * P:j * P],
                                       PT[:, j - 1, (j - 1) * P:T], start=(j == 1), stop=(j == TT))
                mm.then_inc(outs, 1)

            turns_with_tails(HEADS, RET, retention_turn, (output_sum, centred_sum))

            pe.wait_ge(dves, n.at("dve", 1))
            emptied(3)
            pe.matmul(bank[3][:, 0:2], ones[0:64, :], lprod[0:64, :], start=True, stop=True).then_inc(stats, 1)
            n.past(LAM)

            def head_sum(c):
                def run(t=1):
                    if t == 1:
                        pe.wait_ge(sqs, n.at("sqs", c + 1))
                        stat(c, blocks64, sqh[:, c, :])
                return run

            with n.turns(pe, HEADS, DIFF):
                emptied(0)
                h_panel(0, bank[0][:, :])
                emptied(1)
                h_panel(1, bank[1][:, :], between=head_sum(0))
                emptied(2)
                h_panel(2, lambda t: bank[2][:, t * P:(t + 1) * P], True, between=head_sum(1))
                emptied(0, 1)
                emptied(1, 1)
                emptied(2, 1)
                for s in range(8 + 2):
                    if s < 8:
                        i, m = s // 2, s % 2
                        half = slice(64 * m, 64 * m + 64)
                        scores_of(s, [qs[half, 0, i * P:(i + 1) * P]], [ks[half, 0, 0:(i + 1) * P]], (i + 1) * P)
                    if s >= 2 and s % 2 == 1:
                        i = (s - 2) // 2
                        turn_probs(i, i + 1, o_sb[:, i % 2, :], i + 1)
                emptied(6, 4)
                emptied(7)
                causal_out(bank[7], lambda j: vs[:, j * P:(j + 1) * P]).then_inc(outs, 1)
                pe.wait_ge(sqs, n.at("sqs", 3))
                stat(2, ones, sqh[:, 0, :])
            out_product(OUT_X)
            norm()
            n.past(NORM)

            h_done = n.at("hlos")
            with n.turns(pe, HEADS, MEM1):
                pe.wait_ge(mems, n.at("mems"))
                emptied(0)
                for c in range(2):
                    panel(c, bank[0][:, c * M:(c + 1) * M], memh)

                def key_sum():
                    pe.wait_ge(sqs, n.at("sqs", 1))
                    stat(0, ones, sqh[:, 0, 0:M], sqh[:, 0, M:T])

                for c in range(2):
                    emptied(1 + c)
                    h_panel(c, bank[1 + c][:, :], ready=h_done, between=None if c else key_sum)
                emptied(0, 1)
                for c in range(2):
                    panel(4 + c, lambda t: bank[0][:, t * M + c * P:t * M + (c + 1) * P], memh, True)
                    if c == 0:
                        pe.wait_ge(sqs, n.at("sqs", 2))
                        stat(1, ones, sqh[:, 0, :], sqh[:, 1, :])
                for b in (1, 2, 0):
                    emptied(b, 2 if b == 0 else 1)
                for s in range(TT + 2):
                    if s < TT:
                        scores_of(s, [qs[:, c, s * P:(s + 1) * P] for c in range(2)],
                                  [ks[:, c, 0:M] for c in range(2)], M)
                    if s >= 2:
                        turn_probs(s - 2, MT, ex[:, (s - 2) % 3, :], s - 1)
                emptied(6, 4)
                for c in range(2):
                    emptied(7, c)
                    for j in range(MT):
                        mm = pe.matmul(bank[7][:, :], vs[:, j * M + c * P:j * M + (c + 1) * P], PT[:, j, :],
                                       start=(j == 0), stop=(j == MT - 1))
                    mm.then_inc(outs, 1)
            out_product(OUT_X)
            norm()
            n.past(NORM)
            ffn(True)
            norm()
            n.past(RESCALE)
            norm()
            n.past(NORM)

            def group_product(g):
                emptied(g % 2, g // 2)
                h_panel(g, bank[g % 2][:, :], ready=None if g else n.at("hlos"))

            pe.wait_ge(tables_loaded, 16)
            pe.wait_ge(params_loaded, 16)
            pe.wait_ge(cmp_loaded, 48)
            pe.wait_ge(h32s, n.at("h32s"))
            emptied(7)
            for k in range(KD):
                mm = pe.matmul(bank[7][0:GATE_COLS, :], gate_w[:, k, :], h32[:, k, :], start=(k == 0), stop=(k == KD - 1))
            mm.then_inc(outs, 1)
            group_product(0)
            emptied(7, 1)
            emptied(2)
            for t in range(TT):
                mm = pe.matmul(bank[2][:, t * GATE_COLS:(t + 1) * GATE_COLS], gate_rows[:, t * P:(t + 1) * P],
                               ident[0:GATE_COLS, 0:GATE_COLS], start=True, stop=True)
            mm.then_inc(gates_made, 1)
            group_product(1)
            pe.wait_ge(dves, n.at("dve", 3))
            emptied(3)
            for t in range(TT):
                mm = pe.matmul(bank[3][0:4, t * P:T], lf[:, 1, t, :], tables[:, K_CUM:K_CUM + T - t * P],
                               start=(t == 0), stop=(t == TT - 1))
            mm.then_inc(stats, 1)
            emptied(6)
            for t in range(TT):
                pe.matmul(bank[6][0:4, t * P:T], lf[:, 2, t, :], tables[:, K_CUM:K_CUM + T - t * P],
                          start=(t == 0), stop=False)
            for t in range(TT):
                mm = pe.matmul(bank[6][0:4, t * P:(t + 1) * P], ifp[:, t, 0:4], ident, start=False,
                               stop=(t == TT - 1))
            mm.then_inc(turned, 1)
            group_product(2)
            emptied(6, 1)
            emptied(3, 1)
            for t in range(TT):
                mm = pe.matmul(bank[3][:, 4 * t:4 * t + 4], rows[0:4, 0, t * P:(t + 1) * P], ident[0:4, 0:4],
                               start=True, stop=True)
            mm.then_inc(stats, 1)
            n.past(GATES)

            group_product(3)
            emptied(0, 2)
            emptied(1, 2)
            pe.wait_ge(dves, n.at("dve", 1))
            width = (GROUPS + 1) * CMP_N
            for row, b, done in ((slice(0, 64), 3, stats), (slice(64, P), 6, turned)):
                emptied(b)
                for l in range(CMP_L):
                    mm = pe.matmul(bank[b][:, 0:width].rearrange("p (g b) -> p g b", b=CMP_N), w1c[row, l, :],
                                   kvc[row, :, l:l + CMP_S * (CMP_N - 1) + 1:CMP_S],
                                   start=(l == 0), stop=(l == CMP_L - 1))
                mm.then_inc(done, 1)
            emptied(3, 1)
            pe.matmul(bank[3][:, 0:GROUPS * CMP_N], w2[:, 0:P], hidk, start=True, stop=True).then_inc(stats, 1)
            emptied(6, 1)
            for g in range(GROUPS):
                mm = pe.matmul(bank[6][:, 64 * g:64 * (g + 1)], hidv[:, g, :, :].rearrange("p a b -> p (a b)"),
                               w2[:, P:P + 64], start=True, stop=True)
            mm.then_inc(turned, 1)
            n.past(CMP)

            def compressed_scores(i):
                for odd in range(2):
                    half = slice(64 * odd, 64 * odd + 64)
                    emptied(4 + odd, i)
                    for p in range(2):
                        mm = pe.matmul(bank[4 + odd][:, p * 32:p * 32 + CMP_N], qs[half, p, i * P:(i + 1) * P],
                                       kc2[half, :], start=True, stop=True)
                    mm.then_inc(scores, 1)

            def turn_compressed(i):
                pe.wait_ge(probs, n.at("probs", i + 1))
                emptied(6, i)
                pe.transpose(bank[6][:, 0:P], pc[:, :, :].rearrange("p a b -> p (a b)"), ident).then_inc(turned, 1)

            def first_compressed():
                emptied(0, 1)
                emptied(1, 1)
                pe.wait_ge(heads, n.at("heads", 1))
                compressed_scores(0)

            def next_compressed(t):
                turn_compressed(t - 1)
                if t + 1 < TT:
                    compressed_scores(t + 1)

            with n.turns(pe, GROUPS, NSA):
                emptied(0)
                h_panel(0, bank[0][:, :])
                emptied(1)
                h_panel(1, bank[1][:, :])
                emptied(3)
                h_panel(2, bank[3][:, :], between=first_compressed)
                compressed_scores(1)
                emptied(2)
                h_panel(3, lambda t: bank[2][:, t * P:(t + 1) * P], True, between=next_compressed)
                emptied(3, 1)
                for s in range(NJ + 4):
                    if s == 1:
                        turn_compressed(TT - 1)
                    if s == 4:
                        pe.wait_ge(twins, 32 * n.at("twins", 1))
                    if s < NJ:
                        head, br, i = s // 8, s // 4 % 2, s % 4
                        half = slice(64 * (head % 2), 64 * (head % 2) + 64)
                        b = 4 + s % 2
                        emptied(b, 4 + s // 2)
                        pe.matmul(bank[b][:, 0:(i + 1) * P], qs[half, head // 2, i * P:(i + 1) * P],
                                  ks[half, br, 0:(i + 1) * P], start=True, stop=True).then_inc(scores, 1)
                    if s >= 4 and (s - 4) % 4 == 3:
                        head, br = (s - 4) // 8, (s - 4) // 4 % 2
                        emptied(6, 4 + s - 3)
                        if head % 2 == 0 and br == 0:
                            emptied(2, 1)
                            emptied(7, head // 2)
                            pe.matmul(bank[7][:, :], vb[:, head // 2, :], PTc, start=True, stop=True)
                        half = slice(64 * (head % 2), 64 * (head % 2) + 64)
                        mm = causal_out(bank[7][half, :], lambda j: vs[:, j * P + 64 * br:j * P + 64 * br + 64],
                                        start=False)
                        if head % 2 == 1 and br == 1:
                            mm.then_inc(outs, 1)
                    if 3 <= s < NJ + 3:
                        turn_probs(4 + s - 3, (s - 3) % 4 + 1, exs[(s - 3) % 4], 4 + s - 2)

            pe.wait_ge(dves, n.at("dve"))
            pe.wait_ge(acts, n.at("acts"))
            for s in range(8):
                scores_of(s, [ident[0:4, s % 4:s % 4 + 1].to_broadcast([4, P])],
                          [rows[0:4, 1 if s < 4 else 3, :]], T)
            n.past(SPREAD)

            def normed_sum():
                pe.wait_ge(sqs, n.at("sqs"))
                stat(-1, ones, sqh[:, 0, :])

            def mlstm_turn(tails):
                emptied(0)
                h_panel(0, bank[0][:, :])
                emptied(1)
                h_panel(1, bank[1][:, :], between=tails[0])
                emptied(2)
                h_panel(2, lambda t: bank[2][:, t * P:(t + 1) * P], True)
                emptied(0, 1)
                h_panel(3, bank[0][:, :])
                pe.wait_ge(convs, n.at("convs", 2))
                emptied(2, 1)
                emptied(7)
                emptied(6)
                for j in range(TT + 1):
                    if j < TT:
                        scores_of(j, [ks[:, 0, j * P:(j + 1) * P]], [qs[:, 0, j * P:T]], T - j * P)
                    if j >= 1:
                        a = j - 1
                        emptied(4 + a % 2, a // 2 + 1)
                        mm = pe.matmul(bank[7][:, a * P:T], vs[:, a * P:j * P], PT[:, a, a * P:T],
                                       start=(a == 0), stop=(j == TT))
                        if j == TT:
                            mm.then_inc(outs, 1)
                        mm = pe.matmul(bank[6][:, a * P:T], ones, PT[:, a, a * P:T],
                                       start=(a == 0), stop=(j == TT))
                mm.then_inc(turned, 1)

            turns_with_tails(HEADS, ML, mlstm_turn, (normed_sum,))

            pe.wait_ge(mems, n.at("mems"))
            with n.turns(pe, HEADS, MEM2):
                emptied(0)
                h_panel(0, bank[0][:, :])
                emptied(1)
                panel(1, bank[1][:, 0:M], memh)
                emptied(2)
                panel(2, lambda t: bank[2][:, t * P:(t + 1) * P], memh, True)
                emptied(0, 1)
                emptied(1, 1)
                emptied(2, 1)
                for s in range(TT + 2):
                    if s < TT:
                        scores_of(s, [qs[:, 0, s * P:(s + 1) * P]], [ks[:, 0, 0:M]], M)
                    if s >= 2:
                        turn_probs(s - 2, MT, ex[:, (s - 2) % 3, :], s - 1)
                emptied(6, 4)
                emptied(7)
                for j in range(MT):
                    mm = pe.matmul(bank[7][:, :], vs[:, j * P:(j + 1) * P], PT[:, j, :],
                                   start=(j == 0), stop=(j == MT - 1))
                mm.then_inc(outs, 1)

            branches_done = (n.at("cats"), n.at("free7"))
            with n.turns(pe, KD, MERGE):
                for j, (k0, kt) in enumerate(((0, 8), (8, 4), (12, 4))):
                    emptied(0, j)
                    h_panel(j, bank[0][:, :])
                    emptied(1, j)
                    pe.wait_ge(cats, branches_done[0])
                    pe.wait_ge(free[7], branches_done[1])
                    panel(2 * j + 1, bank[1][:, :], hid, k0=k0, ks_=kt)
            out_product(OUT_Z)
            norm()
            n.past(ADD_Z)
            norm()
            n.past(NORM)
            ffn()
            norm()
            n.past(ADD_Z_LAST)

        @block.scalar
        def _(act):
            n = Counts()
            act.dma_start(params[:, :], par).then_inc(params_loaded, 16)
            act.dma_start(x[:, :, :], xT).then_inc(x_loaded, 16)
            act.dma_start(consts[:, :], con).then_inc(consts_loaded, 16)
            act.dma_start(memh[:, :, :], memT).then_inc(mem_loaded, 16)
            act.dma_start(tables[:, :], tab).then_inc(tables_loaded, 16)
            act.dma_start(gate_w[:, :, :], gatew).then_inc(cmp_loaded, 16)
            act.dma_start(w2[:, :], cmpw2).then_inc(cmp_loaded, 16)

            def square(k, parity, source, first=False):
                if not (first and k < 2):
                    act.wait_ge(sums, n.at("sums", k - 1))
                act.activation(sq[:, parity, 0:source.shape[1]], source, ACT.Square).then_inc(squares, 1)

            def root(k):
                act.wait_ge(rcp, n.at("rcp", k + 1))
                act.activation(rinv[:, :], var[:, :], ACT.Sqrt).then_inc(rinvs, 1)

            def head_square(k, half, source, read):
                act.wait_ge(stats, n.at("stats", read))
                act.activation(sqh[:, half, 0:source.shape[1]], source, ACT.Square).then_inc(sqs, 1)

            def copy(out, source, b, scale=1.0):
                act.activation(out, source, ACT.Copy, scale=scale).then_inc(free[b], 1)

            def high_part(nth, j, product, load=1, kt=KD):
                act.wait_ge(loaded[j], 16 * n.at(f"loads{j}", load))
                if product is not None:
                    act.wait_ge(products, n.at("products", product))
                act.activation(parts[nth % 2][:, 0, 0:kt, :], slot[j][:, 0:kt, :], ACT.Copy).then_inc(highs, 1)

            def out_product(source, written, count, events, square_of):
                for q in range(2):
                    high_part(q, q, 0)
                act.wait_ge(written, count)
                for k in range(KD):
                    act.activation(hhi[:, k, :], source[:, k, :], ACT.Copy).then_inc(hhis, 1)
                for q in range(2, KD):
                    high_part(q, q % RING, q - 1, load=1 + q // RING)
                    square_of(q - 2)
                for k in range(KD - 2, KD):
                    square_of(k)
                n.past(events)

            def x_square(k):
                act.wait_ge(xs, n.at("xs", k + 1))
                square(k, k % 2, x[:, k, :])

            def z_square(k):
                act.wait_ge(products, n.at("products", k + 1))
                square(k, k % 2, bank[k % 2][:, :])
                copy(hid[:, k, :], bank[k % 2][:, :], k % 2)

            def norm(ffn=False):
                if ffn:
                    for u in range(2):
                        high_part(u, u, u - RING if n.base.get("products", 0) else None)
                root(0)
                for k in range(KD):
                    act.wait_ge(h32s, n.at("h32s", k + 1))
                    act.activation(hhi[:, k, :], h32[:, k, :], ACT.Copy).then_inc(hhis, 1)
                n.past(NORM)

            def ffn_up():
                for last in (False, True):
                    with n.turns(act, 1 if last else KF // 2 - 1, FFN_UP):
                        for u in range(2):
                            if u == 0:
                                high_part(2, 2, 1)
                            elif not last:
                                high_part(4, 0, 3, load=2)
                            act.wait_ge(products, n.at("products", 2 * u + 1))
                            act.wait_ge(free[1], n.at("free1", u - 1) if u else n.at("free1"))
                            act.activation(silu[:, u, :], bank[0][:, :], ACT.Silu).then_inc(free[0], 1)
                            if u == 0:
                                high_part(3, 3, 2)
                            elif not last:
                                high_part(5, 1, 4, load=2)

            def x_square_down(m):
                act.wait_ge(free[m], n.at(f"free{m}", 1))
                square(m, m % 2, x[:, m, :])

            def z_square_down(m):
                act.wait_ge(products, n.at("products", DOWN - KD + m + 1))
                square(m, m % 2, bank[m][:, :])
                copy(big8[:, m, :], bank[m][:, :], m)

            def ffn_down(square_of, memory=False):
                def hidden_highs(c):
                    k0 = sum(CHUNKS[:c])
                    for k in range(CHUNKS[c]):
                        act.activation(stores[c % 2][0][:, k, :], hid[:, k0 + k, :], ACT.Copy).then_inc(hhis, 1)

                high_part(0, 0, -1, kt=CHUNKS[0])
                act.wait_ge(free[1], n.at("free1"))
                hidden_highs(0)
                high_part(1, 1, 0, kt=CHUNKS[0])
                if memory:
                    root(0)
                    n.past(MEM_NORM)
                n.past(CLEAR)
                hidden_highs(1)
                for q in range(2, DOWN):
                    high_part(q, q % RING, q - 1, load=1 + q // RING, kt=CHUNKS[q // KD])
                    if q == KD + 2:
                        hidden_highs(2)
                    if q == 2 * KD + 2:
                        hidden_highs(3)
                    if q >= DOWN - 6:
                        square_of(q - DOWN + 6)
                for k in range(6, KD):
                    square_of(k)
                n.past(FFN_DOWN)

            def ffn_of_memory(loads):
                act.wait_ge(mem_loaded, 16 * loads)
                for k in range(KD):
                    square(k, k % 2, memh[:, k, :])
                n.past(SQUARES)
                ffn_up()
                ffn_down(x_square_down, memory=True)

            def exponential(k, width):
                act.wait_ge(negmaxs, n.at("negmax", k + 1))
                act.activation(ex[:, k % 3, 0:width], sc[:, k % 2, 0:width], ACT.Exp, bias=negmax[:, k % 2:k % 2 + 1],
                               accum_out=esum[:, k % 3:k % 3 + 1]).then_inc(exps, 1)

            def place_turned(k, i, blocks):
                act.wait_ge(turned, n.at("turned", k + 1))
                copy(PT[:, 0:blocks, i * P:(i + 1) * P],
                     bank[6][:, 0:blocks * P].rearrange("p (a b) -> p a b", a=blocks), 6)

            act.wait_ge(x_loaded, 16)
            for k in range(KD):
                square(k, k % 2, x[:, k, :], first=True)
            n.past(SQUARES)
            norm(ffn=True)
            ffn_of_memory(1)
            norm()

            def load_strip(i):
                act.wait_ge(cats, n.at("cats"))
                act.dma_start(strip[:, :], headtab[bass.ds(i, 1)].rearrange("a p t -> p (a t)")).then_inc(strips, 16)

            with n.turns(act, HEADS, RET) as i:
                load_strip(i)
                act.wait_ge(products, n.at("products", 1))
                copy(qs[:, 0, :], bank[0][:, :], 0)
                act.wait_ge(products, n.at("products", 3))
                copy(vs[:, :], bank[2][:, :], 2)
                act.wait_ge(products, n.at("products", 4))
                act.wait_ge(cats, n.at("cats"))
                act.activation(silu[:, 0, :], bank[0][:, :], ACT.Silu).then_inc(free[0], 1)
                act.wait_ge(outs, n.at("outs", 1))
                copy(o_sb[:, 0, :], bank[7][:, :], 7)
                act.wait_ge(free[3], n.at("free3", 1))
                head_square(0, 0, o_sb[:, 1, :], 1)
                root(0)

            act.wait_ge(stats, n.at("stats", 1))
            act.activation(le, bank[3][:, 0:2], ACT.Exp).then_inc(free[3], 1)
            n.past(LAM)

            with n.turns(act, HEADS, DIFF) as i:
                load_strip(i + HEADS)
                for c in range(2):
                    act.wait_ge(products, n.at("products", c + 1))
                    head_square(c, c, bank[c][:, :], 0)
                root(0)
                root(1)
                act.wait_ge(products, n.at("products", 3))
                copy(vs[:, :], bank[2][:, :], 2)
                for s in range(8 + 4):
                    if s < 8:
                        exponential(s, (s // 2 + 1) * P)
                    if s >= 4 and s % 2 == 1:
                        i = (s - 4) // 2
                        place_turned(i, i, i + 1)
                act.wait_ge(outs, n.at("outs", 1))
                head_square(2, 0, bank[7][:, :], 2)
                root(2)
            n.past(CLEAR)
            out_product(hid, cats, n.at("cats"), OUT_X, x_square)
            norm()

            with n.turns(act, HEADS, MEM1) as i:
                act.wait_ge(products, n.at("products", 2))
                act.wait_ge(stats, n.at("stats"))
                act.activation(sqh[:, 0, :], bank[0][:, :], ACT.Square).then_inc(sqs, 1)
                root(0)
                for c in range(2):
                    act.wait_ge(products, n.at("products", c + 3))
                    act.wait_ge(stats, n.at("stats", 1))
                    mm = act.activation(sqh[:, c, :], bank[1 + c][:, :], ACT.Square)
                mm.then_inc(sqs, 1)
                root(1)
                act.wait_ge(products, n.at("products", 6))
                copy(vs[:, :], bank[0][:, :], 0)
                for s in range(TT + 2):
                    if s < TT:
                        exponential(s, M)
                    if s >= 2:
                        place_turned(s - 2, s - 2, MT)
                for c in range(2):
                    act.wait_ge(outs, n.at("outs", c + 1))
                    copy(hid[:, bass.ds(i * 2 + c, 1), :].rearrange("p a t -> p (a t)"), bank[7][:, :], 7)
            act.dma_start(memh[:, :, :], mem2T).then_inc(mem_loaded, 16)
            n.past(CLEAR)
            out_product(hid, free[7], n.at("free7"), OUT_X, x_square)
            norm(ffn=True)
            ffn_of_memory(2)
            act.wait_ge(products, n.at("products"))
            act.dma_start(w1c[:, :, :], cmpw1).then_inc(cmp_loaded, 16)
            root(0)
            for k in range(KD):
                act.wait_ge(xs, n.at("xs", k + 1))
                square(k, k % 2, x[:, k, :])
            n.past(RESCALE)
            norm()

            act.wait_ge(outs, n.at("outs", 1))
            copy(gate_rows, bank[7][0:GATE_COLS, :], 7)
            act.wait_ge(gates_made, 1)
            g4 = bank[2][:, 0:TT * GATE_COLS].rearrange("p (t c) -> p t c", t=TT)
            act.activation(gates[:, :, :], g4[:, :, 0:48], ACT.Sigmoid).then_inc(acts, 1)
            act.wait_ge(free[2], n.at("free2", 1))
            act.activation(lf[:, 3, :, :], ifp[:, :, 4:8], ACT.Abs).then_inc(acts, 1)
            act.wait_ge(acts, 2)
            act.activation(lf[:, 3, :, :], lf[:, 3, :, :], ACT.Exp, scale=-1.0).then_inc(acts, 1)
            act.wait_ge(acts, 3)
            act.activation(lf[:, 3, :, :], lf[:, 3, :, :], ACT.Ln, bias=1.0).then_inc(acts, 1)

            def place_group(g):
                act.wait_ge(products, n.at("products", g + 1))
                copy(kvc[:, g, :], bank[g % 2][:, :], g % 2)

            for g in (0, 1):
                place_group(g)
            act.wait_ge(free[3], n.at("free3", 1))
            act.activation(rows[0:4, 3, :], rows[0:4, 2, :], ACT.Exp, scale=-1.0).then_inc(acts, 1)
            n.past(GATES)
            for g in (2, 3):
                place_group(g)
            all_n, bias_at = GROUPS * CMP_N, GROUPS * CMP_N
            act.wait_ge(stats, n.at("stats", 1))
            act.activation(pebias[:, 0:1], bank[3][:, bias_at:bias_at + 1], ACT.Copy).then_inc(acts, 1)
            act.wait_ge(acts, n.at("acts", 1))
            act.activation(hidk, bank[3][:, 0:all_n], ACT.Silu, bias=pebias[:, 0:1]).then_inc(free[3], 1)
            act.wait_ge(turned, n.at("turned", 1))
            act.activation(pebias[:, 1:2], bank[6][:, bias_at:bias_at + 1], ACT.Copy).then_inc(acts, 1)
            act.wait_ge(acts, n.at("acts", 2))
            act.wait_ge(dves, n.at("dve", 2))
            for a in range(4):
                mm = act.activation(hidv[:, :, a, 0:CMP_N], bank[6][:, 0:all_n].rearrange("p (g b) -> p g b", g=GROUPS),
                                    ACT.Silu, bias=pebias[:, 1:2])
            mm.then_inc(free[6], 1)
            act.wait_ge(stats, n.at("stats", 2))
            copy(kc_all, bank[3][:, 0:all_n], 3)
            n.past(CMP)

            act.wait_ge(zeros_set, 1)
            with n.turns(act, GROUPS, NSA) as i:
                act.wait_ge(products, n.at("products", 1))
                copy(qs[:, 0, :], bank[0][:, :], 0, 64 ** -0.5)
                act.wait_ge(products, n.at("products", 2))
                copy(qs[:, 1, :], bank[1][:, :], 1, 64 ** -0.5)

                def compressed_exp(s):
                    act.wait_ge(cmps, n.at("cmps", s + 1))
                    c4 = sc[:, s % 2, 0:P].rearrange("p (a b) -> p a b", a=4)[:, :, 0:CMP_N]
                    e4 = ex[:, s % 2, 0:P].rearrange("p (a b) -> p a b", a=4)[:, :, 0:CMP_N]
                    act.activation(e4, c4, ACT.Exp).then_inc(exps, 1)

                def place_compressed(s):
                    act.wait_ge(turned, n.at("turned", s + 1))
                    copy(PTc[:, s * P:(s + 1) * P], bank[6][:, 0:P], 6)

                compressed_exp(0)
                act.wait_ge(products, n.at("products", 3))
                act.activation(ks[0:64, 0, :], bank[3][0:64, :], ACT.Copy)
                copy(ks[64:P, 1, :], bank[3][64:P, :], 3)
                act.wait_ge(free[3], n.at("free3", 1))
                act.dma_start(ks[64:P, 0, :], ks[0:64, 0, :]).then_inc(twins, 16)
                act.dma_start(ks[0:64, 1, :], ks[64:P, 1, :]).then_inc(twins, 16)
                for s in range(1, TT):
                    compressed_exp(s)
                    place_compressed(s - 1)
                act.wait_ge(products, n.at("products", 4))
                copy(vs[:, :], bank[2][:, :], 2)
                for s in range(NJ + 3):
                    if s == 1:
                        place_compressed(TT - 1)
                    if s < NJ:
                        act.wait_ge(negmaxs, n.at("negmax", s + 1))
                        width = (s % 4 + 1) * P
                        act.activation(exs[s % 4][:, 0:width], sc[:, s % 2, 0:width], ACT.Exp,
                                       bias=negmax[:, s % 2:s % 2 + 1],
                                       accum_out=esum[:, s % 4:s % 4 + 1]).then_inc(exps, 1)
                    if s >= 3:
                        place_turned(4 + s - 3, (s - 3) % 4, (s - 3) % 4 + 1)
                    if s >= 4 and (s - 4) % 16 == 15:
                        pair = (s - 4) // 16
                        act.wait_ge(outs, n.at("outs", pair + 1))
                        copy(hid[:, bass.ds(i * 2 + pair, 1), :].rearrange("p a t -> p (a t)"), bank[7][:, :], 7)
                act.wait_ge(outs, n.at("outs", 2))
                copy(hid[:, bass.ds(i * 2 + 1, 1), :].rearrange("p a t -> p (a t)"), bank[7][:, :], 7)

            for s in range(8):
                act.wait_ge(scores, n.at("scores", s + 1))
                copy((negM if s < 4 else emb)[:, s % 4, :], bank[4 + s % 2][:, :], 4 + s % 2,
                     -1.0 if s < 4 else 1.0)
            n.past(SPREAD)
            act.wait_ge(pads, 1)
            with n.turns(act, HEADS, ML):
                for c in range(2):
                    act.wait_ge(products, n.at("products", c + 1))
                    copy(xp[:, c, 3:T + 3], bank[c][:, :], c)
                for c, dst in ((0, qs), (1, ks)):
                    act.wait_ge(dves, n.at("dve", 4 * c + 4))
                    act.activation(dst[:, 0, :], o_sb[:, c, :], ACT.Silu, bias=hp[:, 8 + c:9 + c]).then_inc(convs, 1)
                act.wait_ge(products, n.at("products", 3))
                copy(vs[:, :], bank[2][:, :], 2)
                act.wait_ge(products, n.at("products", 4))
                act.wait_ge(cats, n.at("cats"))
                act.activation(silu[:, 0, :], bank[0][:, :], ACT.Sigmoid).then_inc(free[0], 1)
                for j in range(TT):
                    act.wait_ge(dves, n.at("dve", 9 + j))
                    act.activation(hid[:, 18 + j, 0:T - j * P], hid[:, 18 + j, 0:T - j * P], ACT.Exp).then_inc(exps, 1)
                act.wait_ge(turned, n.at("turned", 1))
                act.activation(var[:, :], bank[6][:, :], ACT.Abs).then_inc(free[6], 1)
                act.wait_ge(free[7], n.at("free7", 1))
                head_square(0, 0, o_sb[:, 0, :], 0)
                root(0)

            with n.turns(act, HEADS, MEM2) as i:
                act.wait_ge(products, n.at("products", 1))
                copy(qs[:, 0, :], bank[0][:, :], 0, P ** -0.5)
                act.wait_ge(products, n.at("products", 2))
                copy(ks[:, 0, 0:M], bank[1][:, 0:M], 1)
                act.wait_ge(products, n.at("products", 3))
                copy(vs[:, 0:MT * P], bank[2][:, 0:MT * P], 2)
                for s in range(TT + 2):
                    if s < TT:
                        exponential(s, M)
                    if s >= 2:
                        place_turned(s - 2, s - 2, MT)
                act.wait_ge(outs, n.at("outs", 1))
                copy(hid[:, bass.ds(i + 12, 1), :].rearrange("p a t -> p (a t)"), bank[7][:, :], 7)

            high_part(0, 0, -1)
            for last in (False, True):
                with n.turns(act, 1 if last else KD - 1, MERGE):
                    high_part(1, 2, -3)
                    for j in range(3):
                        if j == 1:
                            high_part(2, 4, 1)
                        if j == 2 and not last:
                            high_part(0, 0, 5, load=2)
                        act.wait_ge(products, n.at("products", 2 * j + 1))
                        act.wait_ge(free[1], n.at("free1", j) if j < 1 else n.at("free1", j - 1))
                        act.activation(silu[:, j, :], bank[0][:, :], ACT.Sigmoid).then_inc(free[0], 1)
            n.past(CLEAR)
            out_product(big8, dves, n.at("dve"), OUT_Z, z_square)
            root(0)
            for k in range(KD):
                act.wait_ge(xs, n.at("xs", k + 1))
                square(k, k % 2, x[:, k, :])
            n.past(ADD_Z)
            norm(ffn=True)
            ffn_up()
            ffn_down(z_square_down)
            root(0)
            n.past(ADD_Z_LAST)

        @block.vector
        def _(dve):
            n = Counts()

            def reciprocal_mean(k, r, scale, eps, width=T):
                dve.wait_ge(stats, n.at("stats", k + 1))
                dve.tensor_scalar(var[:, 0:width], bank[3][:, 0:width], scale, eps, ALU.mult, ALU.add).then_inc(free[3], 1)
                dve.wait_ge(free[3], n.at("free3", k + 1))
                dve.reciprocal(var[:, 0:width], var[:, 0:width]).then_inc(rcp, 1)
                dve.wait_ge(rinvs, n.at("rinv", r + 1))

            def scaled(out, source, gain, width=T):
                return dve.scalar_tensor_tensor(out, source, gain, rinv[:, 0:width], ALU.mult, ALU.mult)

            def apply_norm(g):
                for k in range(KD + 2):
                    if k < KD:
                        scaled(h32[:, k, :], x[:, k, :], params[:, g + k:g + k + 1]).then_inc(h32s, 1)
                    if k >= 2:
                        a = k - 2
                        dve.wait_ge(hhis, n.at("hhis", a + 1))
                        dve.tensor_tensor(hlo[:, a, :], h32[:, a, :], hhi[:, a, :].bitcast(F32),
                                          ALU.subtract).then_inc(hlos, 1)

            def norm(g):
                reciprocal_mean(0, 0, 1.0 / D, EPS)
                apply_norm(g)
                n.past(NORM)

            def tile(a, k):
                return a[:, bass.ds(k, 1), :].rearrange("p a t -> p (a t)")

            def ffn_up():
                with n.turns(dve, KF // 2, FFN_UP) as i:
                    for u in range(2):
                        dve.wait_ge(free[0], n.at("free0", u + 1))
                        dve.wait_ge(products, n.at("products", 2 * u + 2))
                        dve.tensor_tensor(tile(hid, i * 2 + u), silu[:, u, :], bank[1][:, :],
                                          ALU.mult).then_inc(free[1], 1)

            def norm_memory(g):
                reciprocal_mean(0, 0, 1.0 / D, EPS, M)
                for k in range(KD):
                    last = scaled(memh[:, k, :], memh[:, k, :], params[:, g + k:g + k + 1], M)
                last.then_inc(mems, 1)
                n.past(MEM_NORM)

            def ffn_down(memory_gain=None, into_x=True):
                for c, k_tiles in enumerate(CHUNKS):
                    k0 = sum(CHUNKS[:c])
                    for k in range(k_tiles):
                        high, low = (store[:, k, :] for store in stores[c % 2])
                        dve.wait_ge(hhis, n.at("hhis", k0 + k + 1))
                        dve.tensor_tensor(low, hid[:, k0 + k, :], high.bitcast(F32), ALU.subtract).then_inc(hlos, 1)
                    if c == 0 and memory_gain is not None:
                        norm_memory(memory_gain)
                n.past(CLEAR)
                if into_x:
                    for m in range(KD):
                        dve.wait_ge(products, n.at("products", DOWN - KD + m + 1))
                        dve.scalar_tensor_tensor(x[:, m, :], bank[m][:, :], 0.5, x[:, m, :],
                                                 ALU.mult, ALU.add).then_inc(free[m], 1)
                n.past(FFN_DOWN)

            def low_parts(source):
                for k in range(KD):
                    dve.wait_ge(hhis, n.at("hhis", k + 1))
                    dve.tensor_tensor(hlo[:, k, :], source[:, k, :], hhi[:, k, :].bitcast(F32),
                                      ALU.subtract).then_inc(hlos, 1)

            def out_x():
                n.past(CLEAR)
                low_parts(hid)
                for k in range(KD):
                    dve.wait_ge(products, n.at("products", k + 1))
                    dve.tensor_tensor(x[:, k, :], bank[k % 2][:, :], x[:, k, :], ALU.add).then_inc(xs, 1)
                n.past(OUT_X)

            def masked_scores(k, width, mask, b_more=0, s_more=0):
                b = 4 + k % 2
                dve.wait_ge(scores, n.at("scores", s_more + k + 1))
                dve.memset(lanes[:, 42:43], 0.0)
                dve.tensor_tensor_reduce(sc[:, k % 2, 0:width], bank[b][:, 0:width], mask, 1.0, -3e38,
                                         ALU.add, ALU.max, maxs[:, k % 2:k % 2 + 1]).then_inc(free[b], 1)
                dve.wait_ge(free[b], n.at(f"free{b}", b_more + k // 2 + 1))
                dve.tensor_scalar(negmax[:, k % 2:k % 2 + 1], maxs[:, k % 2:k % 2 + 1], -1.0, None,
                                  ALU.mult).then_inc(negmaxs, 1)

            def normalise(k, width, gate=None, d_more=0, e_more=0, buffers=(ex[:, 0, :], ex[:, 1, :], ex[:, 2, :])):
                r = rsm[:, k % len(buffers):k % len(buffers) + 1]
                total = esum[:, k % len(buffers):k % len(buffers) + 1]
                dve.wait_ge(exps, n.at("exps", e_more + k + 1))
                dve.reciprocal(r, total).then_inc(dves, 1)
                dve.wait_ge(dves, n.at("dve", d_more + k + 1))
                e = buffers[k % len(buffers)][:, 0:width]
                if gate is None:
                    dve.tensor_scalar(e, e, r, None, ALU.mult).then_inc(probs, 1)
                else:
                    dve.tensor_scalar(e, e, r, gate, ALU.mult, ALU.mult).then_inc(probs, 1)

            no_mask = tables[:, K_CAUS:K_CAUS + M]

            for s in (*free, cats, xs):
                dve.sem_inc(s, 1)
            dve.wait_ge(params_loaded, 16)
            dve.wait_ge(tables_loaded, 16)
            n.past(SQUARES)
            norm(G_FFN1)
            n.past(SQUARES)
            ffn_up()
            ffn_down(G_MEMKV)
            norm(G_MIX)

            with n.turns(dve, HEADS, RET) as i:
                dve.wait_ge(products, n.at("products", 2))
                dve.tensor_copy(ks[:, 0, :], bank[1][:, :]).then_inc(free[1], 1)
                dve.wait_ge(strips, 16 * n.at("strips", 1))
                for j in range(TT):
                    b = 4 + j % 2
                    dve.wait_ge(scores, n.at("scores", j + 1))
                    dve.tensor_tensor(PT[:, j, j * P:T], bank[b][:, 0:T - j * P], strip[:, 0:T - j * P],
                                      ALU.mult).then_inc(free[b], 1)
                dve.wait_ge(stats, n.at("stats", 1))
                dve.wait_ge(free[7], n.at("free7", 1))
                dve.scalar_tensor_tensor(o_sb[:, 1, :], bank[3][:, :], -1.0 / P, o_sb[:, 0, :],
                                         ALU.mult, ALU.add).then_inc(free[3], 1)
                reciprocal_mean(1, 0, 1.0 / P, EPS)
                scaled(o_sb[:, 1, :], o_sb[:, 1, :], params[:, C_RET:C_RET + 1]).then_inc(dves, 1)
                dve.wait_ge(dves, n.at("dve", 1))
                dve.wait_ge(free[0], n.at("free0", 2))
                dve.tensor_tensor(tile(hid, i), o_sb[:, 1, :], silu[:, 0, :], ALU.mult).then_inc(cats, 1)

            dve.tensor_tensor(lprod[0:64, :], params[0:64, C_LAM:C_LAM + 2], params[0:64, C_LAM + 2:C_LAM + 4],
                              ALU.mult).then_inc(dves, 1)
            dve.tensor_scalar(dn_gain, params[:, C_DN:C_DN + 1], 1.0 - LAM_INIT, None, ALU.mult).then_inc(dves, 1)
            dve.wait_ge(free[3], n.at("free3", 1))
            dve.tensor_scalar(nlam, le[:, 1:2], le[:, 0:1], -LAM_INIT, ALU.subtract, ALU.add).then_inc(dves, 1)
            n.past(LAM)
            dve.wait_ge(dves, n.at("dve"))

            with n.turns(dve, HEADS, DIFF) as i:
                reciprocal_mean(0, 0, 1.0, 64 * EPS)
                scaled(qs[:, 0, :], bank[0][:, :], params[:, C_DQ:C_DQ + 1]).then_inc(free[0], 1)
                reciprocal_mean(1, 1, 1.0 / 64, EPS)
                scaled(ks[:, 0, :], bank[1][:, :], params[:, C_DK:C_DK + 1]).then_inc(free[1], 1)
                dve.wait_ge(strips, 16 * n.at("strips", 1))
                for s in range(8 + 1):
                    if s < 8:
                        width = (s // 2 + 1) * P
                        masked_scores(s, width, strip[:, T - width:T])
                    if s >= 1:
                        a, row, m = s - 1, (s - 1) // 2, (s - 1) % 2
                        width = (row + 1) * P
                        r, e = rsm[:, a % 3:a % 3 + 1], ex[:, a % 3, 0:width]
                        dve.wait_ge(exps, n.at("exps", a + 1))
                        dve.reciprocal(r, esum[:, a % 3:a % 3 + 1]).then_inc(dves, 1)
                        dve.wait_ge(dves, n.at("dve", 2 * a + 1))
                        if m == 0:
                            dve.tensor_scalar(e, e, r, None, ALU.mult).then_inc(dves, 1)
                        else:
                            dve.tensor_scalar(r, r, nlam, None, ALU.mult).then_inc(dves, 1)
                            dve.wait_ge(dves, n.at("dve", 2 * a + 2))
                            dve.scalar_tensor_tensor(o_sb[:, row % 2, 0:width], e, r, ex[:, (a - 1) % 3, 0:width],
                                                     ALU.mult, ALU.add).then_inc(probs, 1)
                reciprocal_mean(2, 2, 1.0 / P, EPS)
                scaled(tile(hid, i + HEADS), bank[7][:, :], dn_gain).then_inc(free[7], 1)
                dve.wait_ge(free[7], n.at("free7", 1))
                dve.tensor_copy(lanes[:, 40:41], lanes[:, 8:9]).then_inc(cats, 1)
            out_x()
            norm(G_MEMQ)

            with n.turns(dve, HEADS, MEM1):
                reciprocal_mean(0, 0, 1.0 / M, EPS, M)
                for c in range(2):
                    last = scaled(ks[:, c, 0:M], bank[0][:, c * M:(c + 1) * M], params[:, C_MK + c:C_MK + c + 1], M)
                last.then_inc(free[0], 1)
                reciprocal_mean(1, 1, 1.0, M * EPS)
                for c in range(2):
                    scaled(qs[:, c, :], bank[1 + c][:, :], params[:, C_MQ + c:C_MQ + c + 1]).then_inc(free[1 + c], 1)
                for s in range(TT + 1):
                    if s < TT:
                        masked_scores(s, M, no_mask)
                    if s >= 1:
                        normalise(s - 1, M)
            out_x()
            norm(G_FFN2)
            n.past(SQUARES)
            ffn_up()
            ffn_down(G_MEM2)
            reciprocal_mean(0, 0, 1.0 / D, EPS)
            for k in range(KD):
                scaled(x[:, k, :], x[:, k, :], params[:, G_OUT + k:G_OUT + k + 1]).then_inc(xs, 1)
            n.past(RESCALE)
            norm(G_PRE2)

            dve.wait_ge(acts, 1)
            g4 = bank[2][:, 0:TT * GATE_COLS].rearrange("p (t c) -> p t c", t=TT)
            dve.tensor_tensor(ifp[:, :, :], g4[:, :, 48:56],
                              params[:, C_GATEB:C_GATEB + 8].unsqueeze(1).to_broadcast([P, TT, 8]),
                              ALU.add).then_inc(free[2], 1)
            dve.wait_ge(free[2], n.at("free2", 1))
            dve.tensor_scalar(lf[:, 0, :, :], ifp[:, :, 4:8], 0.0, None, ALU.min).then_inc(dves, 1)
            dve.wait_ge(dves, n.at("dve", 1))
            dve.wait_ge(acts, 4)
            dve.tensor_tensor(lf[:, 1, :, :], lf[:, 0, :, :], lf[:, 3, :, :], ALU.subtract).then_inc(dves, 1)
            dve.tensor_tensor(lf[:, 2, :, :], lf[:, 3, :, :], lf[:, 0, :, :], ALU.subtract).then_inc(dves, 1)
            dve.wait_ge(turned, n.at("turned", 1))
            dve.tensor_copy(rows[0:4, 0, :], bank[6][0:4, :]).then_inc(free[6], 1)
            dve.wait_ge(free[6], n.at("free6", 1))
            dve.tensor_tensor_scan(rows[0:4, 1, :], rows[0:4, 0, :], rows[0:4, 0, :], 0.0, ALU.max,
                                   ALU.max).then_inc(dves, 1)
            dve.wait_ge(dves, n.at("dve", 4))
            dve.wait_ge(stats, n.at("stats", 1))
            dve.tensor_tensor(rows[0:4, 2, :], bank[3][0:4, :], rows[0:4, 1, :], ALU.add).then_inc(free[3], 1)
            dve.wait_ge(stats, n.at("stats", 2))
            dve.tensor_copy(acol[:, :, :], bank[3][:, 0:16].rearrange("p (t h) -> p h t", t=TT)).then_inc(free[3], 1)
            n.past(GATES)
            dve.wait_ge(gates_made, 1)
            dve.tensor_copy(kvc[:, GROUPS, 0:CMP_L], params[:, C_PE:C_PE + CMP_L]).then_inc(dves, 1)
            dve.memset(vb_all, 0.0)
            dve.memset(hidv, 0.0).then_inc(dves, 1)
            dve.wait_ge(dves, n.at("dve", 2))
            dve.wait_ge(turned, n.at("turned", 2))
            for a in range(4):
                rows_a, at = slice(32 * a, 32 * a + 32), a // 2 * P + 64 * (a % 2)
                last = dve.tensor_copy(vb_all[rows_a, :, at:at + 64],
                                       bank[6][rows_a, 0:GROUPS * 64].rearrange("p (g b) -> p g b", g=GROUPS))
            last.then_inc(free[6], 1)
            n.past(CMP)

            with n.turns(dve, GROUPS, NSA):
                dve.wait_ge(heads, n.at("heads", 1))
                done = [0]

                def step(instruction):
                    instruction.then_inc(dves, 1)
                    done[0] += 1

                def front(s):
                    c4 = sc[:, s % 2, 0:P].rearrange("p (a b) -> p a b", a=4)[:, :, 0:CMP_N]
                    add = tables[:, K_CADD + s * CMP_N:K_CADD + (s + 1) * CMP_N]
                    for odd in range(2):
                        dve.wait_ge(scores, n.at("scores", 2 * s + odd + 1))
                        dve.tensor_tensor(c4[:, odd::2, :],
                                          bank[4 + odd][:, 0:64].rearrange("p (a b) -> p a b", a=2)[:, :, 0:CMP_N],
                                          add.unsqueeze(1).to_broadcast([P, 2, CMP_N]),
                                          ALU.add).then_inc(free[4 + odd], 1)
                    dve.wait_ge(free[5], n.at("free5", s + 1))
                    step(dve.tensor_reduce(cmx, c4, AX.X, ALU.max))
                    dve.wait_ge(dves, n.at("dve", done[0]))
                    dve.tensor_tensor(c4, c4, cmx.unsqueeze(2).to_broadcast([P, 4, CMP_N]),
                                      ALU.subtract).then_inc(cmps, 1)

                def back(s):
                    e4 = ex[:, s % 2, 0:P].rearrange("p (a b) -> p a b", a=4)[:, :, 0:CMP_N]
                    mul = tables[:, K_CMUL + s * CMP_N:K_CMUL + (s + 1) * CMP_N]
                    dve.wait_ge(exps, n.at("exps", s + 1))
                    step(dve.tensor_reduce(csum, e4, AX.X, ALU.add))
                    dve.wait_ge(dves, n.at("dve", done[0]))
                    step(dve.reciprocal(cgate, csum))
                    dve.wait_ge(dves, n.at("dve", done[0]))
                    step(dve.tensor_tensor(cgate, cgate, ggate[:, s, 0::3], ALU.mult))
                    step(dve.tensor_tensor(e4, e4, mul.unsqueeze(1).to_broadcast([P, 4, CMP_N]), ALU.mult))
                    dve.wait_ge(dves, n.at("dve", done[0]))
                    if s >= 1:
                        dve.wait_ge(turned, n.at("turned", s))
                    dve.tensor_tensor(pc[:, :, 0:CMP_N], e4, cgate.unsqueeze(2).to_broadcast([P, 4, CMP_N]),
                                      ALU.mult).then_inc(probs, 1)

                front(0)
                for s in range(1, TT):
                    dve.wait_ge(cmps, n.at("cmps", s))
                    front(s)
                    back(s - 1)
                back(TT - 1)
                for s in range(NJ + 1):
                    if s < NJ:
                        width = (s % 4 + 1) * P
                        masked_scores(s, width, tables[:, K_CAUS + T - width:K_CAUS + T], 4, 8)
                    if s >= 1:
                        a = s - 1
                        head, br, row = a // 8, a // 4 % 2, a % 4
                        normalise(a, (row + 1) * P, ggate[:, row, head * 3 + 1 + br:head * 3 + 2 + br], 20, 4, exs)
            n.past(SPREAD)

            dve.wait_ge(turned, n.at("turned"))
            dve.memset(xp[:, :, 0:3], 0.0).then_inc(pads, 1)
            with n.turns(dve, HEADS, ML) as i:
                dve.tensor_scalar(hp[:, 12:16], acol[:, bass.ds(i, 1), :].rearrange("p a t -> p (a t)"), 1.0, None,
                                  ALU.mult)
                dve.tensor_scalar(hp[:, 0:C_HEADN], params[:, bass.ds(C_HEAD + i * C_HEADN, C_HEADN)], 1.0, None,
                                  ALU.mult).then_inc(heads, 1)
                dve.wait_ge(heads, n.at("heads", 1))
                for c in range(2):
                    dve.wait_ge(free[c], n.at(f"free{c}", 1))
                    y = o_sb[:, c, :]
                    for tap in range(4):
                        w = hp[:, 4 * c + tap:4 * c + tap + 1]
                        if tap == 0:
                            dve.tensor_scalar(y, xp[:, c, 0:T], w, None, ALU.mult).then_inc(dves, 1)
                        else:
                            dve.wait_ge(dves, n.at("dve", 4 * c + tap))
                            dve.scalar_tensor_tensor(y, xp[:, c, tap:tap + T], w, y, ALU.mult, ALU.add).then_inc(dves, 1)
                for j in range(TT):
                    w = T - j * P
                    dve.scalar_tensor_tensor(hid[:, 18 + j, 0:w], negM[:, bass.ds(i, 1), j * P:T].rearrange("p a t -> p (a t)"),
                                             hp[:, 12 + j:13 + j], tables[:, K_CAUST:K_CAUST + w],
                                             ALU.add, ALU.add).then_inc(dves, 1)
                for j in range(TT):
                    b, w = 4 + j % 2, T - j * P
                    dve.wait_ge(exps, n.at("exps", j + 1))
                    dve.wait_ge(scores, n.at("scores", j + 1))
                    dve.scalar_tensor_tensor(PT[:, j, j * P:T], bank[b][:, 0:w], P ** -0.5, hid[:, 18 + j, 0:w],
                                             ALU.mult, ALU.mult).then_inc(free[b], 1)
                dve.wait_ge(free[6], n.at("free6", 1))
                dve.tensor_tensor(var[:, :], var[:, :], tile(emb, i), ALU.max).then_inc(dves, 1)
                dve.wait_ge(dves, n.at("dve", 13))
                dve.reciprocal(var[:, :], var[:, :]).then_inc(dves, 1)
                dve.wait_ge(dves, n.at("dve", 14))
                dve.wait_ge(outs, n.at("outs", 1))
                dve.tensor_tensor(o_sb[:, 0, :], bank[7][:, :], var[:, :], ALU.mult).then_inc(free[7], 1)
                reciprocal_mean(0, 0, 1.0 / P, EPS)
                scaled(o_sb[:, 1, :], o_sb[:, 0, :], hp[:, 10:11]).then_inc(dves, 1)
                dve.wait_ge(dves, n.at("dve", 15))
                dve.wait_ge(free[0], n.at("free0", 2))
                dve.tensor_tensor(tile(hid, i + 8), o_sb[:, 1, :], silu[:, 0, :], ALU.mult).then_inc(cats, 1)

            with n.turns(dve, HEADS, MEM2):
                for s in range(TT + 1):
                    if s < TT:
                        masked_scores(s, M, no_mask)
                    if s >= 1:
                        normalise(s - 1, M)

            with n.turns(dve, KD, MERGE) as i:
                for j in range(3):
                    dve.wait_ge(free[0], n.at("free0", j + 1))
                    dve.wait_ge(products, n.at("products", 2 * j + 2))
                    dve.tensor_tensor(ex[:, j, :], silu[:, j, :], bank[1][:, :], ALU.mult).then_inc(free[1], 1)
                    if j == 1:
                        dve.wait_ge(free[1], n.at("free1", 2))
                        dve.tensor_tensor(sc[:, 0, :], ex[:, 0, :], ex[:, 1, :], ALU.add).then_inc(dves, 1)
                dve.wait_ge(free[1], n.at("free1", 3))
                dve.wait_ge(dves, n.at("dve", 1))
                dve.tensor_tensor(tile(big8, i), sc[:, 0, :], ex[:, 2, :], ALU.add).then_inc(dves, 1)

            def add_z(z, g, events):
                reciprocal_mean(0, 0, 1.0 / D, EPS)
                for k in range(KD + 1):
                    if k < KD:
                        scaled(z[:, k, :], z[:, k, :], params[:, g + k:g + k + 1]).then_inc(dves, 1)
                    if k >= 1:
                        dve.wait_ge(dves, n.at("dve", k))
                        dve.tensor_tensor(x[:, k - 1, :], x[:, k - 1, :], z[:, k - 1, :], ALU.add).then_inc(xs, 1)
                n.past(events)

            n.past(CLEAR)
            low_parts(big8)
            n.past(OUT_Z)
            add_z(hid, G_POST2, ADD_Z)
            norm(G_PREF2)
            ffn_up()
            ffn_down(into_x=False)
            add_z(big8, G_POSTF2, ADD_Z_LAST)


TOTAL = {"xs": 1 + 2 * KD + 3 * KD}


def _panels(np_, w, cols, k0=0, k1=None):
    w = w[k0:k1]
    a = w.reshape(w.shape[0] // P, P, w.shape[1])
    return [np_.ascontiguousarray(a[:, :, c].transpose(1, 0, 2)) for c in cols]


def _tables():
    r = np.arange(P)
    con = np.zeros((P, K_BASE), np.float32)
    con[:, K_ID:K_ID + P] = np.eye(P)
    con[:, K_ONE:K_ONE + P] = 1
    con[:, K_BLK:K_BLK + P] = (r[:, None] // 64 == r[None, :] // 64)
    tab = np.zeros((P, NTAB), np.float32)
    tab[:, K_CAUS + T - P:K_CAUS + T] = np.where(r[None, :] <= r[:, None], 0, NEG)
    tab[:, K_CAUST:K_CAUST + P] = np.where(r[None, :] >= r[:, None], 0, NEG)
    c = np.arange(T)
    tab[:, K_CUM:K_CUM + T] = c[None, :] >= r[:, None]
    for t in range(TT):
        ok = (np.arange(CMP_N)[None, :] * CMP_S + CMP_L - 1) <= (t * P + r)[:, None]
        tab[:, K_CADD + t * CMP_N:K_CADD + (t + 1) * CMP_N] = np.where(ok, 0, NEG)
        tab[:, K_CMUL + t * CMP_N:K_CMUL + (t + 1) * CMP_N] = ok
    headtab = np.zeros((2 * HEADS, P, T), np.float32)
    for hd in range(HEADS):
        gamma = np.log1p(-2.0 ** (-5.0 - hd))
        rel = c[None, :] - r[:, None]
        headtab[hd] = np.where(rel >= 0, np.exp(gamma * np.maximum(rel, 0)), 0) * P ** -0.5
        slope = 2.0 ** (-8.0 * (hd + 1) / HEADS)
        dist = r[:, None] - (c[None, :] - (T - P))
        headtab[HEADS + hd] = np.where(dist >= 0, -slope * dist, NEG)
    return con, tab, headtab


def kernel(**inputs):
    import numpy as _np
    import concourse.bacc as _bacc
    from concourse import mybir as _mybir
    from concourse.bass_utils import run_bass_kernel_spmd as _run

    I = {k: _np.asarray(v) for k, v in inputs.items()}

    def W(name):
        return I[name][0]

    def cols(start, width=P):
        return slice(start, start + width)

    def two(a, b, width=64):
        return _np.r_[a:a + width, b:b + width]

    w8, w7, w4 = [], [], []

    def ffn(w1, w3, w2, off3=0):
        for f in range(KF):
            w8.extend(_panels(_np, w1, [cols(f * P)]))
            w8.extend(_panels(_np, w3, [cols(off3 + f * P)]))
        k0 = 0
        for k in CHUNKS:
            for m in range(KD):
                {4: w4, 7: w7}[k].extend(_panels(_np, w2, [cols(m * P)], k0 * P, (k0 + k) * P))
            k0 += k

    ffn(W("ffn1_w1"), W("ffn1_w3"), W("ffn1_w2"))
    win = W("w_in")
    for hd in range(HEADS):
        w8.extend(_panels(_np, win, [cols(b * 512 + hd * P) for b in range(4)]))
    for hd in range(HEADS):
        w8.extend(_panels(_np, win, [cols(2048 + b * 512 + hd * P) for b in range(3)]))
    w8.extend(_panels(_np, W("w_out"), [cols(m * P) for m in range(KD)]))
    for hd in range(HEADS):
        w8.extend(_panels(_np, W("mem_w_kv"), [cols(hd * M + c * P) for c in range(2)]))
        w8.extend(_panels(_np, W("mem_w_q"), [cols(hd * M + c * P) for c in range(2)]))
        w8.extend(_panels(_np, W("mem_w_kv"), [cols(D + hd * M + c * P) for c in range(2)]))
    w8.extend(_panels(_np, W("mem_w_o"), [cols(m * P) for m in range(KD)]))
    ffn(W("ffn2_w1"), W("ffn2_w3"), W("ffn2_w2"))
    win = W("w_in_2")
    kv0 = 1024

    def kv(b, g):
        return kv0 + b * 256 + g * 64

    w8.extend(_panels(_np, win, [two(kv(0, g), kv(1, g)) for g in range(GROUPS)]))
    for g in range(GROUPS):
        w8.extend(_panels(_np, win, [cols(g * 256), cols(g * 256 + P), two(kv(2, g), kv(4, g)),
                                     two(kv(3, g), kv(5, g))]))
    ml0 = 1024 + 1536 + 48
    if0 = ml0 + 1536
    o0 = if0 + 8
    mq0 = o0 + 512
    gm0 = mq0 + 512
    for hd in range(HEADS):
        w8.extend(_panels(_np, win, [cols(ml0 + hd * P), cols(ml0 + 512 + hd * P), cols(ml0 + 1024 + hd * P),
                                     cols(o0 + hd * P)]))
    mkv = W("w_mem_kv_2")
    for hd in range(HEADS):
        w8.extend(_panels(_np, win, [cols(mq0 + hd * P)]))
        w8.extend(_panels(_np, mkv, [cols(hd * P), cols(512 + hd * P)]))
    for m in range(KD):
        w8.extend(_panels(_np, win, [cols(gm0 + m * P)]))
        w8.extend(_panels(_np, W("w_proj_nsa_2"), [cols(m * P)]))
        w8.extend(_panels(_np, win, [cols(gm0 + D + m * P)]))
        w4.extend(_panels(_np, W("w_proj_ml_2"), [cols(m * P)]))
        w8.extend(_panels(_np, win, [cols(gm0 + 2 * D + m * P)]))
        w4.extend(_panels(_np, W("w_proj_mem_2"), [cols(m * P)]))
    w8.extend(_panels(_np, W("w_out_2"), [cols(m * P) for m in range(KD)]))
    ffn(W("w_ffn_in_2"), W("w_ffn_in_2"), W("w_ffn_down_2"), FF)

    gatew = _np.concatenate([win[:, 2560:2608], win[:, if0:if0 + 8]], 1).reshape(KD, P, 56).transpose(1, 0, 2)
    cw1 = _np.concatenate([W("cmp_w1_k_2").transpose(1, 0, 2), W("cmp_w1_v_2").transpose(1, 0, 2)], 0)
    cw2 = _np.concatenate([W("cmp_w2_k_2"), W("cmp_w2_k_2"), W("cmp_w2_v_2")], 1)

    par = [W(k).reshape(KD, P).T for k in ("norm_ffn1", "norm_mix", "norm_mem_q", "norm_mem_kv", "norm_ffn2",
                                           "norm_out", "g_pre_mix_2", "g_mem_2", "g_post_mix_2", "g_pre_ffn_2",
                                           "g_post_ffn_2")]
    twice = lambda v: _np.concatenate([v, v])[:, None]
    par += [W("ret_norm")[:, None], twice(W("diff_q_norm")), twice(W("diff_k_norm")), W("diff_norm")[:, None],
            W("mem_q_norm").reshape(2, P).T, W("mem_k_norm").reshape(2, P).T,
            twice(W("lambda_q1")), twice(W("lambda_q2")), twice(W("lambda_k1")), twice(W("lambda_k2"))]
    cw, cb, hg = W("ml_conv_w_2"), W("ml_conv_b_2"), W("ml_head_g_2")
    for hd in range(HEADS):
        a, b = hd * P, 512 + hd * P
        par += [cw[:, a:a + P].T, cw[:, b:b + P].T, cb[a:a + P, None], cb[b:b + P, None], hg[a:a + P, None]]
    par += [_np.repeat(W("ml_gate_b_2")[None, :], P, 0),
            _np.concatenate([W("cmp_pe_k_2").T, W("cmp_pe_v_2").T], 0)]
    con, tab, headtab = _tables()

    arrays = {
        "xT": I["x"][0].T.reshape(KD, P, T).transpose(1, 0, 2),
        "memT": I["mem"][0].T.reshape(KD, P, M).transpose(1, 0, 2),
        "mem2T": I["mem_2"][0].T.reshape(KD, P, M).transpose(1, 0, 2),
        "par": _np.concatenate(par, 1), "con": con, "tab": tab, "headtab": headtab,
        "w8": _np.stack(w8), "w7": _np.stack(w7), "w4": _np.stack(w4),
        "gatew": gatew, "cmpw1": cw1, "cmpw2": cw2,
    }
    arrays = {k: _np.ascontiguousarray(v) for k, v in arrays.items()}
    nc = _bacc.Bacc("TRN2", target_bir_lowering=False, num_devices=1)
    args = [nc.dram_tensor(k, a.shape, _mybir.dt.from_np(a.dtype), kind="ExternalInput").ap() for k, a in arrays.items()]
    args.append(nc.dram_tensor("outT", (KD, P, T), _mybir.dt.float32, kind="ExternalOutput").ap())
    build(nc, *args)
    r = _run(nc, [arrays], core_ids=[0])
    return _np.ascontiguousarray(r.results[0]["outT"].reshape(D, T).T)[None]
```
